# Optimizing a Trainium2 kernel written in Bass

```python
import jax, jax.numpy as jnp
from jax import lax
import numpy as np

D_MODEL = 2048
BATCH = 1
SEQ = 256
DEPTH = 1

GRID_W = 64
D_MIX = D_MODEL
NH_A = 4
DH_A = D_MIX // 2 // NH_A
W_A = NH_A * DH_A
NH_B = 8
DH_B = (D_MIX - W_A) // NH_B
W_B = NH_B * DH_B
CHUNK = 64
WIN_ROWS_MAX = 8
WIN_COLS = 16
D_FF = ((8 * D_MODEL // 3 + 255) // 256) * 256
CONV_W = 3
N_MOD = 6
N_GATES = 4 * NH_A
IN_SIZES = (W_A, W_A, W_A, W_A, N_GATES, W_B, W_B, W_B)
IN_COLS = sum(IN_SIZES)
IN_SPLITS = tuple(int(s) for s in np.cumsum(IN_SIZES)[:-1])
EPS = 1e-6


def rms_norm(x, g):
    xf = x.astype(jnp.float32)
    y = xf * lax.rsqrt(jnp.mean(xf * xf, axis=-1, keepdims=True) + EPS)
    return (y * g.astype(jnp.float32)).astype(x.dtype)

def modulate(h, shift, scale):
    return h * (1 + scale[:, None, :]) + shift[:, None, :]

def to_heads(t, n_heads):
    b, s, _ = t.shape
    return t.reshape(b, s, n_heads, -1).transpose(0, 2, 1, 3)

def from_heads(t):
    b, h, s, d = t.shape
    return t.transpose(0, 2, 1, 3).reshape(b, s, h * d)

def mlstm_scan(q, k, v, log_i, log_f):
    b_, h_, s_, d_ = q.shape
    nc = s_ // CHUNK

    def chunks(t):
        return jnp.moveaxis(t.reshape(t.shape[:2] + (nc, CHUNK) + t.shape[3:]), 2, 0)

    xs = (chunks(q), chunks(k), chunks(v), chunks(log_i), chunks(log_f))
    lower = jnp.tril(jnp.ones((CHUNK, CHUNK), dtype=bool))

    def step(carry, inp):
        C, n, m = carry
        qc, kc, vc, li, lf = inp
        bcum = jnp.cumsum(lf, axis=-1)
        gsum = bcum[..., -1]
        log_d = jnp.where(lower, bcum[..., :, None] - bcum[..., None, :] + li[..., None, :], -jnp.inf)
        m_inter = bcum + m[..., None]
        m_t = jnp.maximum(m_inter, jnp.max(log_d, axis=-1))
        s = jnp.einsum('bhtd,bhsd->bhts', qc, kc) * jnp.exp(log_d - m_t[..., None])
        a = jnp.exp(m_inter - m_t)
        num = jnp.einsum('bhts,bhse->bhte', s, vc) + a[..., None] * jnp.einsum('bhtd,bhde->bhte', qc, C)
        den = jnp.sum(s, axis=-1) + a * jnp.einsum('bhtd,bhd->bht', qc, n)
        h = num / jnp.maximum(jnp.abs(den), jnp.exp(-m_t))[..., None]
        log_w = gsum[..., None] - bcum + li
        m_new = jnp.maximum(gsum + m, jnp.max(log_w, axis=-1))
        decay = jnp.exp(gsum + m - m_new)
        w = jnp.exp(log_w - m_new[..., None])
        C = decay[..., None, None] * C + jnp.einsum('bhs,bhsd,bhse->bhde', w, kc, vc)
        n = decay[..., None] * n + jnp.einsum('bhs,bhsd->bhd', w, kc)
        return (C, n, m_new), h

    init = (jnp.zeros((b_, h_, d_, d_), jnp.float32),
            jnp.zeros((b_, h_, d_), jnp.float32),
            jnp.full((b_, h_), -1e30, jnp.float32))
    _, hs = lax.scan(step, init, xs)
    return jnp.moveaxis(hs, 0, 2).reshape(b_, h_, s_, d_)

def mlstm_bidirectional(q, k, v, gates):
    i_f, f_f, i_b, f_b = jnp.split(gates, 4, axis=1)
    h_fwd = mlstm_scan(q, k, v, i_f, jax.nn.log_sigmoid(f_f))
    flip = lambda t: jnp.flip(t, axis=2)
    h_bwd = flip(mlstm_scan(flip(q), flip(k), flip(v), flip(i_b), flip(jax.nn.log_sigmoid(f_b))))
    return h_fwd + h_bwd

def neighborhood_attention(q, k, v, rpb):
    b_, h_, s_, d_ = q.shape
    rows = s_ // GRID_W
    kr = min(WIN_ROWS_MAX, rows)
    kc = WIN_COLS
    grid = lambda t: t.reshape(b_, h_, rows, GRID_W, d_)
    q, k, v = grid(q), grid(k), grid(v)
    row_start = jnp.clip(jnp.arange(rows) - kr // 2, 0, rows - kr)
    cols = jnp.arange(GRID_W)
    col_idx = jnp.clip(cols - kc // 2, 0, GRID_W - kc)[:, None] + jnp.arange(kc)
    dc = col_idx - cols[:, None] + (WIN_COLS - 1)
    scale = d_ ** -0.5

    def row_block(r):
        rs = row_start[r]
        qr = lax.dynamic_index_in_dim(q, r, axis=2, keepdims=False)
        kb = lax.dynamic_slice_in_dim(k, rs, kr, axis=2)[:, :, :, col_idx]
        vb = lax.dynamic_slice_in_dim(v, rs, kr, axis=2)[:, :, :, col_idx]
        dr = rs + jnp.arange(kr) - r + (WIN_ROWS_MAX - 1)
        bias = rpb[:, dr[None, :, None], dc[:, None, :]]
        s = jnp.einsum('bhcd,bhrcjd->bhcrj', qr, kb).astype(jnp.float32) * scale + bias.astype(jnp.float32)
        p = jax.nn.softmax(s.reshape(b_, h_, GRID_W, kr * kc), axis=-1).reshape(s.shape)
        return jnp.einsum('bhcrj,bhrcjd->bhcd', p.astype(v.dtype), vb)

    out = lax.map(row_block, jnp.arange(rows))
    return jnp.moveaxis(out, 0, 2).reshape(b_, h_, s_, d_)

def conv_glu(h, w_up, conv_w, conv_b, w_down):
    u, g = jnp.split(h @ w_up, 2, axis=-1)
    s_ = g.shape[1]
    pad = CONV_W // 2
    gp = jnp.pad(g, ((0, 0), (pad, pad), (0, 0)))
    g = sum(gp[:, j:j + s_] * conv_w[j] for j in range(CONV_W)) + conv_b
    return (jax.nn.gelu(g, approximate=False) * u) @ w_down

def first_inputs(seed: int = 0) -> dict:
    key = jax.random.key(seed)
    ks = jax.random.split(key, 20)
    nrm = jax.random.normal
    f32 = jnp.float32
    x = nrm(ks[0], (BATCH, SEQ, D_MODEL), f32)
    c = nrm(ks[1], (BATCH, D_MODEL), f32)
    w_ada = nrm(ks[2], (DEPTH, D_MODEL, N_MOD * D_MODEL), f32) * (0.5 * D_MODEL ** -0.5)
    b_ada = nrm(ks[3], (DEPTH, N_MOD * D_MODEL), f32) * 0.02
    g_norm1 = 1.0 + 0.02 * nrm(ks[4], (DEPTH, D_MODEL), f32)
    w_in = nrm(ks[5], (DEPTH, D_MODEL, IN_COLS), f32) * D_MODEL ** -0.5
    gk = jax.random.split(ks[6], 4)
    b_gates = jnp.concatenate([
        0.1 * nrm(gk[0], (DEPTH, NH_A), f32),
        3.0 + 0.5 * nrm(gk[1], (DEPTH, NH_A), f32),
        0.1 * nrm(gk[2], (DEPTH, NH_A), f32),
        3.0 + 0.5 * nrm(gk[3], (DEPTH, NH_A), f32),
    ], axis=-1)
    g_head_a = 1.0 + 0.02 * nrm(ks[7], (DEPTH, W_A), f32)
    rpb = 0.1 * nrm(ks[8], (DEPTH, NH_B, 2 * WIN_ROWS_MAX - 1, 2 * WIN_COLS - 1), f32)
    w_out = nrm(ks[9], (DEPTH, D_MIX, D_MODEL), f32) * D_MIX ** -0.5
    g_norm2 = 1.0 + 0.02 * nrm(ks[10], (DEPTH, D_MODEL), f32)
    w_up = nrm(ks[11], (DEPTH, D_MODEL, 2 * D_FF), f32) * D_MODEL ** -0.5
    conv_w = nrm(ks[12], (DEPTH, CONV_W, D_FF), f32) * CONV_W ** -0.5
    conv_b = 0.02 * nrm(ks[13], (DEPTH, D_FF), f32)
    w_down = nrm(ks[14], (DEPTH, D_FF, D_MODEL), f32) * D_FF ** -0.5
    g_final = 1.0 + 0.02 * nrm(ks[15], (D_MODEL,), f32)
    return {'x': x, 'c': c, 'w_ada': w_ada, 'b_ada': b_ada, 'g_norm1': g_norm1, 'w_in': w_in,
            'b_gates': b_gates, 'g_head_a': g_head_a, 'rpb': rpb, 'w_out': w_out, 'g_norm2': g_norm2,
            'w_up': w_up, 'conv_w': conv_w, 'conv_b': conv_b, 'w_down': w_down, 'g_final': g_final}

def first_block(x, c, w_ada, b_ada, g_norm1, w_in, b_gates, g_head_a, rpb, w_out, g_norm2,
              w_up, conv_w, conv_b, w_down, g_final):
    f32 = jnp.float32
    for l in range(DEPTH):
        mod = jax.nn.silu(c) @ w_ada[l] + b_ada[l]
        sh1, sc1, ga1, sh2, sc2, ga2 = jnp.split(mod, N_MOD, axis=-1)

        h = modulate(rms_norm(x, g_norm1[l]), sh1, sc1)
        qa, ka, va, oa, gates, qb, kb, vb = jnp.split(h @ w_in[l], IN_SPLITS, axis=-1)

        q_a = to_heads(qa, NH_A).astype(f32)
        k_a = to_heads(ka, NH_A).astype(f32) * (DH_A ** -0.5)
        v_a = to_heads(va, NH_A).astype(f32)
        g_a = (gates.astype(f32) + b_gates[l].astype(f32)).transpose(0, 2, 1)
        h_a = mlstm_bidirectional(q_a, k_a, v_a, g_a)
        h_a = h_a * lax.rsqrt(jnp.mean(h_a * h_a, axis=-1, keepdims=True) + EPS)
        h_a = (from_heads(h_a) * g_head_a[l] * jax.nn.sigmoid(oa.astype(f32))).astype(x.dtype)

        h_b = from_heads(neighborhood_attention(to_heads(qb, NH_B), to_heads(kb, NH_B),
                                                to_heads(vb, NH_B), rpb[l])).astype(x.dtype)

        mixed = jnp.concatenate([h_a, h_b], axis=-1) @ w_out[l]
        x = x + ga1[:, None, :] * mixed

        h = modulate(rms_norm(x, g_norm2[l]), sh2, sc2)
        x = x + ga2[:, None, :] * conv_glu(h, w_up[l], conv_w[l], conv_b[l], w_down[l])
    return rms_norm(x, g_final)


DEPTH_2 = 2

N_MIXERS = 2
N_A = (DEPTH_2 + N_MIXERS - 1) // N_MIXERS
N_B = DEPTH_2 // N_MIXERS
NORM_EPS = 1e-6

SGU_BLOCK = 128
SGU_WIDTH = 2 * D_MODEL
SGU_GROUPS = 16
SGU_GROUP_DIM = SGU_WIDTH // SGU_GROUPS

MLA_HEADS = 16
Q_LORA_RANK = 448
KV_LORA_RANK = 512
QK_NOPE_DIM = 128
QK_ROPE_DIM = 64
V_HEAD_DIM = 128
MLA_WIDTH = MLA_HEADS * V_HEAD_DIM
ROPE_THETA = 10000.0
Q_BLOCK = 128


def rms_norm_2(x, g):
    xf = x.astype(jnp.float32)
    y = xf * lax.rsqrt(jnp.mean(xf * xf, axis=-1, keepdims=True) + NORM_EPS)
    return (y * g.astype(jnp.float32)).astype(x.dtype)

def layer_norm(x, g):
    xf = x.astype(jnp.float32)
    mu = jnp.mean(xf, axis=-1, keepdims=True)
    var = jnp.mean(jnp.square(xf - mu), axis=-1, keepdims=True)
    return ((xf - mu) * lax.rsqrt(var + NORM_EPS) * g.astype(jnp.float32)).astype(x.dtype)

def apply_rope(x, cos, sin):
    xf = x.astype(jnp.float32)
    x1, x2 = jnp.split(xf, 2, axis=-1)
    return jnp.concatenate([x1 * cos - x2 * sin, x1 * sin + x2 * cos], axis=-1).astype(x.dtype)

def sgu_mixer(h, w_in, norm_g, w_s, b_s, w_out):
    B, S, _ = h.shape
    u, v, z = jnp.split(h @ w_in, 3, axis=-1)
    u = jax.nn.gelu(u, approximate=False)
    v = layer_norm(jax.nn.gelu(v, approximate=False), norm_g)
    t_chunk = jnp.arange(SGU_BLOCK) // CHUNK
    mask = (t_chunk[None, :] <= t_chunk[:, None]).astype(w_s.dtype)
    w = w_s * mask[None]
    vb = v.reshape(B, S // SGU_BLOCK, SGU_BLOCK, SGU_GROUPS, SGU_GROUP_DIM)
    vm = jnp.einsum('gts,bnsgc->bntgc', w, vb) + b_s.T[:, :, None]
    y = u * vm.reshape(B, S, SGU_WIDTH) * jax.nn.silu(z)
    return y @ w_out

def chunk_causal_attention(q_nope, q_rope, k_nope, k_rope, v):
    B, S, H, _ = q_nope.shape
    nqb = S // Q_BLOCK
    scale = (QK_NOPE_DIM + QK_ROPE_DIM) ** -0.5
    k_chunk = jnp.arange(S) // CHUNK

    def to_blocks(t):
        return jnp.moveaxis(t.reshape(B, nqb, Q_BLOCK, *t.shape[2:]), 1, 0)

    def one_block(args):
        idx, qn, qr = args
        s = (jnp.einsum('bqhd,bkhd->bhqk', qn, k_nope)
             + jnp.einsum('bqhd,bkd->bhqk', qr, k_rope)).astype(jnp.float32) * scale
        q_chunk = (idx * Q_BLOCK + jnp.arange(Q_BLOCK)) // CHUNK
        mask = k_chunk[None, :] <= q_chunk[:, None]
        p = jax.nn.softmax(jnp.where(mask, s, -1e30), axis=-1).astype(v.dtype)
        return jnp.einsum('bhqk,bkhd->bqhd', p, v)

    out = lax.map(one_block, (jnp.arange(nqb), to_blocks(q_nope), to_blocks(q_rope)))
    return jnp.moveaxis(out, 0, 1).reshape(B, S, H, V_HEAD_DIM)

def mla_mixer(h, w_in, q_norm_g, kv_norm_g, w_uq, w_ukv, w_out):
    B, S, _ = h.shape
    o1 = Q_LORA_RANK
    o2 = o1 + KV_LORA_RANK
    o3 = o2 + QK_ROPE_DIM
    cq, ckv, k_rope, z = jnp.split(h @ w_in, [o1, o2, o3], axis=-1)
    q = (rms_norm_2(cq, q_norm_g) @ w_uq).reshape(B, S, MLA_HEADS, QK_NOPE_DIM + QK_ROPE_DIM)
    kv = (rms_norm_2(ckv, kv_norm_g) @ w_ukv).reshape(B, S, MLA_HEADS, QK_NOPE_DIM + V_HEAD_DIM)
    q_nope, q_rope = q[..., :QK_NOPE_DIM], q[..., QK_NOPE_DIM:]
    k_nope, v = kv[..., :QK_NOPE_DIM], kv[..., QK_NOPE_DIM:]
    pos = jnp.arange(S, dtype=jnp.float32)
    inv_freq = ROPE_THETA ** (-jnp.arange(0, QK_ROPE_DIM, 2, dtype=jnp.float32) / QK_ROPE_DIM)
    ang = pos[:, None] * inv_freq[None, :]
    cos, sin = jnp.cos(ang), jnp.sin(ang)
    q_rope = apply_rope(q_rope, cos[:, None, :], sin[:, None, :])
    k_rope = apply_rope(k_rope, cos, sin)
    o = chunk_causal_attention(q_nope, q_rope, k_nope, k_rope, v)
    y = o.reshape(B, S, MLA_WIDTH) * jax.nn.silu(z)
    return y @ w_out

def second_inputs(seed: int = 0) -> dict:
    key = jax.random.key(seed)
    ks = jax.random.split(key, 17)
    f32 = jnp.float32
    D = D_MODEL

    def nrm(k, shape, s):
        return jax.random.normal(k, shape, f32) * s

    def gain(k, shape):
        return 1.0 + 0.05 * jax.random.normal(k, shape, f32)

    mla_in_cols = Q_LORA_RANK + KV_LORA_RANK + QK_ROPE_DIM + MLA_WIDTH
    return {
        'x': nrm(ks[0], (BATCH, SEQ, D), 1.0),
        'c': nrm(ks[1], (BATCH, D), 1.0),
        'ada_w': nrm(ks[2], (DEPTH_2, D, 3 * D), 0.5 * D ** -0.5),
        'ada_b': nrm(ks[3], (DEPTH_2, 3 * D), 0.01),
        'pre_g': gain(ks[4], (DEPTH_2, D)),
        'post_g': gain(ks[5], (DEPTH_2, D)),
        'sgu_w_in': nrm(ks[6], (N_A, D, 3 * SGU_WIDTH), D ** -0.5),
        'sgu_norm_g': gain(ks[7], (N_A, SGU_WIDTH)),
        'sgu_w_s': nrm(ks[8], (N_A, SGU_GROUPS, SGU_BLOCK, SGU_BLOCK), SGU_BLOCK ** -0.5),
        'sgu_b_s': gain(ks[9], (N_A, SGU_GROUPS, SGU_BLOCK)),
        'sgu_w_out': nrm(ks[10], (N_A, SGU_WIDTH, D), SGU_WIDTH ** -0.5),
        'mla_w_in': nrm(ks[11], (N_B, D, mla_in_cols), D ** -0.5),
        'mla_q_norm_g': gain(ks[12], (N_B, Q_LORA_RANK)),
        'mla_kv_norm_g': gain(ks[13], (N_B, KV_LORA_RANK)),
        'mla_w_uq': nrm(ks[14], (N_B, Q_LORA_RANK, MLA_HEADS * (QK_NOPE_DIM + QK_ROPE_DIM)), Q_LORA_RANK ** -0.5),
        'mla_w_ukv': nrm(ks[15], (N_B, KV_LORA_RANK, MLA_HEADS * (QK_NOPE_DIM + V_HEAD_DIM)), KV_LORA_RANK ** -0.5),
        'mla_w_out': nrm(ks[16], (N_B, MLA_WIDTH, D), MLA_WIDTH ** -0.5),
    }

def second_block(x, c, ada_w, ada_b, pre_g, post_g, sgu_w_in, sgu_norm_g, sgu_w_s, sgu_b_s, sgu_w_out,
              mla_w_in, mla_q_norm_g, mla_kv_norm_g, mla_w_uq, mla_w_ukv, mla_w_out):
    cond = jax.nn.silu(c)
    for i in range(DEPTH_2):
        mod = cond @ ada_w[i] + ada_b[i]
        shift, scale, gate = jnp.split(mod, 3, axis=-1)
        h = rms_norm_2(x, pre_g[i]) * (1 + scale[:, None, :]) + shift[:, None, :]
        j = i // N_MIXERS
        if i % N_MIXERS == 0:
            y = sgu_mixer(h, sgu_w_in[j], sgu_norm_g[j], sgu_w_s[j], sgu_b_s[j], sgu_w_out[j])
        else:
            y = mla_mixer(h, mla_w_in[j], mla_q_norm_g[j], mla_kv_norm_g[j], mla_w_uq[j], mla_w_ukv[j], mla_w_out[j])
        x = x + gate[:, None, :] * rms_norm_2(y, post_g[i])
    return x


def setup_inputs(seed=0):
    out = dict(first_inputs(seed))
    for name, value in second_inputs(seed + 1).items():
        if name != "x":
            out[name + "_2"] = value
    return out


def reference(
    x, c, w_ada, b_ada, g_norm1, w_in, b_gates, g_head_a, rpb, w_out, g_norm2, w_up, conv_w,
    conv_b, w_down, g_final, c_2, ada_w_2, ada_b_2, pre_g_2, post_g_2, sgu_w_in_2, sgu_norm_g_2,
    sgu_w_s_2, sgu_b_s_2, sgu_w_out_2, mla_w_in_2, mla_q_norm_g_2, mla_kv_norm_g_2, mla_w_uq_2,
    mla_w_ukv_2, mla_w_out_2,
):
    x = first_block(
        x, c, w_ada, b_ada, g_norm1, w_in, b_gates, g_head_a, rpb, w_out, g_norm2, w_up, conv_w,
        conv_b, w_down, g_final,
    )
    return second_block(
        x, c_2, ada_w_2, ada_b_2, pre_g_2, post_g_2, sgu_w_in_2, sgu_norm_g_2, sgu_w_s_2,
        sgu_b_s_2, sgu_w_out_2, mla_w_in_2, mla_q_norm_g_2, mla_kv_norm_g_2, mla_w_uq_2,
        mla_w_ukv_2, mla_w_out_2,
    )


_drawn_inputs = setup_inputs


def setup_inputs(seed=0):
    import zlib

    import numpy as np

    out = dict(_drawn_inputs(seed))
    spreads = {}
    factors = {'g_norm1': 8.0,
     'g_head_a': 8.0,
     'rpb': 8.0,
     'g_norm2': 8.0,
     'conv_b': 8.0,
     'ada_b_2': 3.246,
     'post_g_2': 2.752,
     'sgu_norm_g_2': 6.012,
     'sgu_b_s_2': 5.077,
     'mla_q_norm_g_2': 8.0,
     'mla_kv_norm_g_2': 3.817}
    for name, (base, spread) in spreads.items():
        noise = np.random.default_rng([zlib.crc32(name.encode()), seed]).standard_normal(out[name].shape)
        drawn = base * np.exp(spread * noise) if base else spread * noise
        out[name] = __import__('jax').numpy.asarray(drawn.astype(out[name].dtype))
    for name, factor in factors.items():
        out[name] = (out[name] * factor).astype(out[name].dtype)
    return out
```

```python
from contextlib import ExitStack

import concourse.bass as bass
import numpy as np
from concourse import mybir

F32 = mybir.dt.float32
ALU = mybir.AluOpType
ACT = mybir.ActivationFunctionType
AX = mybir.AxisListType

P = 128
D = 2048
KC = D // P
T = 256
TT = T // P
COLS = 256
RING = 4
EPS = 1e-6
NEG = -1e30

NH_A, DH_A = 4, 256
NH_B, DH_B = 8, 128
GRID_W, WIN_COLS, ROWS = 64, 16, 4
D_FF = 5632
FC = D_FF // P
SGU_W = 4096
SC = SGU_W // P
GROUPS = 16
MH, NOPE, ROPE, VD = 16, 128, 64, 128
QR, KVR = 448, 512
SCALE_A = DH_A ** -0.5
SCALE_B = DH_B ** -0.5
SCALE_M = (NOPE + ROPE) ** -0.5
GROW = 36

STAGES = [("w_in", 28), ("w_out", 8), ("w_up", 44), ("w_down", 32), ("sgu_v", 16), ("sgu_u", 16),
          ("mix", 4), ("sgu_z", 16), ("sgu_out", 16), ("lat", 4), ("mla_z", 8), ("heads", 16), ("mla_out", 8)]
NBLOCKS = dict(STAGES)
TRIP, BASE, _trip, _n = {}, {}, 0, 0
for _name, _blocks in STAGES:
    TRIP[_name], BASE[_name] = _trip, _n
    _trip += _blocks // RING
    _n += _blocks if _name != "mix" else 0
BLOCK_ELEMS = {"w_down": 11 * COLS, "mix": 4 * 2 * P, "heads": 4 * 448}
W_DOWN_KC = 11

SH1, SC1, GA1, SH2, SC2, GA2, S0, C0, G0, S1, C1, G1 = range(12)
UNITS = 4
UCOLS = D // UNITS
QUARTS = 4
QKC = KC // QUARTS
VQ = UNITS * QUARTS

PCOL, _n = {}, 0
for _name, _cols in [("c", KC), ("c2", KC), ("bias", 12 * KC), ("g1", KC), ("ghead", 8), ("g2", KC),
                     ("conv", FC * 4), ("gfinal", KC), ("pre", 2 * KC), ("post", 2 * KC), ("gsgu", SC),
                     ("gq", 4), ("gkv", 4), ("bi", 1), ("bf", 1)]:
    PCOL[_name] = _n
    _n += _cols
NPAR = _n

NORMS = [("norm1", 4), ("norm2", 4), ("final", 4), ("pre0", 4), ("post0", 4), ("pre1", 4), ("kv", 1), ("q", 1), ("post1", 4)]
NORM_INDEX = {n: i for i, (n, _) in enumerate(NORMS)}
SQ_BEFORE = {n: sum(c for _, c in NORMS[:i]) for i, (n, _) in enumerate(NORMS)}

W_IN_STEPS = {11: [("sum", GA1), ("scores", 0)], 13: [("mix", 0)], 14: [("norm", 0), ("scores", 1)], 15: [("mix", 1)],
              16: [("norm", 1), ("scores", 2)], 17: [("mix", 2)], 18: [("norm", 2), ("scores", 3)], 19: [("mix", 3)],
              20: [("norm", 3)], 22: [("sum", SH2)], 27: [("sum", SC2)]}


def waves(jobs, stages):
    return [(w - j, j) for w in range(jobs + stages - 1) for j in range(jobs) if 0 <= w - j < stages]


class Chain:

    def __init__(self, eng, sem):
        self.eng, self.sem, self.count, self.i, self.per = eng, sem, 0, None, 0

    def link(self, ins):
        ins.then_inc(self.sem, 1)
        self.count += 1
        self.eng.wait_ge(self.sem, self.count if self.i is None else self.i * self.per + self.count)

    def enter(self, i, per):
        self.i, self.per, self.start = i, per, self.count

    def leave(self, trips):
        assert self.count - self.start == self.per, (self.count - self.start, self.per)
        self.count = self.start + trips * self.per
        self.i = None


def build(nc, a):
    with ExitStack() as ctx:
        def sb(name, shape):
            return ctx.enter_context(nc.sbuf_tensor(name, shape, F32))

        def sem(name):
            return ctx.enter_context(nc.semaphore(name))

        x = sb("x", [P, KC, T])
        h = sb("h", [P, KC, T])
        ring = sb("ring", [P, RING, KC * COLS])
        ada = sb("ada", [P, 2, QKC * UCOLS])
        acc = sb("acc", [P, 2, D])
        par = sb("par", [P, NPAR])
        mods = sb("mods", [P, 12, KC])
        csil = sb("csil", [P, 2, KC])
        gain = sb("gain", [P, 5, KC])
        ident = sb("ident", [P, P])
        ones = sb("ones", [P, P])
        rstd = sb("rstd", [P, T])
        work = sb("work", [P, 18500])
        pm = [ctx.enter_context(nc.psum_tensor(f"pm{b}", [P, 512], F32)) for b in range(4)]
        px = [ctx.enter_context(nc.psum_tensor(f"px{b}", [P, 512], F32)) for b in range(4)]
        used = [0]

        def area(n, at=None):
            o = used[0] if at is None else at
            if at is None:
                used[0] += n
            assert o + n <= 18500, (o, n)
            return work[:, o:o + n]

        def split(ap, n, m):
            return ap.rearrange("p (a b) -> p a b", a=n, b=m)

        o_ka, o_qa = 0, 2048
        ka = split(area(2048), 8, T)
        qa = split(area(2048), 8, T)
        va = split(area(2048), 2, 1024)
        oa = split(area(2048), 8, T)
        qb = split(area(2048), 8, T)
        kb = split(work[:, o_ka:o_ka + 2048], 8, T)
        vb = split(work[:, o_qa:o_qa + 2048], 2, 1024)
        gates = split(work[:, 4 * 2048:5 * 2048], 8, T)
        bias_b = area(3072)
        gate_w = bias_b[:, 0:2 * KC * GROW].rearrange("p (a k m) -> p a k m", a=2, k=KC)
        neg_rows = area(512)
        bcol = split(area(2 * GROW), 2, GROW)
        mask_a = split(area(1024), 2, 512)
        decay = split(area(1024), 2, 512)
        expm = split(area(512), 2, T)
        hf = split(area(512), 2, T)
        hb = split(area(512), 2, T)
        mix_end = used[0]
        wmask = decay[:, 0, 0:64]
        s_b = [decay[:, j, :].rearrange("p (a b) -> p a b", a=2) for j in range(2)]
        pt_b = [split(work[:, mix_end - 1536 + 512 * j:mix_end - 1024 + 512 * j], 2, T) for j in range(2)]
        small_b = sb("small_b", [P, 2, 4, 2])
        glu = split(work[:, 0:FC * T], FC, T)
        gpad = split(work[:, FC * T:FC * T + 2 * 258], 2, 258)
        conv = split(work[:, FC * T + 516:FC * T + 516 + 512], 2, T)
        v_sgu = split(work[:, 0:2 * SGU_W], TT, SGU_W)
        gu = split(work[:, 2 * SGU_W:2 * SGU_W + SC * T], SC, T)
        stmp = split(work[:, 16384:16384 + 1024], 2, 512)
        ysq = split(work[:, 0:KC * T], KC, T)
        stat = sb("stat", [P, 2, 32])
        lat = split(work[:, 0:2048], 8, T)
        zo = split(work[:, 2048:2048 + 4096], MH, T)
        cst = work[:, 6144:6144 + 1024]
        cos, sin, mask_m, rot = cst[0:64, 0:256], cst[0:64, 256:512], cst[:, 512:896], cst[0:64, 896:1024]
        kro = work[0:64, 7168:7424]
        lsq = split(work[:, 7424:7424 + 2048], 8, T)
        hd = split(work[:, 9472:9472 + 4 * 2048], 4, 2048)
        qn = [hd[:, j, 0:256] for j in range(4)]
        qr = [hd[0:64, j, 256:512] for j in range(4)]
        kv = [hd[:, j, 512:1024] for j in range(4)]
        pr = [hd[:, j, 1024:1408] for j in range(4)]
        pt = [hd[:, j, 1408:1792] for j in range(4)]
        rt = [hd[0:64, j, 1792:2048] for j in range(4)]
        small_m = sb("small_m", [P, 4, 4, 2])

        const_in = sem("const_in")
        x_in = sem("x_in")
        mix_const_in = sem("mix_const_in")
        bias_in = sem("bias_in")
        mla_const_in = sem("mla_const_in")
        slot_full = [sem(f"slot_full{s}") for s in range(RING)]
        block_done = sem("block_done")
        bank_free = [sem(f"bank_free{b}") for b in range(4)]
        ada_full = [sem(f"ada_full{s}") for s in range(2)]
        ada_used = sem("ada_used")
        vec_summed = sem("vec_summed")
        vec_taken = sem("vec_taken")
        silu_c = sem("silu_c")
        ones_set = sem("ones_set")
        sq_ready = sem("sq_ready")
        ss_ready = sem("ss_ready")
        ms_ready = sem("ms_ready")
        std_ready = sem("std_ready")
        xn_ready = sem("xn_ready")
        h_ready = sem("h_ready")
        x_ready = sem("x_ready")
        dve_step = sem("dve_step")
        act_step = sem("act_step")
        gate_ps = sem("gate_ps")
        gate_rows = sem("gate_rows")
        gate_exp = sem("gate_exp")
        rows_ready = sem("rows_ready")
        bcol_ps = sem("bcol_ps")
        bcol_ready = sem("bcol_ready")
        a_scores = sem("a_scores")
        a_arg = sem("a_arg")
        a_exp = sem("a_exp")
        a_probs = sem("a_probs")
        a_num = sem("a_num")
        a_h = sem("a_h")
        a_sq = sem("a_sq")
        a_ss = sem("a_ss")
        a_ms = sem("a_ms")
        a_std = sem("a_std")
        a_out = sem("a_out")
        b_scores = sem("b_scores")
        b_negmax = sem("b_negmax")
        b_exp = sem("b_exp")
        b_probs = sem("b_probs")
        b_pt = sem("b_pt")
        b_ptsb = sem("b_ptsb")
        b_num = sem("b_num")
        b_out = sem("b_out")
        mask_ready = sem("mask_ready")
        g_copied = sem("g_copied")
        conv_ready = sem("conv_ready")
        gelu_ready = sem("gelu_ready")
        pad_set = sem("pad_set")
        v_mean = sem("v_mean")
        v_sq = sem("v_sq")
        v_var = sem("v_var")
        v_std = sem("v_std")
        v_normed = sem("v_normed")
        vm_ready = sem("vm_ready")
        vm_taken = sem("vm_taken")
        z_silu = sem("z_silu")
        lat_ready = sem("lat_ready")
        kr_rot = sem("kr_rot")
        m_proj = sem("m_proj")
        m_rot = sem("m_rot")
        m_rope = sem("m_rope")
        m_scores = sem("m_scores")
        m_negmax = sem("m_negmax")
        m_exp = sem("m_exp")
        m_probs = sem("m_probs")
        m_pt = sem("m_pt")
        m_ptsb = sem("m_ptsb")
        m_num = sem("m_num")
        m_out = sem("m_out")
        out_done = sem("out_done")

        BANK, _taken = {}, [0] * 4
        for name, blocks in STAGES:
            BANK[name] = list(_taken)
            grouped = {"w_down": 8, "sgu_out": 8}
            if name in grouped:
                _taken = [t + grouped[name] // 2 * (b < 2) for b, t in enumerate(_taken)]
            elif name != "mix":
                _taken = [t + blocks // 4 for t in _taken]
        BANK["end"] = list(_taken)

        def flat(ap):
            return ap.rearrange("p a b -> p (a b)")

        def pcol(name, c, rows=slice(0, P)):
            c = c + PCOL[name]
            return par[rows, c:c + 1] if isinstance(c, int) else par[rows, bass.ds(c, 1)]

        def pcols(name, n, c=0):
            return par[:, PCOL[name] + c:PCOL[name] + c + n]

        def at(ap, i, n=1):
            return ap[:, i:i + n, :] if isinstance(i, int) else ap[:, bass.ds(i, n), :]

        def one(ap, i):
            return at(ap, i).rearrange("p a b -> p (a b)")

        def over(ap, n):
            return ap.unsqueeze(1).to_broadcast([ap.shape[0], n, ap.shape[1]])

        def wait_banks(eng, name):
            for b in range(4):
                if BANK[name][b]:
                    eng.wait_ge(bank_free[b], BANK[name][b])

        block = ctx.enter_context(nc.Block())

        @block.sync
        def _(sp):
            sp.dma_start(par[:, :], a["par"]).then_inc(const_in, 16)
            sp.dma_start(ident[:, :], a["ident"]).then_inc(const_in, 16)
            sp.dma_start(flat(x[:, :, :]), a["x"]).then_inc(x_in, 16)
            sp.dma_start(bias_b[:, 0:2 * KC * GROW], a["gate_w"]).then_inc(mix_const_in, 16)
            sp.dma_start(flat(mask_a), a["mask_a"]).then_inc(mix_const_in, 16)
            sp.dma_start(wmask, a["wmask"]).then_inc(mix_const_in, 16)

            def load(name, s, trip):
                elems = BLOCK_ELEMS.get(name, KC * COLS)
                n = trip * RING + s
                src = a[name][n] if isinstance(n, int) else a[name][bass.ds(n, 1)].rearrange("o p n -> (o p) n")
                sp.dma_start(ring[:, s, 0:elems], src).then_inc(slot_full[s], 16)

            for name, blocks in STAGES:
                first = 0
                if name == "w_in":
                    for s in range(RING):
                        load(name, s, 0)
                    first = 1
                    sp.wait_ge(gate_ps, 1)
                    sp.dma_start(bias_b, a["bias_b"]).then_inc(bias_in, 16)
                if name == "sgu_z":
                    for s in range(RING):
                        sp.wait_ge(vm_taken, RING * (s + 1))
                        load(name, s, 0)
                    first = 1
                if name == "mla_z":
                    sp.wait_ge(block_done, BASE["lat"])
                    sp.dma_start(cst, a["mla_cst"]).then_inc(mla_const_in, 16)
                if blocks // RING > first:
                    with sp.Fori(first, blocks // RING) as i:
                        for s in range(RING):
                            sp.wait_ge(block_done, i * RING + (BASE[name] - RING + s + 1))
                            load(name, s, i)
            sp.wait_ge(x_ready, 3)
            sp.dma_start(a["out"], flat(x[:, :, :])).then_inc(out_done, 16)
            sp.wait_ge(out_done, 16)

        @block.gpsimd
        def _(pool):
            for s in range(2):
                pool.dma_start(ada[:, s, :], a["ada"][s]).then_inc(ada_full[s], 16)
            with pool.Fori(1, 12 * VQ // 2) as i:
                for s in range(2):
                    pool.wait_ge(ada_used, i * 2 + s - 1)
                    pool.dma_start(ada[:, s, :], a["ada"][bass.ds(i * 2 + s, 1)].rearrange("o p n -> (o p) n")
                                   ).then_inc(ada_full[s], 16)

        @block.tensor
        def _(pe):
            def columns(s, stage, trip, bank, act, kcs, first=True, last=True, elems=None):
                pe.wait_ge(slot_full[s], (trip + (TRIP[stage] + 1)) * 16)
                w = ring[:, s, 0:kcs * COLS].rearrange("p (k n) -> p k n", k=kcs)
                for kc in range(kcs):
                    for j in range(2):
                        mm = pe.matmul(pm[bank][:, j * T:(j + 1) * T], w[:, kc, j * P:(j + 1) * P], act(kc),
                                       start=(first and kc == 0 and j == 0), stop=(last and kc == kcs - 1),
                                       skip_group_check=True)
                mm.then_inc(block_done, 1)

            def tokens(s, stage, trip, bank):
                pe.wait_ge(slot_full[s], (trip + (TRIP[stage] + 1)) * 16)
                w = ring[:, s, :].rearrange("p (k n) -> p k n", k=KC)
                for tt in range(TT):
                    for kc in range(KC):
                        mm = pe.matmul(pm[bank][:, tt * COLS:(tt + 1) * COLS], h[:, kc, tt * P:(tt + 1) * P], w[:, kc, :],
                                       start=(kc == 0), stop=(kc == KC - 1))
                mm.then_inc(block_done, 1)

            def stage_columns(name, act, lo=0, hi=None):
                with pe.Fori(lo, hi or NBLOCKS[name] // RING) as i:
                    for s in range(RING):
                        pe.wait_ge(bank_free[s], i + BANK[name][s])
                        columns(s, name, i, s, act, KC)

            def sum_vector(v):
                pe.wait_ge(ada_used, VQ * (v + 1))
                if v:
                    pe.wait_ge(vec_taken, v)
                for c in range(KC):
                    mm = pe.matmul(px[3][:, c:c + 1], acc[:, v % 2, c * P:(c + 1) * P], ones[:, 0:1], start=True, stop=True)
                mm.then_inc(vec_summed, 1)

            def sum_squares(name, chunks):
                k = NORM_INDEX[name]
                if k:
                    pe.wait_ge(ms_ready, k)
                n, total = 0, sum(len(p) for p in chunks)
                for p, piece in enumerate(chunks):
                    pe.wait_ge(sq_ready, SQ_BEFORE[name] + p + 1)
                    for rows, ap in piece:
                        mm = pe.matmul(px[0][:, 0:T], ones[rows, :], ap, start=(n == 0), stop=(n == total - 1))
                        n += 1
                mm.then_inc(ss_ready, 1)

            def quarters(ap):
                return [[(slice(0, P), ap[:, kc, :]) for kc in range(4 * p, 4 * p + 4)] for p in range(4)]

            def h_chunk(kc):
                return h[:, kc, :]

            pe.wait_ge(const_in, 32)
            pe.wait_ge(ones_set, 1)
            sum_squares("norm1", quarters(h))
            sum_vector(SH1)
            sum_vector(SC1)
            pe.wait_ge(h_ready, KC)

            pe.wait_ge(mix_const_in, 48)
            for g in range(2):
                for kc in range(KC):
                    mm = pe.matmul(px[0][0:GROW, g * T:(g + 1) * T], gate_w[:, g, kc, :], h[:, kc, :],
                                   start=(kc == 0), stop=(kc == KC - 1))
            mm.then_inc(gate_ps, 1)

            def a_head_scores(hd_):
                pe.wait_ge(rows_ready, 1)
                if hd_ == 0:
                    for b in range(4):
                        pe.wait_ge(bank_free[b], 3)
                else:
                    pe.wait_ge(a_out, hd_)
                for sc in range(TT):
                    for dc in range(2):
                        pe.matmul(px[0][:, sc * T:(sc + 1) * T], ka[:, 2 * hd_ + dc, sc * P:(sc + 1) * P],
                                  qa[:, 2 * hd_ + dc, :], start=(dc == 0), stop=(dc == 1))
                for d in range(2):
                    r = hd_ + 32 * d
                    mm = pe.matmul(px[1 + d][:, :], ident[0:GROW, r:r + 1].to_broadcast([GROW, P]), neg_rows[0:GROW, :],
                                   start=True, stop=True)
                mm.then_inc(a_scores, 1)

            def a_head_mix(hd_):
                pe.wait_ge(a_probs, 2 * hd_ + 2)
                if hd_ == 0:
                    pe.wait_ge(vec_taken, GA1 + 1)
                else:
                    pe.wait_ge(a_ms, hd_)
                for d in range(2):
                    for sc in range(TT):
                        pe.matmul(px[3][:, d * T:(d + 1) * T], ones[:, :], decay[:, d, sc * T:(sc + 1) * T],
                                  start=(sc == 0), stop=(sc == 1))
                    for ec in range(2):
                        for sc in range(TT):
                            mm = pe.matmul(px[1 + d][:, ec * T:(ec + 1) * T],
                                           va[:, sc, hd_ * DH_A + ec * P:hd_ * DH_A + (ec + 1) * P],
                                           decay[:, d, sc * T:(sc + 1) * T], start=(sc == 0), stop=(sc == 1))
                mm.then_inc(a_num, 1)

            def a_head_norm(hd_):
                pe.wait_ge(a_sq, hd_ + 1)
                for ec in range(2):
                    mm = pe.matmul(px[3][:, 0:T], ones[:, :], hb[:, ec, :], start=(ec == 0), stop=(ec == 1))
                mm.then_inc(a_ss, 1)

            for n in range(NBLOCKS["w_in"]):
                s, trip, group = n % RING, n // RING, n // 4
                if trip:
                    pe.wait_ge(bank_free[s], trip)
                if group in (2, 6):
                    tokens(s, "w_in", trip, s)
                else:
                    columns(s, "w_in", trip, s, h_chunk, KC)
                if n == 3:
                    pe.wait_ge(rows_ready, 1)
                    for sc in range(TT):
                        mm = pe.transpose(px[1][:, sc * GROW:(sc + 1) * GROW], gates[0:GROW, 5, sc * P:(sc + 1) * P],
                                          ident[0:GROW, 0:GROW])
                    mm.then_inc(bcol_ps, 1)
                for step, k in W_IN_STEPS.get(n, []):
                    if step == "sum":
                        if k == SH2:
                            pe.wait_ge(a_out, NH_A)
                        sum_vector(k)
                    else:
                        {"scores": a_head_scores, "mix": a_head_mix, "norm": a_head_norm}[step](k)

            for st, hd_ in waves(NH_B, 3):
                bank = px[hd_ % 4]
                if st == 0:
                    if hd_ == 0:
                        wait_banks(pe, "w_out")
                        pe.wait_ge(vec_taken, SC2 + 1)
                    if hd_ >= 4:
                        pe.wait_ge(b_out, hd_ - 3)
                    for tt in range(TT):
                        mm = pe.matmul(bank[:, tt * T:(tt + 1) * T], qb[:, hd_, tt * P:(tt + 1) * P], kb[:, hd_, :],
                                       start=True, stop=True)
                    mm.then_inc(b_scores, 1)
                elif st == 1:
                    pe.wait_ge(b_probs, hd_ + 1)
                    for sc in range(TT):
                        for tt in range(TT):
                            mm = pe.transpose(bank[:, sc * T + tt * P:sc * T + (tt + 1) * P],
                                              s_b[hd_ % 2][:, tt, sc * P:(sc + 1) * P], ident[:, :])
                    mm.then_inc(b_pt, 1)
                else:
                    pe.wait_ge(b_ptsb, hd_ + 1)
                    for sc in range(TT):
                        mm = pe.matmul(bank[:, 0:T], vb[:, sc, hd_ * DH_B:(hd_ + 1) * DH_B], pt_b[hd_ % 2][:, sc, :],
                                       start=(sc == 0), stop=(sc == 1))
                    mm.then_inc(b_num, 1)

            pe.wait_ge(b_out, NH_B)
            stage_columns("w_out", lambda kc: oa[:, kc, :] if kc < 8 else qb[:, kc - 8, :])
            sum_vector(GA2)
            sum_squares("norm2", quarters(h))
            pe.wait_ge(h_ready, 2 * KC)

            stage_columns("w_up", h_chunk, 0, 8)
            sum_vector(S0)
            stage_columns("w_up", h_chunk, 8)
            sum_vector(C0)
            wait_banks(pe, "w_down")
            with pe.Fori(0, 4) as i:
                for g in range(2):
                    pe.wait_ge(bank_free[g], i + BANK["w_down"][g])
                    for s in range(RING):
                        columns(s, "w_down", i * 2 + g, g, lambda kc: glu[:, s * W_DOWN_KC + kc, :], W_DOWN_KC,
                                first=(s == 0), last=(s == RING - 1))
            sum_squares("final", quarters(h))
            sum_squares("pre0", quarters(h))
            pe.wait_ge(h_ready, 3 * KC)

            with pe.Fori(0, NBLOCKS["sgu_v"] // RING) as i:
                for s in range(RING):
                    pe.wait_ge(bank_free[s], i + BANK["sgu_v"][s])
                    tokens(s, "sgu_v", i, s)
            stage_columns("sgu_u", h_chunk)
            sum_vector(G0)
            pe.wait_ge(v_normed, 2)
            for g in range(GROUPS):
                s, r = divmod(g, 4)
                if r == 0:
                    pe.wait_ge(slot_full[s], (TRIP["mix"] + 1) * 16)
                if g < 4:
                    pe.wait_ge(vec_taken, G0 + 1)
                else:
                    pe.wait_ge(vm_taken, g - 3)
                w = ring[:, s, 0:4 * 2 * P].rearrange("p (r a t) -> p r a t", r=4, a=2)
                for c in range(2):
                    for n in range(TT):
                        for chunk in range(2):
                            seen = slice(0, 64 * (chunk + 1))
                            t0 = 64 * chunk
                            mm = pe.matmul(px[g % 4][:, c * T + n * P + t0:c * T + n * P + t0 + 64],
                                           v_sgu[seen, n, g * 2 * P + c * P:g * 2 * P + (c + 1) * P],
                                           w[seen, r, 0, t0:t0 + 64], start=True, stop=True)
                mm.then_inc(vm_ready, 1)
            stage_columns("sgu_z", h_chunk)
            sum_vector(S1)
            wait_banks(pe, "sgu_out")
            with pe.Fori(0, 4) as i:
                for g in range(2):
                    pe.wait_ge(bank_free[g], i + BANK["sgu_out"][g])
                    for kb_ in range(2):
                        columns(2 * g + kb_, "sgu_out", i, g, lambda kc: gu[:, kb_ * KC + kc, :], KC,
                                first=(kb_ == 0), last=(kb_ == 1))
            sum_vector(C1)
            sum_squares("post0", quarters(ysq))
            sum_squares("pre1", quarters(h))
            pe.wait_ge(h_ready, 4 * KC)

            stage_columns("lat", h_chunk)
            stage_columns("mla_z", h_chunk)
            full = slice(0, P)
            sum_squares("kv", [[(full, lsq[:, c, :]) for c in range(4)]])
            sum_squares("q", [[(full, lsq[:, c, :]) for c in range(4, 7)] + [(slice(64, P), lsq[64:P, 7, :])]])
            pe.wait_ge(mla_const_in, 16)
            pe.matmul(px[1][:, 0:T], rot, lat[0:64, 7, :], start=True, stop=True).then_inc(kr_rot, 1)
            pe.wait_ge(lat_ready, 3)
            with pe.Fori(0, MH // 4) as i:
                for st, j in waves(4, 5):
                    w = ring[:, j, 0:4 * 448].rearrange("p (k n) -> p k n", k=4)
                    hn = i * 4 + j
                    if st == 0:
                        pe.wait_ge(slot_full[j], (i + (TRIP["heads"] + 1)) * 16)
                        pe.wait_ge(bank_free[j], i + BANK["heads"][j])
                        for lo, n, dst in ((0, NOPE, pm[j][:, 0:T]), (NOPE, ROPE, pm[j][0:ROPE, T:2 * T])):
                            for kc in range(4):
                                rows = slice(0, P) if kc < 3 else slice(64, P)
                                pe.matmul(dst, w[rows, kc, lo:lo + n], lat[rows, 4 + kc, :], start=(kc == 0), stop=(kc == 3))
                        for kc in range(4):
                            pe.matmul(px[j][:, 0:T], w[:, kc, 192:320], lat[:, kc, :], start=(kc == 0), stop=(kc == 3))
                        for tt in range(TT):
                            for kc in range(4):
                                mm = pe.matmul(px[j][:, T + tt * P:T + (tt + 1) * P], lat[:, kc, tt * P:(tt + 1) * P],
                                               w[:, kc, 320:448], start=(kc == 0), stop=(kc == 3))
                        mm.then_inc(block_done, 1)
                    elif st == 1:
                        pe.wait_ge(m_proj, hn + 1)
                        pe.matmul(px[j][:, 0:T], rot, qr[j], start=True, stop=True).then_inc(m_rot, 1)
                    elif st == 2:
                        pe.wait_ge(m_rope, hn + 1)
                        for lo, tt in ((0, 0), (P, 1)):
                            keys = P * (tt + 1)
                            pe.matmul(pm[j][:, lo:lo + keys], qn[j][:, tt * P:(tt + 1) * P], kv[j][:, 0:keys],
                                      start=True, stop=False)
                            mm = pe.matmul(pm[j][:, lo:lo + keys], qr[j][:, tt * P:(tt + 1) * P], kro[:, 0:keys],
                                           start=False, stop=True)
                        mm.then_inc(m_scores, 1)
                    elif st == 3:
                        pe.wait_ge(m_probs, hn + 1)
                        for lo, src in ((0, 0), (P, P), (2 * P, 2 * P)):
                            mm = pe.transpose(px[j][:, lo:lo + P], pr[j][:, src:src + P], ident[:, :])
                        mm.then_inc(m_pt, 1)
                    else:
                        pe.wait_ge(m_ptsb, hn + 1)
                        pe.matmul(pm[j][:, 0:T], kv[j][:, T:T + P], pt[j][:, 0:T], start=True, stop=False, skip_group_check=True)
                        pe.matmul(pm[j][:, P:T], kv[j][:, T + P:2 * T], pt[j][:, T:T + P], start=False, stop=True,
                                  skip_group_check=True).then_inc(m_num, 1)
            wait_banks(pe, "mla_out")
            stage_columns("mla_out", lambda kc: zo[:, kc, :])
            sum_vector(G1)
            sum_squares("post1", quarters(ysq))

        @block.scalar
        def _(act):
            chain = Chain(act, act_step)

            def squares(name, dst, src):
                for p in range(4):
                    act.activation(dst[:, 4 * p:4 * p + 4, :], src[:, 4 * p:4 * p + 4, :], ACT.Square).then_inc(sq_ready, 1)

            def root(name):
                act.wait_ge(ms_ready, NORM_INDEX[name] + 1)
                act.activation(rstd[:, :], rstd[:, :], ACT.Sqrt).then_inc(std_ready, 1)

            def modulate(k, shift):
                for kc in range(KC):
                    act.wait_ge(xn_ready, k * KC + kc + 1)
                    act.activation(h[:, kc, :], h[:, kc, :], ACT.Identity, bias=mods[:, shift, kc:kc + 1],
                                   scale=gain[:, k, kc:kc + 1]).then_inc(h_ready, 1)

            def stage_copy(name, dst, func=ACT.Copy):
                with act.Fori(0, NBLOCKS[name] // RING) as i:
                    for s in range(RING):
                        act.wait_ge(block_done, i * RING + (BASE[name] + s + 1))
                        act.activation(at(dst, i * 8 + 2 * s, 2), pm[s][:, :], func).then_inc(bank_free[s], 1)

            act.wait_ge(const_in, 32)
            act.activation(csil[:, :, :].rearrange("p a k -> p (a k)"), pcols("c", 2 * KC), ACT.Silu).then_inc(silu_c, 1)
            act.wait_ge(x_in, 16)
            squares("norm1", h, x)
            root("norm1")
            modulate(0, SH1)

            act.wait_ge(gate_rows, 1)
            chain.link(act.activation(gates[0:GROW, 3, :], gates[0:GROW, 2, :], ACT.Exp))
            act.activation(gates[0:GROW, 3, :], gates[0:GROW, 3, :], ACT.Ln, bias=1.0).then_inc(gate_exp, 1)

            def a_head_scores(hd_):
                for d in range(2):
                    r = hd_ + 32 * d
                    act.wait_ge(a_arg, 2 * hd_ + d + 1)
                    for sc in range(TT):
                        act.activation(decay[:, d, sc * T:(sc + 1) * T], decay[:, d, sc * T:(sc + 1) * T], ACT.Exp,
                                       bias=bcol[:, sc, r:r + 1])
                    act.activation(expm[:, d, :], px[1 + d][:, T:2 * T], ACT.Exp).then_inc(a_exp, 1)

            def a_head_mix(hd_):
                act.wait_ge(a_h, hd_ + 1)
                act.activation(hb, hf, ACT.Square).then_inc(a_sq, 1)

            def a_head_norm(hd_):
                act.wait_ge(a_ms, hd_ + 1)
                act.activation(expm[:, 0, :], expm[:, 0, :], ACT.Sqrt).then_inc(a_std, 1)

            dsts = [ka, qa, va, oa, qb, kb, vb]
            for n in range(NBLOCKS["w_in"]):
                group, s = divmod(n, 4)
                act.wait_ge(block_done, n + 1)
                if group in (2, 6):
                    dst = dsts[group][:, :, s * COLS:(s + 1) * COLS]
                else:
                    dst = dsts[group][:, 2 * s:2 * s + 2, :]
                if n == 16:
                    act.wait_ge(rows_ready, 1)
                    act.wait_ge(bcol_ready, 1)
                act.activation(dst, pm[s][:, :].rearrange("p (a b) -> p a b", a=2), ACT.Sigmoid if group == 3 else ACT.Copy
                               ).then_inc(bank_free[s], 1)
                for step, k in W_IN_STEPS.get(n, []):
                    if step != "sum":
                        {"scores": a_head_scores, "mix": a_head_mix, "norm": a_head_norm}[step](k)

            for st, hd_ in waves(NH_B, 3):
                j = hd_ % 2
                if st == 0:
                    act.wait_ge(b_negmax, hd_ + 1)
                    for tt in range(TT):
                        ex = act.activation(s_b[j][:, tt, :], s_b[j][:, tt, :], ACT.Exp, bias=small_b[:, j, 1, tt:tt + 1],
                                            accum_out=small_b[:, j, 2, tt:tt + 1])
                    ex.then_inc(b_exp, 1)
                elif st == 1:
                    act.wait_ge(b_pt, hd_ + 1)
                    if hd_ >= 2:
                        act.wait_ge(b_num, hd_ - 1)
                    act.activation(flat(pt_b[j]), px[hd_ % 4][:, :], ACT.Copy).then_inc(b_ptsb, 1)
                else:
                    act.wait_ge(b_num, hd_ + 1)
                    act.activation(qb[:, hd_, :], px[hd_ % 4][:, 0:T], ACT.Copy).then_inc(b_out, 1)

            wait_banks(act, "w_up")
            squares("norm2", h, x)
            root("norm2")
            modulate(1, SH2)

            with act.Fori(0, NBLOCKS["w_up"] // RING) as i:
                for s in range(RING):
                    k = i * RING + s
                    j = s % 2
                    act.wait_ge(block_done, k + (BASE["w_up"] + 1))
                    act.wait_ge(bank_free[(s + 2) % 4], i + (BANK["w_up"][(s + 2) % 4] + (s >= 2)))
                    act.activation(gpad[:, j, 1:1 + T], pm[s][:, 0:T], ACT.Copy).then_inc(g_copied, 1)
                    act.wait_ge(conv_ready, k + 1)
                    act.activation(conv[:, j, :], conv[:, j, :], ACT.Gelu).then_inc(gelu_ready, 1)

            wait_banks(act, "sgu_v")
            squares("final", h, x)
            root("final")
            act.wait_ge(x_ready, 1)
            squares("pre0", h, x)
            root("pre0")
            modulate(2, S0)

            with act.Fori(0, NBLOCKS["sgu_v"] // RING) as i:
                for s in range(RING):
                    act.wait_ge(block_done, i * RING + (BASE["sgu_v"] + s + 1))
                    for tt in range(TT):
                        ge = act.activation(v_sgu[:, tt, bass.ds((i * RING + s) * COLS, COLS)], pm[s][:, tt * COLS:(tt + 1) * COLS],
                                            ACT.Gelu, accum_out=stat[:, tt, bass.ds(i * RING + s, 1)])
                    ge.then_inc(bank_free[s], 1)
            for tt in range(TT):
                act.wait_ge(v_mean, tt + 1)
                for p in range(8):
                    chain.link(act.activation(stmp[:, 0, :], v_sgu[:, tt, p * 512:(p + 1) * 512], ACT.Square,
                                              accum_out=stat[:, tt, 16 + p:17 + p]))
                act.sem_inc(v_sq, 1)
            for tt in range(TT):
                act.wait_ge(v_var, tt + 1)
                act.activation(stat[:, tt, 28:29], stat[:, tt, 27:28], ACT.Sqrt).then_inc(v_std, 1)
            stage_copy("sgu_u", gu, ACT.Gelu)
            with act.Fori(0, NBLOCKS["sgu_z"] // RING) as i:
                for s in range(RING):
                    act.wait_ge(block_done, i * RING + (BASE["sgu_z"] + s + 1))
                    if s < 2:
                        act.wait_ge(vm_taken, GROUPS)
                    act.wait_ge(bank_free[(s + 2) % 4], i + (BANK["sgu_z"][(s + 2) % 4] + (s >= 2)))
                    act.activation(stmp[:, s % 2, :], pm[s][:, :], ACT.Silu).then_inc(z_silu, 1)

            def copy_groups(name, per):
                with act.Fori(0, 4) as i:
                    for g in range(2):
                        act.wait_ge(block_done, i * (2 * per) + (BASE[name] + (g + 1) * per))
                        act.activation(at(h, i * 4 + 2 * g, 2), pm[g][:, :], ACT.Copy).then_inc(bank_free[g], 1)

            copy_groups("sgu_out", 2)
            wait_banks(act, "lat")
            squares("post0", ysq, h)
            root("post0")
            act.wait_ge(x_ready, 2)
            squares("pre1", h, x)
            root("pre1")
            modulate(3, S1)

            stage_copy("lat", lat)
            wait_banks(act, "mla_z")
            for part in range(2):
                act.activation(lsq[:, 4 * part:4 * part + 4, :], lat[:, 4 * part:4 * part + 4, :], ACT.Square).then_inc(sq_ready, 1)
            stage_copy("mla_z", zo, ACT.Silu)
            root("kv")
            root("q")
            with act.Fori(0, MH // 4) as i:
                for st, j in waves(4, 5):
                    hn = i * 4 + j
                    if st == 0:
                        act.wait_ge(block_done, hn + (BASE["heads"] + 1))
                        act.activation(qn[j], pm[j][:, 0:T], ACT.Copy)
                        act.activation(qr[j], pm[j][0:ROPE, T:2 * T], ACT.Copy)
                        act.activation(kv[j], px[j][:, :], ACT.Copy).then_inc(m_proj, 1)
                    elif st == 2:
                        act.wait_ge(m_negmax, hn + 1)
                        for lo, tt in ((0, 0), (P, 1)):
                            keys = P * (tt + 1)
                            ex = act.activation(pr[j][:, lo:lo + keys], pr[j][:, lo:lo + keys], ACT.Exp,
                                                bias=small_m[:, j, 1, tt:tt + 1], accum_out=small_m[:, j, 2, tt:tt + 1])
                        ex.then_inc(m_exp, 1)
                    elif st == 3:
                        act.wait_ge(m_pt, hn + 1)
                        act.activation(pt[j], px[j][:, 0:3 * P], ACT.Copy).then_inc(m_ptsb, 1)
            stage_copy("mla_out", h)
            wait_banks(act, "end")
            squares("post1", ysq, h)
            root("post1")

        @block.vector
        def _(dve):
            chain = Chain(dve, dve_step)
            tt_ = dve.tensor_tensor
            ts_ = dve.tensor_scalar
            stt = dve.scalar_tensor_tensor

            def unit(v, u, cond):
                for q in range(QUARTS):
                    piece = u * QUARTS + (v * VQ + q)
                    s = q % 2
                    dve.wait_ge(ada_full[s], (u * (QUARTS // 2) + (v * VQ // 2 + q // 2 + 1)) * 16)
                    dst = acc[:, v % 2, bass.ds(u * UCOLS, UCOLS)] if not isinstance(u, int) else \
                        acc[:, v % 2, u * UCOLS:(u + 1) * UCOLS]
                    for r in range(QKC):
                        w = ada[:, s, r * UCOLS:(r + 1) * UCOLS]
                        c = csil[:, cond, q * QKC + r:q * QKC + r + 1]
                        if q == 0 and r == 0:
                            if v >= 2:
                                dve.wait_ge(vec_summed, v - 1)
                            ins = ts_(dst, w, c, None, ALU.mult)
                        else:
                            ins = stt(dst, w, c, dst, ALU.mult, ALU.add)
                        if r < QKC - 1:
                            chain.link(ins)
                        else:
                            ins.then_inc(ada_used, 1)
                            dve.wait_ge(ada_used, piece + 1)

            LINKS = 12

            def take_vector(v):
                dve.wait_ge(vec_summed, v + 1)
                tt_(mods[:, v, :], px[3][:, 0:KC], pcols("bias", KC, v * KC), ALU.add).then_inc(vec_taken, 1)
                dve.wait_ge(vec_taken, v + 1)

            def rsqrt_mean(name, width):
                k = NORM_INDEX[name]
                dve.wait_ge(ss_ready, k + 1)
                ts_(rstd[:, :], px[0][:, 0:T], 1.0 / width, EPS, ALU.mult, ALU.add).then_inc(ms_ready, 1)
                dve.wait_ge(std_ready, k + 1)
                chain.link(dve.reciprocal(rstd[:, :], rstd[:, :]))

            def modulation(k, g, gc, scale):
                chain.link(stt(gain[:, k, :], mods[:, scale, :], 1.0, pcols(g, KC, gc), ALU.add, ALU.mult))

            def normed():
                for kc in range(KC):
                    tt_(h[:, kc, :], x[:, kc, :], rstd[:, :], ALU.mult).then_inc(xn_ready, 1)

            def residual(bank, chunk, gate, last):
                for j in range(2):
                    c = chunk + j
                    g = mods[:, gate, c:c + 1] if isinstance(c, int) else mods[:, gate, bass.ds(c, 1)]
                    xc = one(x, c)
                    ins = stt(xc, pm[bank][:, j * T:(j + 1) * T], g, xc, ALU.mult, ALU.add)
                ins.then_inc(bank_free[bank], 1)

            dve.memset(ones[:, :], 1.0).then_inc(ones_set, 1)
            dve.memset(gates[0:GROW, :, :], 0.0)
            dve.wait_ge(silu_c, 1)
            for v in (SH1, SC1):
                with dve.Fori(0, UNITS) as u:
                    chain.enter(u, LINKS)
                    unit(v, u, 0)
                    chain.leave(UNITS)
            rsqrt_mean("norm1", D)
            take_vector(SH1)
            take_vector(SC1)
            modulation(0, "g1", 0, SC1)
            normed()

            G = slice(0, GROW)
            dve.wait_ge(gate_ps, 1)
            chain.link(ts_(gates[G, 0, :], px[0][G, 0:T], pcol("bi", 0, G), None, ALU.add))
            chain.link(ts_(gates[G, 1, :], px[0][G, T:2 * T], pcol("bf", 0, G), None, ALU.add))
            stt(gates[G, 2, :], gates[G, 1, :], -1.0, gates[G, 1, :], ALU.mult, ALU.min).then_inc(gate_rows, 1)
            dve.wait_ge(gate_exp, 1)
            chain.link(stt(gates[G, 1, :], gates[G, 1, :], 0.0, gates[G, 3, :], ALU.min, ALU.subtract))
            for rows, step in ((slice(0, NH_A), 1), (slice(32, GROW), -1)):
                chain.link(dve.tensor_tensor_scan(gates[rows, 4, ::step], ones[rows, 0:1].to_broadcast([NH_A, T]),
                                                  gates[rows, 1, ::step], 0.0, ALU.mult, ALU.add))
            chain.link(tt_(gates[G, 5, :], gates[G, 0, :], gates[G, 4, :], ALU.subtract))
            for rows, step in ((slice(0, NH_A), 1), (slice(32, GROW), -1)):
                chain.link(dve.tensor_tensor_scan(gates[rows, 6, ::step], gates[rows, 5, ::step], gates[rows, 5, ::step],
                                                  -3.0e38, ALU.max, ALU.max))
            chain.link(ts_(neg_rows[G, 0:T], gates[G, 6, :], -1.0, None, ALU.mult))
            stt(neg_rows[G, T:2 * T], gates[G, 4, :], -1.0, gates[G, 6, :], ALU.mult, ALU.subtract).then_inc(rows_ready, 1)
            dve.wait_ge(bias_in, 16)
            dve.wait_ge(mix_const_in, 48)
            b3 = bias_b.rearrange("p (a c) -> p a c", c=GRID_W)
            chain.link(tt_(b3, b3, over(wmask, NH_B * 6), ALU.add))
            dve.wait_ge(bcol_ps, 1)
            dve.tensor_copy(flat(bcol), px[1][:, 0:2 * GROW]).then_inc(bcol_ready, 1)

            def a_head_scores(hd_):
                dve.wait_ge(a_scores, hd_ + 1)
                if hd_:
                    dve.wait_ge(a_num, hd_)
                for d in range(2):
                    tt_(split(decay[:, d, :], 2, T), over(px[1 + d][:, 0:T], 2), split(mask_a[:, d, :], 2, T),
                        ALU.add).then_inc(a_arg, 1)
                for d in range(2):
                    dve.wait_ge(a_exp, 2 * hd_ + d + 1)
                    stt(decay[:, d, :], px[0][:, :], SCALE_A, decay[:, d, :], ALU.mult, ALU.mult).then_inc(a_probs, 1)

            def a_head_mix(hd_):
                dve.wait_ge(a_num, hd_ + 1)
                chain.link(stt(flat(expm), px[3][:, :], -1.0, flat(expm), ALU.mult, ALU.max))
                chain.link(tt_(flat(expm), px[3][:, :], flat(expm), ALU.max))
                chain.link(dve.reciprocal(flat(expm), flat(expm)))
                tt_(hf, split(px[1][:, :], 2, T), over(expm[:, 0, :], 2), ALU.mult)
                chain.link(tt_(hb, split(px[2][:, :], 2, T), over(expm[:, 1, :], 2), ALU.mult))
                tt_(hf, hf, hb, ALU.add).then_inc(a_h, 1)

            def a_head_norm(hd_):
                dve.wait_ge(a_ss, hd_ + 1)
                ts_(expm[:, 0, :], px[3][:, 0:T], 1.0 / DH_A, EPS, ALU.mult, ALU.add).then_inc(a_ms, 1)
                dve.wait_ge(a_std, hd_ + 1)
                chain.link(dve.reciprocal(expm[:, 0, :], expm[:, 0, :]))
                dve.wait_ge(bank_free[hd_], 4)
                for ec in range(2):
                    c = 2 * hd_ + ec
                    chain.link(stt(hf[:, ec, :], hf[:, ec, :], pcol("ghead", c), expm[:, 0, :], ALU.mult, ALU.mult))
                tt_(oa[:, 2 * hd_:2 * hd_ + 2, :], oa[:, 2 * hd_:2 * hd_ + 2, :], hf, ALU.mult).then_inc(a_out, 1)

            for n in range(NBLOCKS["w_in"]):
                group = n // 4
                for step, k in W_IN_STEPS.get(n, []):
                    if step == "sum":
                        take_vector(k)
                    else:
                        {"scores": a_head_scores, "mix": a_head_mix, "norm": a_head_norm}[step](k)
                if n % 2 and group < 6:
                    unit(GA1 + group // 2, (n % 8) // 2, 0)

            for st, hd_ in waves(NH_B, 3):
                if st:
                    continue
                j = hd_ % 2
                dve.wait_ge(b_scores, hd_ + 1)
                if hd_ >= 2:
                    dve.wait_ge(b_pt, hd_ - 1)
                for tt in range(TT):
                    lo = hd_ * 6 * GRID_W + (2 - 2 * tt) * GRID_W
                    ins = stt(s_b[j][:, tt, :], px[hd_ % 4][:, tt * T:(tt + 1) * T], SCALE_B, bias_b[:, lo:lo + T],
                              ALU.mult, ALU.add)
                chain.link(ins)
                chain.link(dve.tensor_reduce(small_b[:, j, 0, :], s_b[j], AX.X, ALU.max))
                ts_(small_b[:, j, 1, :], small_b[:, j, 0, :], -1.0, None, ALU.mult).then_inc(b_negmax, 1)
                dve.wait_ge(b_exp, hd_ + 1)
                chain.link(dve.reciprocal(small_b[:, j, 3, :], small_b[:, j, 2, :]))
                for tt in range(TT):
                    ins = ts_(s_b[j][:, tt, :], s_b[j][:, tt, :], small_b[:, j, 3, tt:tt + 1], None, ALU.mult)
                ins.then_inc(b_probs, 1)

            with dve.Fori(0, 2) as i:
                chain.enter(i, 2 * LINKS)
                for s in range(RING):
                    dve.wait_ge(block_done, i * RING + (BASE["w_out"] + s + 1))
                    residual(s, i * 8 + 2 * s, GA1, False)
                    if s % 2:
                        unit(GA2, i * 2 + s // 2, 0)
                chain.leave(2)
            take_vector(GA2)
            rsqrt_mean("norm2", D)
            modulation(1, "g2", 0, SC2)
            normed()

            dve.memset(gpad[:, :, 0:1], 0.0)
            chain.link(dve.memset(gpad[:, :, T + 1:T + 2], 0.0))

            def up(lo, hi, v):
                with dve.Fori(lo, hi) as i:
                    chain.enter(i - lo, 2 * RING + (LINKS if v is not None else 0))
                    for s in range(RING):
                        k = i * RING + s
                        j = s % 2
                        dve.wait_ge(g_copied, k + 1)
                        chain.link(ts_(conv[:, j, :], gpad[:, j, 0:T], pcol("conv", k * 4), pcol("conv", k * 4 + 3), ALU.mult, ALU.add))
                        chain.link(stt(conv[:, j, :], gpad[:, j, 1:T + 1], pcol("conv", k * 4 + 1), conv[:, j, :], ALU.mult, ALU.add))
                        stt(conv[:, j, :], gpad[:, j, 2:T + 2], pcol("conv", k * 4 + 2), conv[:, j, :], ALU.mult,
                            ALU.add).then_inc(conv_ready, 1)
                        dve.wait_ge(gelu_ready, k + 1)
                        tt_(one(glu, k), conv[:, j, :], pm[s][:, T:2 * T], ALU.mult).then_inc(bank_free[s], 1)
                    if v is not None:
                        unit(v, i - lo, 1)
                    chain.leave(hi - lo)

            up(0, 4, S0)
            up(4, 8, C0)
            take_vector(S0)
            up(8, 11, None)
            take_vector(C0)
            with dve.Fori(0, 4) as i:
                for g in range(2):
                    dve.wait_ge(block_done, i * (2 * RING) + (BASE["w_down"] + (g + 1) * RING))
                    residual(g, i * 4 + 2 * g, GA2, False)
            rsqrt_mean("final", D)
            for kc in range(KC):
                ins = stt(x[:, kc, :], x[:, kc, :], pcol("gfinal", kc), rstd[:, :], ALU.mult, ALU.mult)
            ins.then_inc(x_ready, 1)
            dve.wait_ge(x_ready, 1)
            rsqrt_mean("pre0", D)
            modulation(2, "pre", 0, C0)
            normed()

            with dve.Fori(0, 4) as i:
                chain.enter(i, LINKS)
                unit(G0, i, 1)
                chain.leave(4)
            wait_banks(dve, "sgu_u")
            for tt in range(TT):
                chain.link(dve.tensor_reduce(stat[:, tt, 24:25], stat[:, tt, 0:16], AX.X, ALU.add))
                chain.link(ts_(stat[:, tt, 25:26], stat[:, tt, 24:25], -1.0 / SGU_W, None, ALU.mult))
                ts_(v_sgu[:, tt, :], v_sgu[:, tt, :], stat[:, tt, 25:26], None, ALU.add).then_inc(v_mean, 1)
            for tt in range(TT):
                dve.wait_ge(v_sq, tt + 1)
                chain.link(dve.tensor_reduce(stat[:, tt, 26:27], stat[:, tt, 16:24], AX.X, ALU.add))
                ts_(stat[:, tt, 27:28], stat[:, tt, 26:27], 1.0 / SGU_W, EPS, ALU.mult, ALU.add).then_inc(v_var, 1)
            for tt in range(TT):
                dve.wait_ge(v_std, tt + 1)
                chain.link(dve.reciprocal(stat[:, tt, 29:30], stat[:, tt, 28:29]))
                ts_(v_sgu[:, tt, :], v_sgu[:, tt, :], stat[:, tt, 29:30], None, ALU.mult).then_inc(v_normed, 1)
            with dve.Fori(0, 4) as i:
                chain.enter(i, LINKS)
                unit(S1, i, 1)
                chain.leave(4)
            take_vector(G0)
            wait_banks(dve, "mix")
            for g in range(GROUPS):
                s, r = divmod(g, 4)
                dve.wait_ge(vm_ready, g + 1)
                row = ring[:, s, (r * 2 + 1) * P:(r * 2 + 2) * P]
                for c in range(2):
                    ins = stt(split(stmp[:, g % 2, c * T:(c + 1) * T], 2, P), split(px[g % 4][:, c * T:(c + 1) * T], 2, P),
                              pcol("gsgu", 2 * g + c), over(row, 2), ALU.mult, ALU.add)
                chain.link(ins)
                gg = gu[:, 2 * g:2 * g + 2, :]
                tt_(gg, gg, split(stmp[:, g % 2, :], 2, T), ALU.mult).then_inc(vm_taken, 1)
            with dve.Fori(0, 4) as i:
                chain.enter(i, LINKS)
                for s in range(RING):
                    dve.wait_ge(z_silu, i * RING + s + 1)
                    gg = at(gu, i * 8 + 2 * s, 2)
                    tt_(gg, gg, split(stmp[:, s % 2, :], 2, T), ALU.mult).then_inc(bank_free[s], 1)
                unit(C1, i, 1)
                chain.leave(4)
            take_vector(S1)
            take_vector(C1)

            def post(name, layer, gate, done):
                chain.link(tt_(gain[:, 4, :], pcols("post", KC, layer * KC), mods[:, gate, :], ALU.mult))
                rsqrt_mean(name, D)
                for kc in range(KC):
                    ins = stt(h[:, kc, :], h[:, kc, :], gain[:, 4, kc:kc + 1], rstd[:, :], ALU.mult, ALU.mult)
                chain.link(ins)
                tt_(flat(x[:, :, :]), flat(x[:, :, :]), flat(h[:, :, :]), ALU.add).then_inc(x_ready, 1)
                dve.wait_ge(x_ready, done)

            post("post0", 0, G0, 2)
            rsqrt_mean("pre1", D)
            modulation(3, "pre", KC, C1)
            normed()

            rsqrt_mean("kv", KVR)
            for c in range(4):
                ins = stt(lat[:, c, :], lat[:, c, :], pcol("gkv", c), rstd[:, :], ALU.mult, ALU.mult)
            ins.then_inc(lat_ready, 1)
            dve.wait_ge(lat_ready, 1)
            rsqrt_mean("q", QR)
            for c in range(4):
                rows = slice(0, P) if c < 3 else slice(64, P)
                ins = stt(lat[rows, 4 + c, :], lat[rows, 4 + c, :], pcol("gq", c, rows), rstd[rows, :], ALU.mult, ALU.mult)
            ins.then_inc(lat_ready, 1)
            dve.wait_ge(mla_const_in, 16)
            dve.wait_ge(kr_rot, 1)
            tt_(rt[0], px[1][0:64, 0:T], sin, ALU.mult)
            chain.link(tt_(kro, lat[0:64, 7, :], cos, ALU.mult))
            tt_(kro, kro, rt[0], ALU.add).then_inc(lat_ready, 1)
            with dve.Fori(0, MH // 4) as i:
                chain.enter(i, 4 * 4 + LINKS)
                for st, j in waves(4, 5):
                    hn = i * 4 + j
                    if st == 1:
                        dve.wait_ge(m_rot, hn + 1)
                        tt_(rt[j], px[j][0:64, 0:T], sin, ALU.mult)
                        chain.link(tt_(qr[j], qr[j], cos, ALU.mult))
                        tt_(qr[j], qr[j], rt[j], ALU.add).then_inc(m_rope, 1)
                    elif st == 2:
                        dve.wait_ge(m_scores, hn + 1)
                        chain.link(stt(pr[j], pm[j][:, 0:3 * P], SCALE_M, mask_m, ALU.mult, ALU.add))
                        dve.tensor_reduce(small_m[:, j, 0, 0:1], pr[j][:, 0:P], AX.X, ALU.max)
                        chain.link(dve.tensor_reduce(small_m[:, j, 0, 1:2], pr[j][:, P:3 * P], AX.X, ALU.max))
                        ts_(small_m[:, j, 1, :], small_m[:, j, 0, :], -1.0, None, ALU.mult).then_inc(m_negmax, 1)
                        dve.wait_ge(m_exp, hn + 1)
                        chain.link(dve.reciprocal(small_m[:, j, 3, :], small_m[:, j, 2, :]))
                        for lo, tt in ((0, 0), (P, 1)):
                            keys = P * (tt + 1)
                            ins = ts_(pr[j][:, lo:lo + keys], pr[j][:, lo:lo + keys], small_m[:, j, 3, tt:tt + 1], None, ALU.mult)
                        ins.then_inc(m_probs, 1)
                    elif st == 4:
                        dve.wait_ge(m_num, hn + 1)
                        zc = one(zo, hn)
                        tt_(zc, zc, pm[j][:, 0:T], ALU.mult).then_inc(bank_free[j], 1)
                unit(G1, i, 1)
                chain.leave(MH // 4)
            take_vector(G1)
            post("post1", 1, G1, 3)


def constants():
    f = np.float32
    t = np.arange(T)
    mask_a = np.zeros((P, 2, TT, T), f)
    for sc in range(TT):
        s = (np.arange(P) + sc * P)[:, None]
        mask_a[:, 0, sc] = np.where(t[None] >= s, 0.0, NEG)
        mask_a[:, 1, sc] = np.where(t[None] <= s, 0.0, NEG)
    c = np.arange(GRID_W)
    lo = np.clip(c - WIN_COLS // 2, 0, GRID_W - WIN_COLS)[:, None]
    win = np.where((c[None] >= lo) & (c[None] < lo + WIN_COLS), 0.0, NEG).astype(f)
    cst = np.zeros((P, 1024), f)
    inv = (f(10000.0) ** (-np.arange(0, ROPE, 2, dtype=f) / f(ROPE))).astype(f)
    ang = (t.astype(f)[:, None] * inv[None, :]).astype(f)
    cst[0:64, 0:256] = np.concatenate([np.cos(ang), np.cos(ang)], axis=1).T
    cst[0:64, 256:512] = np.concatenate([np.sin(ang), np.sin(ang)], axis=1).T
    q = np.arange(P)[:, None]
    cst[:, 512:640] = np.where(t[None, :P] // 64 <= q // 64, 0.0, NEG)
    cst[:, 640:896] = np.where(t[None] // 64 <= (q + P) // 64, 0.0, NEG)
    half = ROPE // 2
    for m in range(half):
        cst[m + half, 896 + m] = -1.0
        cst[m, 896 + m + half] = 1.0
    return {"ident": np.eye(P, dtype=f), "mask_a": mask_a.reshape(P, -1), "wmask": np.concatenate([win, win]), "mla_cst": cst}


def blocks(w, k=KC):
    kk, n = w.shape
    w = w.reshape(kk // (P * k), k, P, n // COLS, COLS).transpose(3, 0, 2, 1, 4)
    return np.ascontiguousarray(w).reshape(-1, P, k * COLS)


def columns_of(v):
    return np.asarray(v).reshape(-1, P).T


def lay_out(i):
    i = {n: np.asarray(v) for n, v in i.items()}
    f = np.float32
    d = constants()
    d["x"] = np.ascontiguousarray(i["x"][0].T.reshape(KC, P, T).transpose(1, 0, 2)).reshape(P, -1)
    par = np.zeros((P, NPAR), f)

    def put(name, cols, c=0):
        par[:cols.shape[0], PCOL[name] + c:PCOL[name] + c + cols.shape[1]] = cols

    put("c", columns_of(i["c"][0]))
    put("c2", columns_of(i["c_2"][0]))
    put("bias", columns_of(i["b_ada"][0]))
    put("bias", columns_of(i["ada_b_2"].reshape(-1)), 6 * KC)
    put("g1", columns_of(i["g_norm1"][0]))
    put("ghead", columns_of(i["g_head_a"][0]))
    put("g2", columns_of(i["g_norm2"][0]))
    conv = np.concatenate([i["conv_w"][0], i["conv_b"]], axis=0).reshape(4, FC, P).transpose(2, 1, 0)
    put("conv", conv.reshape(P, -1))
    put("gfinal", columns_of(i["g_final"]))
    put("pre", columns_of(i["pre_g_2"].reshape(-1)))
    put("post", columns_of(i["post_g_2"].reshape(-1)))
    put("gsgu", columns_of(i["sgu_norm_g_2"][0]))
    gq = i["mla_q_norm_g_2"][0]
    put("gq", columns_of(np.concatenate([gq[:384], np.zeros(64, f), gq[384:]])))
    put("gkv", columns_of(i["mla_kv_norm_g_2"][0]))

    def gate_rows(v, first):
        out = np.zeros(v.shape[:-1] + (GROW,), f)
        out[..., 0:NH_A] = v[..., first * NH_A:(first + 1) * NH_A]
        out[..., 32:GROW] = v[..., (first + 2) * NH_A:(first + 3) * NH_A]
        return out

    put("bi", gate_rows(i["b_gates"][0], 0)[:, None])
    put("bf", gate_rows(i["b_gates"][0], 1)[:, None])
    d["par"] = par

    w = i["w_in"][0]
    q_a, k_a, v_a, o_a = (w[:, n * 1024:(n + 1) * 1024] for n in range(4))
    gw = w[:, 4096:4112]
    q_b, k_b, v_b = (w[:, 4112 + n * 1024:4112 + (n + 1) * 1024] for n in range(3))
    d["gate_w"] = np.stack([gate_rows(gw, g).reshape(KC, P, GROW).transpose(1, 0, 2) for g in range(2)], axis=1).reshape(P, -1)
    d["w_in"] = blocks(np.concatenate([k_a, q_a, v_a, o_a, q_b, k_b, v_b], axis=1))
    d["w_out"] = blocks(i["w_out"][0])
    up = i["w_up"][0]
    u, g = up[:, :D_FF].reshape(D, FC, 1, P), up[:, D_FF:].reshape(D, FC, 1, P)
    d["w_up"] = blocks(np.concatenate([g, u], axis=2).reshape(D, -1))
    d["w_down"] = blocks(i["w_down"][0], W_DOWN_KC)

    rpb = i["rpb"][0]
    c = np.arange(GRID_W)
    dc = np.clip(c[None] - c[:, None] + WIN_COLS - 1, 0, 2 * WIN_COLS - 2)
    rows = []
    for half in range(2):
        dr = np.arange(6) + 5 - half
        rows.append(rpb[:, dr][:, :, dc].transpose(2, 0, 1, 3).reshape(GRID_W, -1))
    d["bias_b"] = np.concatenate(rows)

    ada = np.concatenate([i["w_ada"][0], i["ada_w_2"][0], i["ada_w_2"][1]], axis=1)
    ada = ada.reshape(QUARTS, QKC, P, 12 * UNITS, UCOLS).transpose(3, 0, 2, 1, 4)
    d["ada"] = np.ascontiguousarray(ada).reshape(-1, P, QKC * UCOLS)

    w = i["sgu_w_in_2"][0]
    d["sgu_u"], d["sgu_v"], d["sgu_z"] = (blocks(w[:, n * SGU_W:(n + 1) * SGU_W]) for n in range(3))
    ws = i["sgu_w_s_2"][0].transpose(0, 2, 1)
    bs = np.broadcast_to(i["sgu_b_s_2"][0][:, None, :], (GROUPS, P, P))
    d["mix"] = np.ascontiguousarray(np.stack([ws, bs], axis=2).reshape(4, 4, P, 2, P).transpose(0, 2, 1, 3, 4)).reshape(4, P, -1)
    d["sgu_out"] = blocks(i["sgu_w_out_2"][0])

    w = i["mla_w_in_2"][0]
    cq, ckv, kr, z = w[:, :QR], w[:, QR:QR + KVR], w[:, QR + KVR:QR + KVR + ROPE], w[:, QR + KVR + ROPE:]
    d["lat"] = blocks(np.concatenate([ckv, cq[:, :384], kr, cq[:, 384:]], axis=1))
    d["mla_z"] = blocks(z)
    uq = i["mla_w_uq_2"][0]
    uq = np.concatenate([uq[:384], np.zeros((64, uq.shape[1]), f), uq[384:]])
    head = np.concatenate([uq.reshape(512, MH, 192), i["mla_w_ukv_2"][0].reshape(512, MH, 256)], axis=2)
    d["heads"] = np.ascontiguousarray(head.reshape(4, P, MH, 448).transpose(2, 1, 0, 3)).reshape(MH, P, -1)
    d["mla_out"] = blocks(i["mla_w_out_2"][0])
    return {n: np.ascontiguousarray(v, dtype=f) for n, v in d.items()}


def kernel(**inputs):
    import concourse.bacc as bacc
    from concourse.bass_utils import run_bass_kernel_spmd as run

    nc = bacc.Bacc("TRN2", target_bir_lowering=False, num_devices=1)
    arrays = {f"in_{n}": v for n, v in lay_out(inputs).items()}
    args = {n[3:]: nc.dram_tensor(n, v.shape, F32, kind="ExternalInput").ap() for n, v in arrays.items()}
    args["out"] = nc.dram_tensor("out_x", (P, KC * T), F32, kind="ExternalOutput").ap()
    build(nc, args)
    got = run(nc, [arrays], core_ids=[0]).results[0]["out_x"]
    return np.ascontiguousarray(got.reshape(P, KC, T).transpose(2, 1, 0)).reshape(1, T, D)
```

```python
from contextlib import ExitStack

import concourse.bass as bass
import numpy as np
from concourse import mybir

F32 = mybir.dt.float32
F32R = mybir.dt.float32r
ALU = mybir.AluOpType
ACT = mybir.ActivationFunctionType
AX = mybir.AxisListType

P = 128
D = 2048
KC = D // P
T = 256
TT = T // P
COLS = 256
PKC = 8
PIECE = PKC * COLS
QUARTER = PIECE // 2
SLOTS = 4
AHEAD = 3
BODY = 4
EPS = 1e-6
NEG = -1e30

NH_A, DH_A = 4, 256
NH_B, DH_B = 8, 128
GRID_W, WIN_COLS = 64, 16
D_FF = 5632
FC = D_FF // P
FH = FC // 2
SGU_W = 4096
SC = SGU_W // P
GROUPS = 16
MH, NOPE, ROPE, VD = 16, 128, 64, 128
QR, KVR = 448, 512
HEADW = NOPE + ROPE + NOPE + VD
SCALE_A = DH_A ** -0.5
SCALE_B = DH_B ** -0.5
SCALE_M = (NOPE + ROPE) ** -0.5
GROW = 36
GPAD = KC * GROW + P - GROW

STAGES = [("w_in", 28, [4] * 4), ("w_out", 8, [4] * 4), ("w_up0", FH, [4] * 4), ("w_down0", 8, [4] * 5 + [2]),
          ("w_up1", FH, [4] * 4), ("w_down1", 8, [4] * 5 + [2]), ("sgu_v", 16, [4] * 4), ("sgu_u", 16, [4] * 4),
          ("sgu_z", 16, [4] * 4), ("sgu_out", 8, [4] * 8), ("lat", 4, [4] * 4), ("mla_z", 8, [4] * 4),
          ("heads", MH, [2] * 2), ("mla_out", 8, [4] * 4)]
NBLOCKS = {n: b for n, b, _ in STAGES}
QUARTERS = {n: q for n, _, q in STAGES}
QBASE, BBASE, _q, _b = {}, {}, 0, 0
for _name, _blocks, _qs in STAGES:
    QBASE[_name], BBASE[_name] = _q, _b
    _q += _blocks * len(_qs)
    _b += _blocks if _name != "heads" else 0
    assert _q % (2 * SLOTS) == 0 and _b % 2 == 0
LAST = STAGES[-1][0]

SH1, SC1, GA1, SH2, SC2, GA2, S0, C0, G0, S1, C1, G1 = range(12)
UNITS = 4
UCOLS = D // UNITS
APIECES = 8
APIECE = D // P // APIECES * UCOLS
FIRST_UNITS = 2 * UNITS
FROM_C2 = 6 * UNITS
W_IN_UNITS = 3 * UNITS
BODY_PIECES = [3, 3, 2, 0]

PCOL, _n = {}, 0
for _name, _cols in [("c", KC), ("c2", KC), ("bias", 12 * KC), ("g1", KC), ("ghead", 8), ("g2", KC),
                     ("conv", FC * 4), ("gfinal", KC), ("pre", 2 * KC), ("post", 2 * KC), ("gsgu", SC),
                     ("gq", 4), ("gkv", 4), ("bi", 1), ("bf", 1)]:
    PCOL[_name] = _n
    _n += _cols
NPAR = _n

PAIRS = KC // 2
NORMS = ["norm1", "norm2", "final", "post0", "pre1", "post1"]
ADDED = {n: PAIRS * (i + 1) for i, n in enumerate(NORMS)}
SUMS = {n: i + 1 for i, n in enumerate(["norm1", "norm2", "final", "finalg", "post0", "pre1", "kv", "q", "post1"])}
H_NORMS = ["norm1", "norm2", "pre0", "pre1"]

W_IN_STEPS = {11: [("scores", 0)], 13: [("mix", 0)], 14: [("norm", 0), ("scores", 1)], 15: [("mix", 1)],
              16: [("norm", 1), ("scores", 2)], 17: [("mix", 2)], 18: [("norm", 2), ("scores", 3)], 19: [("mix", 3)],
              20: [("norm", 3)]}


def waves(jobs, stages):
    return [(w - j, j) for w in range(jobs + stages - 1) for j in range(jobs) if 0 <= w - j < stages]


class Chain:

    def __init__(self, eng, sem):
        self.eng, self.sem, self.count, self.i, self.per = eng, sem, 0, None, 0

    def link(self, ins):
        ins.then_inc(self.sem, 1)
        self.count += 1
        self.eng.wait_ge(self.sem, self.count if self.i is None else self.i * self.per + self.count)

    def enter(self, i, per):
        self.i, self.per, self.start = i, per, self.count

    def leave(self, trips):
        assert self.count - self.start == self.per, (self.count - self.start, self.per)
        self.count = self.start + trips * self.per
        self.i = None


def build(nc, a):
    with ExitStack() as ctx:
        base = (nc.sbuf_base + 63) // 64 * 64
        cursor = [0]

        def at_(name, shape, offset, dt=F32):
            assert base + 4 * (offset + int(np.prod(shape[1:]))) <= nc.sbuf_usable_end, name
            return nc.alloc_sbuf_tensor_at(name, shape, dt, offset=base + 4 * offset)

        def sb(name, shape, dt=F32):
            o = cursor[0]
            cursor[0] += (int(np.prod(shape[1:])) + 7) // 8 * 8
            return at_(name, shape, o, dt)

        def sem(name):
            return ctx.enter_context(nc.semaphore(name))

        x = sb("x", [P, KC, T])
        o_h = cursor[0]
        h_hi = sb("h_hi", [P, KC, T], F32R)
        h_lo = sb("h_lo", [P, KC, T], F32R)
        raw = sb("raw", [P, SLOTS, PIECE])
        w_hi = sb("w_hi", [P, SLOTS, QUARTER], F32R)
        w_lo = sb("w_lo", [P, SLOTS, QUARTER], F32R)
        ada = sb("ada", [P, SLOTS, APIECE])
        acc = sb("acc", [P, UCOLS])
        par = sb("par", [P, NPAR])
        mods = sb("mods", [P, 12 * KC])
        csil = sb("csil", [P, 2, KC])
        gain = sb("gain", [P, 5, KC])
        ident = sb("ident", [P, P])
        ones = sb("ones", [P, P])
        rstd = sb("rstd", [P, T])
        o_ssq = cursor[0]
        ssq = sb("ssq", [P, 2, T])
        sqt = sb("sqt", [P, 2, T])
        o_nt = cursor[0]
        nt = sb("nt", [P, 4, T])
        stat = sb("stat", [P, 2, 32])
        small_b = sb("small_b", [P, 2, 4, 2])
        small_m = sb("small_m", [P, 4, 4, 2])
        o_work = cursor[0]

        def work(name, shape, offset, dt=F32):
            return at_(name, shape, o_work + offset, dt)

        e1 = work("e1", [P, SLOTS, APIECE], 0)
        ka = work("ka", [P, 8, T], 0)
        qa = work("qa", [P, 8, T], 2048)
        va = work("va", [P, TT, 1024], 4096)
        oa = work("oa", [P, 8, T], 6144)
        gw_lo = work("gw_lo", [P, 2, GPAD], 4096, F32R)
        gw_hi = work("gw_hi", [P, 2, GPAD], 6144, F32R)
        gates = work("gates", [P, 8, T], 8192)
        qb = work("qb", [P, 8, T], 8192)
        kb = work("kb", [P, 8, T], 0)
        vb = work("vb", [P, TT, 1024], 2048)
        mask_a = work("mask_a", [P, 2, 512], 10240)
        gw = work("gw", [P, 2, GPAD], 11264)
        bias_b = work("bias_b", [P, NH_B * 6, GRID_W], 10240)
        neg_rows = work("neg_rows", [P, 2 * T], 13312)
        bcol = work("bcol", [P, TT, GROW], 13824)
        wmask = work("wmask", [P, GRID_W], 13904)
        decay = work("decay", [P, 2, 2 * T], 13968)
        expm = work("expm", [P, 2, T], 14992)
        hf = work("hf", [P, 2, T], 15504)
        hb = sqt
        s_b = [decay[:, j, :].rearrange("p (a b) -> p a b", a=TT) for j in range(2)]
        pt_b = [expm, hf]
        glu_hi = work("glu_hi", [P, FH, T], 0, F32R)
        glu_lo = work("glu_lo", [P, FH, T], FH * T, F32R)
        gpad = work("gpad", [P, T + 2], 2 * FH * T)
        conv = work("conv", [P, T], 2 * FH * T + 264)
        ssqg = work("ssqg", [P, 2, T], 12288)
        sqtg = work("sqtg", [P, 2, T], 12800)
        v_sgu = work("v_sgu", [P, TT, SGU_W], 0)
        gu = work("gu", [P, SC, T], 2 * SGU_W)
        y_hi = work("y_hi", [P, SC, T], 0, F32R)
        y_lo = work("y_lo", [P, SC, T], 2 * SGU_W, F32R)
        stmp = at_("stmp", [P, 2, 2 * T], o_ssq)
        mixw = at_("mixw", [P, 2, 2, 2, P], o_nt)
        ztmp = at_("ztmp", [P, 2, 2 * T], o_nt)
        rs1 = at_("rs1", [P, T], o_ssq)
        y0 = at_("y0", [P, KC, T], o_h)
        lat = work("lat", [P, 8, T], 0)
        lat_hi = work("lat_hi", [P, 8, T], 2048, F32R)
        lat_lo = work("lat_lo", [P, 8, T], 4096, F32R)
        lsq = work("lsq", [P, 8, T], 6144)
        zo = work("zo", [P, MH, T], 8192)
        y1 = work("y1", [P, KC, T], 8192)
        cst = work("cst", [P, 1024], 12288)
        cos, sin, mask_m, rot = cst[0:ROPE, 0:256], cst[0:ROPE, 256:512], cst[:, 512:896], cst[0:ROPE, 896:1024]
        kro = work("kro", [P, T], 13312)[0:ROPE, :]
        hd = [work(f"hd{j}", [P, 1408], o) for j, o in enumerate((0, 6144, 13568, 14976))]
        qn = [b[:, 0:256] for b in hd]
        qr = [b[0:ROPE, 256:512] for b in hd]
        kv = [b[:, 512:1024] for b in hd]
        pr = [b[:, 1024:1408] for b in hd]
        pt = [work(f"pt{j}", [P, 384], o) for j, o in enumerate((1408, 7552))] + \
             [at_(f"pt{j}", [P, 384], o_nt + 384 * (j - 2)) for j in (2, 3)]
        rt = [at_(f"rt{j}", [P, T], o_ssq + j * T)[0:ROPE, :] for j in range(4)]

        pm = [ctx.enter_context(nc.psum_tensor(f"pm{b}", [P, 512], F32)) for b in range(2)]
        px = [ctx.enter_context(nc.psum_tensor(f"px{b}", [P, 512], F32)) for b in range(4)]
        pv = ctx.enter_context(nc.psum_tensor("pv", [P, 512], F32))
        ps = ctx.enter_context(nc.psum_tensor("ps", [P, 512], F32))

        const_in = sem("const_in")
        x_in = sem("x_in")
        mix_const_in = sem("mix_const_in")
        wmask_in = sem("wmask_in")
        bias_in = sem("bias_in")
        mla_const_in = sem("mla_const_in")
        hi_ready = sem("hi_ready")
        lo_even = sem("lo_even")
        lo_odd = sem("lo_odd")
        quarter_done = sem("quarter_done")
        ada_used = sem("ada_used")
        unit_summed = sem("unit_summed")
        unit_taken = sem("unit_taken")
        silu_c = sem("silu_c")
        ones_set = sem("ones_set")
        sq_ready = sem("sq_ready")
        sq_added = sem("sq_added")
        ss_ready = sem("ss_ready")
        ms_ready = sem("ms_ready")
        std_ready = sem("std_ready")
        rstd_ready = sem("rstd_ready")
        xn_ready = sem("xn_ready")
        hh_ready = sem("hh_ready")
        h_ready = sem("h_ready")
        x_ready = sem("x_ready")
        dve_step = sem("dve_step")
        act_step = sem("act_step")
        gw_hi_ready = sem("gw_hi_ready")
        gw_lo_ready = sem("gw_lo_ready")
        gate_ps = sem("gate_ps")
        gate_rows = sem("gate_rows")
        gate_exp = sem("gate_exp")
        rows_ready = sem("rows_ready")
        bcol_ps = sem("bcol_ps")
        bcol_ready = sem("bcol_ready")
        a_scores = sem("a_scores")
        a_arg = sem("a_arg")
        a_exp = sem("a_exp")
        a_probs = sem("a_probs")
        a_num = sem("a_num")
        a_h = sem("a_h")
        a_sq = sem("a_sq")
        a_ss = sem("a_ss")
        a_ms = sem("a_ms")
        a_std = sem("a_std")
        a_out = sem("a_out")
        oa_hi = sem("oa_hi")
        mix_ready = sem("mix_ready")
        b_scores = sem("b_scores")
        b_negmax = sem("b_negmax")
        b_exp = sem("b_exp")
        b_probs = sem("b_probs")
        b_pt = sem("b_pt")
        b_ptsb = sem("b_ptsb")
        b_num = sem("b_num")
        b_hi = sem("b_hi")
        g_copied = sem("g_copied")
        conv_ready = sem("conv_ready")
        gelu_ready = sem("gelu_ready")
        glu_ready = sem("glu_ready")
        glu_hi_ready = sem("glu_hi_ready")
        glu_lo_ready = sem("glu_lo_ready")
        sqg_ready = sem("sqg_ready")
        sqg_added = sem("sqg_added")
        v_mean = sem("v_mean")
        v_sq = sem("v_sq")
        v_var = sem("v_var")
        v_std = sem("v_std")
        v_normed = sem("v_normed")
        vm_ready = sem("vm_ready")
        vm_taken = sem("vm_taken")
        z_silu = sem("z_silu")
        y_ready = sem("y_ready")
        y_hi_ready = sem("y_hi_ready")
        y_lo_ready = sem("y_lo_ready")
        lat_sq = sem("lat_sq")
        lat_normed = sem("lat_normed")
        lat_hi_ready = sem("lat_hi_ready")
        lat_lo_ready = sem("lat_lo_ready")
        kr_rot = sem("kr_rot")
        kr_ready = sem("kr_ready")
        m_proj = sem("m_proj")
        m_rot = sem("m_rot")
        m_rope = sem("m_rope")
        m_scores = sem("m_scores")
        m_negmax = sem("m_negmax")
        m_exp = sem("m_exp")
        m_probs = sem("m_probs")
        m_pt = sem("m_pt")
        m_ptsb = sem("m_ptsb")
        m_num = sem("m_num")
        m_gated = sem("m_gated")
        m_hi = sem("m_hi")
        o_ready = sem("o_ready")
        out_done = sem("out_done")
        slot_full = [sem(f"slot_full{s}") for s in range(SLOTS)]
        ada_full = [sem(f"ada_full{s}") for s in range(2 * SLOTS)]
        mixw_full = [sem(f"mixw_full{s}") for s in range(2)]
        bank_free = [sem(f"bank_free{b}") for b in range(2)]
        head_free = [sem(f"head_free{j}") for j in range(4)]

        def flat(ap):
            return ap.rearrange("p a b -> p (a b)")

        def pcol(name, c, rows=slice(0, P)):
            c = c + PCOL[name]
            return par[rows, c:c + 1] if isinstance(c, int) else par[rows, bass.ds(c, 1)]

        def pcols(name, n, c=0):
            return par[:, PCOL[name] + c:PCOL[name] + c + n]

        def mod(v, c):
            c = c + v * KC
            return mods[:, c:c + 1] if isinstance(c, int) else mods[:, bass.ds(c, 1)]

        def at(ap, i, n=1):
            return ap[:, i:i + n, :] if isinstance(i, int) else ap[:, bass.ds(i, n), :]

        def one(ap, i):
            return at(ap, i).rearrange("p a b -> p (a b)")

        def chunk(ap):
            return lambda c: ap[:, c, :]

        def over(ap, n):
            return ap.unsqueeze(1).to_broadcast([ap.shape[0], n, ap.shape[1]])

        def halves(ap, n=2):
            return ap.rearrange("p (a b) -> p a b", a=n)

        def whole(ap):
            return ap.bitcast(F32)

        def quarter(stage, i, k):
            return i * (BODY * len(QUARTERS[stage])) + (QBASE[stage] + k)

        def pairs(stage, i, k):
            return i * (BODY * len(QUARTERS[stage]) // 2) + ((QBASE[stage] + k) // 2 + 1)

        def done(stage, i, b):
            return quarter(stage, i, (b + 1) * len(QUARTERS[stage]))

        def taken(stage, i, b):
            return i * (BODY // 2) + ((BBASE[stage] + b) // 2 + 1)

        def ahead(stage, i, b):
            n = len(QUARTERS[stage])
            ks = range(b * n + AHEAD, (b + 1) * n + AHEAD)
            return [k for k in ks if stage != LAST or i * BODY * n + k < NBLOCKS[stage] * n]

        def elems(stage, k):
            return QUARTER if stage == "heads" else QUARTERS[stage][k % len(QUARTERS[stage])] * COLS

        def raw_part(stage, k):
            lo = k % 2 * QUARTER
            return raw[:, k // 2 % SLOTS, lo:lo + elems(stage, k)]

        def row(ap, n):
            return ap[n] if isinstance(n, int) else ap[bass.ds(n, 1)].rearrange("o p n -> (o p) n")

        def body_pieces(b):
            lo = sum(BODY_PIECES[:b])
            return range(lo, lo + BODY_PIECES[b])

        block = ctx.enter_context(nc.Block())

        @block.sync
        def _(sp):
            sp.dma_start(par[:, :], a["par"]).then_inc(const_in, 16)
            sp.dma_start(ident[:, :], a["ident"]).then_inc(const_in, 16)
            sp.dma_start(flat(x[:, :, :]), a["x"]).then_inc(x_in, 16)
            sp.dma_start(flat(gw[:, :, :]), a["gate_w"]).then_inc(mix_const_in, 16)
            sp.dma_start(flat(mask_a[:, :, :]), a["mask_a"]).then_inc(mix_const_in, 16)
            sp.dma_start(wmask[:, :], a["wmask"]).then_inc(wmask_in, 16)

            def first_unit_piece(u, k):
                buf = ada[:, k, :] if k < SLOTS else e1[:, k - SLOTS, :]
                sp.dma_start(buf, row(a["ada"], u * APIECES + k)).then_inc(ada_full[k], 16)

            for k in range(APIECES):
                first_unit_piece(0, k)
            with sp.Fori(1, FIRST_UNITS) as u:
                for k in range(APIECES):
                    sp.wait_ge(ada_used, u * APIECES + (k + 1 - APIECES))
                    first_unit_piece(u, k)

            def load(stage, i, j):
                if not (isinstance(i, int) and QBASE[stage] + i + j // SLOTS == 0):
                    sp.wait_ge(lo_even, pairs(stage, i, 2 * j) - SLOTS)
                    sp.wait_ge(lo_odd, pairs(stage, i, 2 * j) - SLOTS)
                n = len(QUARTERS[stage]) // 2
                if stage in ("w_down0", "w_down1"):
                    blk, part = i * BODY + j // n, j % n
                    size = elems(stage, 2 * part) + elems(stage, 2 * part + 1)
                    src = row(a[stage][:, :, part * PIECE:part * PIECE + size], blk)
                else:
                    size, src = PIECE, row(a[stage], i * (BODY * n) + j)
                sp.dma_start(raw[:, j % SLOTS, 0:size], src).then_inc(slot_full[j % SLOTS], 16)

            for stage, blocks_, qs in STAGES:
                per = BODY * len(qs) // 2
                first = 0
                if stage == "w_in":
                    for j in range(per):
                        load(stage, 0, j)
                    first = 1
                if blocks_ // BODY > first:
                    with sp.Fori(first, blocks_ // BODY) as i:
                        for j in range(per):
                            load(stage, i, j)
                for j in range(blocks_ % BODY * len(qs) // 2):
                    load(stage, blocks_ // BODY, j)
            for g in range(4):
                sp.wait_ge(x_ready, 4 + g + 1)
                sp.dma_start(a["out"][:, 4 * g * T:4 * (g + 1) * T], flat(x[:, 4 * g:4 * g + 4, :])).then_inc(out_done, 16)
            sp.wait_ge(out_done, 4 * 16)

        @block.gpsimd
        def _(pool):
            def split(stage, i, k):
                if k % 2:
                    pool.wait_ge(hi_ready, quarter(stage, i, k) + 1)
                    n = elems(stage, k)
                    pool.tensor_tensor(w_lo[:, k % SLOTS, 0:n], raw_part(stage, k), whole(w_hi[:, k % SLOTS, 0:n]),
                                       ALU.subtract).then_inc(lo_odd, 1)

            for k in range(AHEAD):
                split("w_in", 0, k)
            for stage, blocks_, qs in STAGES:
                trips = blocks_ // BODY - (stage == LAST)
                with pool.Fori(0, trips) as i:
                    for b in range(BODY):
                        for k in ahead(stage, i if stage != LAST else 0, b):
                            split(stage, i, k)
                for b in range(blocks_ - trips * BODY):
                    for k in ahead(stage, trips, b):
                        split(stage, trips, k)

        @block.tensor
        def _(pe):
            def columns(stage, i, b, hi, lo, need=None, late=None):
                if not (isinstance(i, int) and taken(stage, i, b) == 1):
                    pe.wait_ge(bank_free[b % 2], taken(stage, i, b) - 1)
                qs, c = QUARTERS[stage], 0
                for q, n in enumerate(qs):
                    k = b * len(qs) + q
                    if need is not None:
                        need(q)
                    if late is not None and q == len(qs) - 1:
                        late()
                    pe.wait_ge(lo_odd if k % 2 else lo_even, pairs(stage, i, k))
                    wh = halves(w_hi[:, k % SLOTS, 0:n * COLS], n)
                    wl = halves(w_lo[:, k % SLOTS, 0:n * COLS], n)
                    for kc in range(n):
                        for j in range(2):
                            dst, cols = pm[b % 2][:, j * T:(j + 1) * T], slice(j * P, (j + 1) * P)
                            pe.matmul(dst, wh[:, kc, cols], hi(c + kc), start=(c + kc + j == 0), stop=False, skip_group_check=True)
                            pe.matmul(dst, wh[:, kc, cols], lo(c + kc), start=False, stop=False, skip_group_check=True)
                            mm = pe.matmul(dst, wl[:, kc, cols], hi(c + kc), start=False,
                                           stop=(q == len(qs) - 1 and kc == n - 1), skip_group_check=True)
                    mm.then_inc(quarter_done, 1)
                    c += n

            def tokens(stage, i, b, need=None, late=None):
                if not (isinstance(i, int) and taken(stage, i, b) == 1):
                    pe.wait_ge(bank_free[b % 2], taken(stage, i, b) - 1)
                for q in range(4):
                    k = b * 4 + q
                    if need is not None:
                        need(q)
                    if late is not None and q == 3:
                        late()
                    pe.wait_ge(lo_odd if k % 2 else lo_even, pairs(stage, i, k))
                    wh, wl = (halves(w[:, k % SLOTS, :], 4) for w in (w_hi, w_lo))
                    for kc in range(4):
                        for tt in range(TT):
                            dst, c, ts = pm[b % 2][:, tt * COLS:(tt + 1) * COLS], 4 * q + kc, slice(tt * P, (tt + 1) * P)
                            pe.matmul(dst, h_hi[:, c, ts], wh[:, kc, :], start=(c + tt == 0), stop=False, skip_group_check=True)
                            pe.matmul(dst, h_hi[:, c, ts], wl[:, kc, :], start=False, stop=False, skip_group_check=True)
                            mm = pe.matmul(dst, h_lo[:, c, ts], wh[:, kc, :], start=False, stop=(c == KC - 1), skip_group_check=True)
                    mm.then_inc(quarter_done, 1)

            def sum_unit(u):
                pe.wait_ge(ada_used, u * APIECES + APIECES)
                if not (isinstance(u, int) and u == 0):
                    pe.wait_ge(unit_taken, u)
                for c in range(UCOLS // P):
                    mm = pe.matmul(pv[:, c:c + 1], acc[:, c * P:(c + 1) * P], ones[:, 0:1], start=True, stop=True)
                mm.then_inc(unit_summed, 1)

            def sum_squares(name, src=ssq, half=0):
                pe.wait_ge(sq_added if src is ssq else sqg_added, ADDED[name] if src is ssq else PAIRS)
                if SUMS[name] - half > 1:
                    pe.wait_ge(ms_ready, SUMS[name] - half - 1)
                for j in range(2):
                    mm = pe.matmul(ps[:, half * T:(half + 1) * T], ones[:, :], src[:, j, :], start=(j == 0), stop=(j == 1))
                mm.then_inc(ss_ready, 1)

            def h_needed(norm):
                return lambda q: pe.wait_ge(h_ready, H_NORMS.index(norm) * KC + 4 * (q + 1))

            def stage_columns(stage, unit, lo=0, hi=None, need=None):
                with pe.Fori(lo, hi or NBLOCKS[stage] // BODY) as i:
                    for b in range(BODY):
                        late = (lambda: sum_unit(i + (unit - lo))) if b == BODY - 1 and unit is not None else None
                        columns(stage, i, b, chunk(h_hi), chunk(h_lo), need if b == 0 else None, late)

            pe.wait_ge(const_in, 32)
            pe.wait_ge(ones_set, 1)
            sum_squares("norm1")
            sum_unit(0)
            with pe.Fori(1, FIRST_UNITS) as u:
                sum_unit(u)

            pe.wait_ge(gw_lo_ready, 1)
            for kc in range(KC):
                pe.wait_ge(h_ready, kc + 1)
                for g in range(2):
                    dst, cols = px[0][:, g * T:(g + 1) * T], slice(kc * GROW, kc * GROW + P)
                    pe.matmul(dst, gw_hi[:, g, cols], h_hi[:, kc, :], start=(kc + g == 0), stop=False, skip_group_check=True)
                    pe.matmul(dst, gw_hi[:, g, cols], h_lo[:, kc, :], start=False, stop=False, skip_group_check=True)
                    mm = pe.matmul(dst, gw_lo[:, g, cols], h_hi[:, kc, :], start=False, stop=(kc == KC - 1), skip_group_check=True)
            mm.then_inc(gate_ps, 1)

            def a_head_scores(hd_):
                pe.wait_ge(rows_ready, 1)
                if hd_ == 0:
                    for b in range(2):
                        pe.wait_ge(bank_free[b], 6)
                else:
                    pe.wait_ge(a_out, hd_)
                for sc in range(TT):
                    for dc in range(2):
                        pe.matmul(px[0][:, sc * T:(sc + 1) * T], ka[:, 2 * hd_ + dc, sc * P:(sc + 1) * P],
                                  qa[:, 2 * hd_ + dc, :], start=(dc == 0), stop=(dc == 1))
                for d in range(2):
                    r = hd_ + 32 * d
                    mm = pe.matmul(px[1 + d][:, :], ident[0:GROW, r:r + 1].to_broadcast([GROW, P]), neg_rows[0:GROW, :],
                                   start=True, stop=True)
                mm.then_inc(a_scores, 1)

            def a_head_mix(hd_):
                pe.wait_ge(a_probs, 2 * hd_ + 2)
                if hd_:
                    pe.wait_ge(a_ms, hd_)
                for d in range(2):
                    for sc in range(TT):
                        pe.matmul(px[3][:, d * T:(d + 1) * T], ones[:, :], decay[:, d, sc * T:(sc + 1) * T],
                                  start=(sc == 0), stop=(sc == 1))
                    for ec in range(2):
                        for sc in range(TT):
                            mm = pe.matmul(px[1 + d][:, ec * T:(ec + 1) * T],
                                           va[:, sc, hd_ * DH_A + ec * P:hd_ * DH_A + (ec + 1) * P],
                                           decay[:, d, sc * T:(sc + 1) * T], start=(sc == 0), stop=(sc == 1))
                mm.then_inc(a_num, 1)

            def a_head_norm(hd_):
                pe.wait_ge(a_sq, hd_ + 1)
                for ec in range(2):
                    mm = pe.matmul(px[3][:, 0:T], ones[:, :], hb[:, ec, :], start=(ec == 0), stop=(ec == 1))
                mm.then_inc(a_ss, 1)

            for n in range(NBLOCKS["w_in"]):
                i, b = divmod(n, BODY)
                late = (lambda: sum_unit(FIRST_UNITS + n // 2 - 1)) if n and n % 2 == 0 and n <= 2 * W_IN_UNITS else None
                if n // 4 in (2, 6):
                    tokens("w_in", i, b, late=late)
                else:
                    columns("w_in", i, b, chunk(h_hi), chunk(h_lo), late=late)
                if n == 3:
                    pe.wait_ge(rows_ready, 1)
                    for sc in range(TT):
                        mm = pe.transpose(px[1][:, sc * GROW:(sc + 1) * GROW], gates[0:GROW, 5, sc * P:(sc + 1) * P],
                                          ident[0:GROW, 0:GROW])
                    mm.then_inc(bcol_ps, 1)
                for step, k in W_IN_STEPS.get(n, []):
                    {"scores": a_head_scores, "mix": a_head_mix, "norm": a_head_norm}[step](k)

            for st, hd_ in waves(NH_B, 3):
                bank = px[hd_ % 4]
                if st == 0:
                    if hd_ == 0:
                        for b in range(2):
                            pe.wait_ge(bank_free[b], BBASE["w_out"] // 2)
                        pe.wait_ge(a_out, NH_A)
                    if hd_ >= 4:
                        pe.wait_ge(mix_ready, 4 + hd_ - 3)
                    for tt in range(TT):
                        mm = pe.matmul(bank[:, tt * T:(tt + 1) * T], qb[:, hd_, tt * P:(tt + 1) * P], kb[:, hd_, :],
                                       start=True, stop=True)
                    mm.then_inc(b_scores, 1)
                elif st == 1:
                    pe.wait_ge(b_probs, hd_ + 1)
                    for sc in range(TT):
                        for tt in range(TT):
                            mm = pe.transpose(bank[:, sc * T + tt * P:sc * T + (tt + 1) * P],
                                              s_b[hd_ % 2][:, tt, sc * P:(sc + 1) * P], ident[:, :])
                    mm.then_inc(b_pt, 1)
                else:
                    pe.wait_ge(b_ptsb, hd_ + 1)
                    for sc in range(TT):
                        mm = pe.matmul(bank[:, 0:T], vb[:, sc, hd_ * DH_B:(hd_ + 1) * DH_B], pt_b[hd_ % 2][:, sc, :],
                                       start=(sc == 0), stop=(sc == 1))
                    mm.then_inc(b_num, 1)

            pe.wait_ge(mix_ready, 4 + NH_B)
            stage_columns("w_out", 20)
            sum_squares("norm2")

            for half in range(2):
                up, down = f"w_up{half}", f"w_down{half}"
                if half == 0:
                    stage_columns(up, 22, need=h_needed("norm2"))
                else:
                    stage_columns(up, 27)
                for b in range(FH % BODY):
                    columns(up, FH // BODY, b, chunk(h_hi), chunk(h_lo))
                with pe.Fori(0, NBLOCKS[down] // BODY) as i:
                    for b in range(BODY):
                        need = (lambda q: pe.wait_ge(glu_lo_ready, half * FH + min(4 * q + 4, FH))) if b == 0 else None
                        columns(down, i, b, chunk(glu_hi), chunk(glu_lo), need)
            sum_squares("final")
            sum_squares("final" + "g", ssqg, 1)

            with pe.Fori(0, NBLOCKS["sgu_v"] // BODY) as i:
                for b in range(BODY):
                    tokens("sgu_v", i, b, h_needed("pre0") if b == 0 else None,
                           (lambda: sum_unit(i + 32)) if b == BODY - 1 else None)
            stage_columns("sgu_u", 36)
            pe.wait_ge(v_normed, 2)
            for g in range(GROUPS):
                s, r = g // 2 % 2, g % 2
                if r == 0:
                    pe.wait_ge(mixw_full[s], (g // 4 + 1) * 16)
                if g >= 4:
                    pe.wait_ge(vm_taken, g - 3)
                for c in range(2):
                    for n in range(TT):
                        for part in range(2):
                            seen = slice(0, 64 * (part + 1))
                            t0 = 64 * part
                            mm = pe.matmul(px[g % 4][:, c * T + n * P + t0:c * T + n * P + t0 + 64],
                                           v_sgu[seen, n, g * 2 * P + c * P:g * 2 * P + (c + 1) * P],
                                           mixw[seen, s, r, 0, t0:t0 + 64], start=True, stop=True)
                mm.then_inc(vm_ready, 1)
            stage_columns("sgu_z", 40)
            with pe.Fori(0, NBLOCKS["sgu_out"] // BODY) as i:
                for b in range(BODY):
                    columns("sgu_out", i, b, chunk(y_hi), chunk(y_lo),
                            (lambda q: pe.wait_ge(y_lo_ready, 2 * (q + 1))) if b == 0 else None,
                            (lambda: sum_unit(i + 44)) if b == BODY - 1 else None)
            sum_squares("post0")
            sum_squares("pre1")

            for b in range(BODY):
                columns("lat", 0, b, chunk(h_hi), chunk(h_lo), h_needed("pre1") if b == 0 else None,
                        (lambda: sum_unit(46)) if b == BODY - 1 else None)

            def latent_squares():
                pe.wait_ge(lat_sq, 2)
                pe.wait_ge(ms_ready, SUMS["pre1"])
                for c in range(4):
                    mm = pe.matmul(ps[:, 0:T], ones[:, :], lsq[:, c, :], start=(c == 0), stop=(c == 3))
                mm.then_inc(ss_ready, 1)
                for c in range(4, 8):
                    rows = slice(0, P) if c < 7 else slice(64, P)
                    mm = pe.matmul(ps[:, T:2 * T], ones[rows, :], lsq[rows, c, :], start=(c == 4), stop=(c == 7))
                mm.then_inc(ss_ready, 1)

            def rotated_key():
                pe.wait_ge(mla_const_in, 16)
                pe.wait_ge(vm_taken, GROUPS)
                pe.matmul(px[1][:, 0:T], rot, lat[0:ROPE, 7, :], start=True, stop=True).then_inc(kr_rot, 1)

            for n in range(NBLOCKS["mla_z"]):
                columns("mla_z", n // BODY, n % BODY, chunk(h_hi), chunk(h_lo),
                        late={0: latent_squares, 3: lambda: sum_unit(47), 4: rotated_key}.get(n))
            for b in range(2):
                pe.wait_ge(bank_free[b], BBASE["heads"] // 2)
            pe.wait_ge(ms_ready, SUMS["q"])
            pe.wait_ge(unit_taken, 12 * UNITS)
            pe.wait_ge(lat_lo_ready, 2)
            pe.wait_ge(kr_ready, 1)
            for j in range(4):
                pe.sem_inc(head_free[j], 1)
            bank_a = [pm[0], pm[1], ps, pv]
            with pe.Fori(0, MH // BODY) as i:
                for st, j in waves(BODY, 6):
                    A, B = bank_a[j], px[j]
                    hn = i * BODY + j
                    if st == 0:
                        pe.wait_ge(head_free[j], i + 1)
                        for q in range(2):
                            k = 2 * j + q
                            pe.wait_ge(lo_odd if k % 2 else lo_even, pairs("heads", i, k))
                            wh, wl = (halves(w[:, k % SLOTS, 0:2 * HEADW]) for w in (w_hi, w_lo))
                            for kc in range(2 * q, 2 * q + 2):
                                first, last = kc == 0, kc == 3
                                rows = slice(0, P) if kc < 3 else slice(64, P)
                                for dst, lo, c, r in ((A[:, 0:T], 0, 4 + kc, rows), (A[:, T:2 * T], NOPE, 4 + kc, rows),
                                                      (B[:, 0:T], NOPE + ROPE, kc, slice(0, P))):
                                    cols = slice(lo, lo + P)
                                    pe.matmul(dst, wh[r, kc % 2, cols], lat_hi[r, c, :], start=(first and lo != NOPE), stop=False,
                                              skip_group_check=True)
                                    pe.matmul(dst, wh[r, kc % 2, cols], lat_lo[r, c, :], start=False, stop=False, skip_group_check=True)
                                    pe.matmul(dst, wl[r, kc % 2, cols], lat_hi[r, c, :], start=False, stop=last, skip_group_check=True)
                                for tt in range(TT):
                                    dst, ts = B[:, T + tt * P:T + (tt + 1) * P], slice(tt * P, (tt + 1) * P)
                                    vc = slice(HEADW - VD, HEADW)
                                    pe.matmul(dst, lat_hi[:, kc, ts], wh[:, kc % 2, vc], start=False, stop=False, skip_group_check=True)
                                    pe.matmul(dst, lat_hi[:, kc, ts], wl[:, kc % 2, vc], start=False, stop=False, skip_group_check=True)
                                    mm = pe.matmul(dst, lat_lo[:, kc, ts], wh[:, kc % 2, vc], start=False, stop=last, skip_group_check=True)
                            mm.then_inc(quarter_done, 1)
                    elif st == 1:
                        pe.wait_ge(m_proj, hn + 1)
                        pe.matmul(B[:, 0:T], rot, qr[j], start=True, stop=True).then_inc(m_rot, 1)
                    elif st == 2:
                        pe.wait_ge(m_rope, hn + 1)
                        for lo, tt in ((0, 0), (P, 1)):
                            keys = P * (tt + 1)
                            pe.matmul(A[:, lo:lo + keys], qn[j][:, tt * P:(tt + 1) * P], kv[j][:, 0:keys],
                                      start=True, stop=False)
                            mm = pe.matmul(A[:, lo:lo + keys], qr[j][:, tt * P:(tt + 1) * P], kro[:, 0:keys],
                                           start=False, stop=True)
                        mm.then_inc(m_scores, 1)
                    elif st == 3:
                        pe.wait_ge(m_probs, hn + 1)
                        for lo in (0, P, 2 * P):
                            mm = pe.transpose(B[:, lo:lo + P], pr[j][:, lo:lo + P], ident[:, :])
                        mm.then_inc(m_pt, 1)
                    elif st == 4:
                        pe.wait_ge(m_ptsb, hn + 1)
                        pe.matmul(A[:, 0:T], kv[j][:, T:T + P], pt[j][:, 0:T], start=True, stop=False, skip_group_check=True)
                        pe.matmul(A[:, P:T], kv[j][:, T + P:2 * T], pt[j][:, T:T + P], start=False, stop=True,
                                  skip_group_check=True).then_inc(m_num, 1)
            for j in range(4):
                pe.wait_ge(head_free[j], MH // BODY + 1)
            stage_columns("mla_out", None, need=lambda q: pe.wait_ge(o_ready, 4 * (q + 1)))
            sum_squares("post1")

        @block.scalar
        def _(act):
            chain = Chain(act, act_step)

            def split(stage, i, b):
                for k in ahead(stage, i, b) if b is not None else range(AHEAD):
                    if k % 2 == 0:
                        act.wait_ge(slot_full[k // 2 % SLOTS], (quarter(stage, i, 0) + k) * 2 + 16 - (QBASE[stage] + k) % 8 * 2)
                    if not (isinstance(i, int) and quarter(stage, i, k) < SLOTS):
                        act.wait_ge(quarter_done, quarter(stage, i, k) - (SLOTS - 1))
                    act.activation(w_hi[:, k % SLOTS, 0:elems(stage, k)], raw_part(stage, k), ACT.Copy).then_inc(hi_ready, 1)

            def load_piece(u, k):
                act.wait_ge(ada_used, u * APIECES + (k + 1 - SLOTS))
                act.dma_start(ada[:, k % SLOTS, :], row(a["ada"], u * APIECES + k)).then_inc(ada_full[k % SLOTS], 16)

            def load_ahead(u, pieces):
                for k in pieces:
                    if not (isinstance(u, int) and u * APIECES + k + SLOTS >= 12 * UNITS * APIECES):
                        load_piece(u, k + SLOTS)

            def load_in_body(unit, b):
                if b:
                    load_ahead(unit, body_pieces(b - 1))

            def squares(name, i, b, src):
                c = i * BODY + (b + ADDED[name] - PAIRS)
                if not (isinstance(c, int) and c == 0):
                    act.wait_ge(sq_added, c)
                act.activation(flat(sqt[:, :, :]), src, ACT.Square).then_inc(sq_ready, 1)

            def root(name):
                act.wait_ge(ms_ready, SUMS[name])
                act.activation(rstd[:, :], rstd[:, :], ACT.Sqrt).then_inc(std_ready, 1)

            def modulate(norm, shift):
                k = H_NORMS.index(norm)
                for kc in range(KC):
                    act.wait_ge(xn_ready, k * KC + kc + 1)
                    src, how = nt[:, kc % 4, :], dict(bias=mod(shift, kc), scale=gain[:, k, kc:kc + 1])
                    act.activation(h_hi[:, kc, :], src, ACT.Identity, **how)
                    if kc >= 2:
                        act.wait_ge(h_ready, k * KC + kc - 1)
                    act.activation(sqt[:, kc % 2, :], src, ACT.Identity, **how).then_inc(hh_ready, 1)

            act.wait_ge(const_in, 32)
            act.activation(flat(csil[:, :, :]), pcols("c", 2 * KC), ACT.Silu).then_inc(silu_c, 1)
            act.wait_ge(x_in, 16)
            for p in range(PAIRS):
                squares("norm1", 0, p, flat(x[:, 2 * p:2 * p + 2, :]))
            act.wait_ge(mix_const_in, 32)
            act.activation(flat(gw_hi[:, :, :]), flat(gw[:, :, :]), ACT.Copy).then_inc(gw_hi_ready, 1)
            root("norm1")
            for k in range(SLOTS):
                load_piece(FIRST_UNITS, k)
            modulate("norm1", SH1)
            split("w_in", 0, None)

            act.wait_ge(gate_rows, 1)
            chain.link(act.activation(gates[0:GROW, 3, :], gates[0:GROW, 2, :], ACT.Exp))
            act.activation(gates[0:GROW, 3, :], gates[0:GROW, 3, :], ACT.Ln, bias=1.0).then_inc(gate_exp, 1)

            def a_head_scores(hd_):
                for d in range(2):
                    r = hd_ + 32 * d
                    act.wait_ge(a_arg, 2 * hd_ + d + 1)
                    for sc in range(TT):
                        act.activation(decay[:, d, sc * T:(sc + 1) * T], decay[:, d, sc * T:(sc + 1) * T], ACT.Exp,
                                       bias=bcol[:, sc, r:r + 1])
                    act.activation(expm[:, d, :], px[1 + d][:, T:2 * T], ACT.Exp).then_inc(a_exp, 1)
                if hd_ == NH_A - 1:
                    act.dma_start(flat(bias_b[:, :, :]), a["bias_b"]).then_inc(bias_in, 16)

            def a_head_mix(hd_):
                act.wait_ge(a_h, hd_ + 1)
                act.activation(hb[:, :, :], hf[:, :, :], ACT.Square).then_inc(a_sq, 1)

            def a_head_norm(hd_):
                act.wait_ge(a_ms, hd_ + 1)
                act.activation(expm[:, 0, :], expm[:, 0, :], ACT.Sqrt).then_inc(a_std, 1)

            dsts = [ka, qa, va, oa, qb, kb, vb]
            for n in range(NBLOCKS["w_in"]):
                i, b = divmod(n, BODY)
                split("w_in", i, b)
                act.wait_ge(quarter_done, done("w_in", i, b))
                dst = dsts[i][:, :, b * COLS:(b + 1) * COLS] if i in (2, 6) else dsts[i][:, 2 * b:2 * b + 2, :]
                if n == 16:
                    act.wait_ge(rows_ready, 1)
                    act.wait_ge(bcol_ready, 1)
                act.activation(dst, halves(pm[b % 2][:, :]), ACT.Sigmoid if i == 3 else ACT.Copy).then_inc(bank_free[b % 2], 1)
                for step, k in W_IN_STEPS.get(n, []):
                    {"scores": a_head_scores, "mix": a_head_mix, "norm": a_head_norm}[step](k)
                if 1 <= n <= 2 * W_IN_UNITS:
                    load_ahead(FIRST_UNITS + (n - 1) // 2, range((n - 1) % 2 * SLOTS, (n - 1) % 2 * SLOTS + SLOTS))

            act.wait_ge(a_out, NH_A)
            for p in range(4):
                act.activation(h_hi[:, 2 * p:2 * p + 2, :], oa[:, 2 * p:2 * p + 2, :], ACT.Copy).then_inc(oa_hi, 1)
            for st, hd_ in waves(NH_B, 3):
                j = hd_ % 2
                if st == 0:
                    act.wait_ge(b_negmax, hd_ + 1)
                    for tt in range(TT):
                        ex = act.activation(s_b[j][:, tt, :], s_b[j][:, tt, :], ACT.Exp, bias=small_b[:, j, 1, tt:tt + 1],
                                            accum_out=small_b[:, j, 2, tt:tt + 1])
                    ex.then_inc(b_exp, 1)
                elif st == 1:
                    act.wait_ge(b_pt, hd_ + 1)
                    if hd_ >= 2:
                        act.wait_ge(b_num, hd_ - 1)
                    act.activation(flat(pt_b[j][:, :, :]), px[hd_ % 4][:, :], ACT.Copy).then_inc(b_ptsb, 1)
                else:
                    act.wait_ge(b_num, hd_ + 1)
                    act.activation(h_hi[:, 8 + hd_, :], px[hd_ % 4][:, 0:T], ACT.Copy).then_inc(b_hi, 1)

            with act.Fori(0, NBLOCKS["w_out"] // BODY) as i:
                for b in range(BODY):
                    split("w_out", i, b)
                    load_in_body(i + 20, b)
                    act.wait_ge(bank_free[b % 2], taken("w_out", i, b))
                    squares("norm2", i, b, at(x, i * (2 * BODY) + 2 * b, 2).rearrange("p a b -> p (a b)"))
            root("norm2")
            modulate("norm2", SH2)

            def up(half, i, b, unit):
                stage, k = f"w_up{half}", i * BODY + (half * FH + b)
                split(stage, i, b)
                act.wait_ge(quarter_done, done(stage, i, b))
                act.activation(gpad[:, 1:1 + T], pm[b % 2][:, 0:T], ACT.Copy).then_inc(g_copied, 1)
                act.wait_ge(conv_ready, k + 1)
                act.activation(conv[:, :], conv[:, :], ACT.Gelu).then_inc(gelu_ready, 1)
                if unit is not None:
                    load_in_body(unit, b)
                act.wait_ge(bank_free[b % 2], taken(stage, i, b))
                act.activation(one(glu_hi, i * BODY + b), conv[:, :], ACT.Copy).then_inc(glu_hi_ready, 1)

            for half in range(2):
                down = f"w_down{half}"
                with act.Fori(0, FH // BODY) as i:
                    for b in range(BODY):
                        up(half, i, b, i + (27 if half else 22))
                for b in range(FH % BODY):
                    up(half, FH // BODY, b, None)
                with act.Fori(0, NBLOCKS[down] // BODY) as i:
                    for b in range(BODY):
                        split(down, i, b)
                        if half == 1:
                            act.wait_ge(bank_free[b % 2], taken(down, i, b))
                            c = i * (2 * BODY) + 2 * b
                            squares("final", i, b, at(x, c, 2).rearrange("p a b -> p (a b)"))
                            for j in range(2):
                                sg = act.activation(sqtg[:, j, :], one(x, c + j), ACT.Square, scale=pcol("gfinal", c + j))
                            sg.then_inc(sqg_ready, 1)
            root("final")
            root("finalg")
            modulate("pre0", S0)

            with act.Fori(0, NBLOCKS["sgu_v"] // BODY) as i:
                for b in range(BODY):
                    split("sgu_v", i, b)
                    act.wait_ge(quarter_done, done("sgu_v", i, b))
                    for tt in range(TT):
                        ge = act.activation(v_sgu[:, tt, bass.ds((i * BODY + b) * COLS, COLS)], pm[b % 2][:, tt * COLS:(tt + 1) * COLS],
                                            ACT.Gelu, accum_out=stat[:, tt, bass.ds(i * BODY + b, 1)])
                    ge.then_inc(bank_free[b % 2], 1)
                    load_in_body(i + 32, b)
            act.wait_ge(h_ready, 3 * KC)

            def load_mix(p):
                act.dma_start(mixw[:, p % 2, :, :, :].rearrange("p a b c -> p (a b c)"), a["mix"][p]).then_inc(mixw_full[p % 2], 16)

            for p in range(2):
                load_mix(p)

            def u_block(i, b):
                split("sgu_u", i, b)
                act.wait_ge(quarter_done, done("sgu_u", i, b))
                act.activation(at(gu, i * (2 * BODY) + 2 * b, 2), halves(pm[b % 2][:, :]), ACT.Gelu).then_inc(bank_free[b % 2], 1)
                load_in_body(i + 36, b)

            with act.Fori(0, 2) as i:
                for b in range(BODY):
                    u_block(i, b)
                    tt = b // 2
                    act.wait_ge(v_mean, tt + 1)
                    for r in range(2):
                        part = i * 4 + (b % 2 * 2 + r)
                        sq = act.activation(stmp[:, r, :], v_sgu[:, tt, bass.ds(part * 512, 512)], ACT.Square,
                                            accum_out=stat[:, tt, bass.ds(part + 16, 1)])
                    sq.then_inc(v_sq, 1)
                    act.wait_ge(v_sq, i * BODY + (b + 1))
            for tt in range(TT):
                act.wait_ge(v_var, tt + 1)
                act.activation(stat[:, tt, 28:29], stat[:, tt, 27:28], ACT.Sqrt).then_inc(v_std, 1)
            with act.Fori(2, 4) as i:
                for b in range(BODY):
                    u_block(i, b)
            for p in range(2, GROUPS // 2):
                act.wait_ge(vm_taken, 2 * p - 2)
                load_mix(p)
            act.wait_ge(vm_taken, GROUPS)
            with act.Fori(0, NBLOCKS["sgu_z"] // BODY) as i:
                for b in range(BODY):
                    split("sgu_z", i, b)
                    act.wait_ge(quarter_done, done("sgu_z", i, b))
                    act.activation(ztmp[:, b % 2, :], pm[b % 2][:, :], ACT.Silu).then_inc(bank_free[b % 2], 1)
                    load_in_body(i + 40, b)
                    act.wait_ge(y_ready, i * BODY + (b + 1))
                    act.activation(at(y_hi, i * (2 * BODY) + 2 * b, 2), at(gu, i * (2 * BODY) + 2 * b, 2), ACT.Copy).then_inc(y_hi_ready, 1)

            def output_block(stage, i, b, norm, dst):
                split(stage, i, b)
                act.wait_ge(quarter_done, done(stage, i, b))
                squares(norm, i, b, pm[b % 2][:, :])
                act.activation(at(dst, i * (2 * BODY) + 2 * b, 2), halves(pm[b % 2][:, :]), ACT.Copy).then_inc(bank_free[b % 2], 1)

            with act.Fori(0, NBLOCKS["sgu_out"] // BODY) as i:
                for b in range(BODY):
                    output_block("sgu_out", i, b, "post0", y0)
                    load_in_body(i + 44, b)
            root("post0")
            for p in range(PAIRS):
                act.wait_ge(x_ready, p // 2 + 1)
                squares("pre1", 0, p, flat(x[:, 2 * p:2 * p + 2, :]))
            root("pre1")
            modulate("pre1", S1)

            for b in range(BODY):
                split("lat", 0, b)
                act.wait_ge(quarter_done, done("lat", 0, b))
                if b == 0:
                    act.dma_start(cst[:, :], a["mla_cst"]).then_inc(mla_const_in, 16)
                act.activation(lat[:, 2 * b:2 * b + 2, :], halves(pm[b % 2][:, :]), ACT.Copy).then_inc(bank_free[b % 2], 1)
                load_in_body(46, b)
            for b in range(2):
                act.wait_ge(bank_free[b], BBASE["mla_z"] // 2)
            for part in range(2):
                act.activation(lsq[:, 4 * part:4 * part + 4, :], lat[:, 4 * part:4 * part + 4, :], ACT.Square).then_inc(lat_sq, 1)
            for n in range(NBLOCKS["mla_z"]):
                i, b = divmod(n, BODY)
                split("mla_z", i, b)
                act.wait_ge(quarter_done, done("mla_z", i, b))
                act.activation(zo[:, 2 * n:2 * n + 2, :], halves(pm[b % 2][:, :]), ACT.Silu).then_inc(bank_free[b % 2], 1)
                if i == 0:
                    load_in_body(47, b)
                if n in (1, 2):
                    root({1: "kv", 2: "q"}[n])
                if n == 3:
                    for part in range(2):
                        act.wait_ge(lat_normed, part + 1)
                        act.activation(lat_hi[:, 4 * part:4 * part + 4, :], lat[:, 4 * part:4 * part + 4, :], ACT.Copy).then_inc(lat_hi_ready, 1)
            with act.Fori(0, MH // BODY) as i:
                for st, j in waves(BODY, 6):
                    hn = i * BODY + j
                    A, B = [pm[0], pm[1], ps, pv][j], px[j]
                    if st == 0:
                        split("heads", i, j)
                        act.wait_ge(quarter_done, done("heads", i, j))
                        act.activation(qn[j], A[:, 0:T], ACT.Copy)
                        act.activation(qr[j], A[0:ROPE, T:2 * T], ACT.Copy)
                        act.activation(kv[j], B[:, :], ACT.Copy).then_inc(m_proj, 1)
                    elif st == 2:
                        act.wait_ge(m_negmax, hn + 1)
                        for lo, tt in ((0, 0), (P, 1)):
                            keys = P * (tt + 1)
                            ex = act.activation(pr[j][:, lo:lo + keys], pr[j][:, lo:lo + keys], ACT.Exp,
                                                bias=small_m[:, j, 1, tt:tt + 1], accum_out=small_m[:, j, 2, tt:tt + 1])
                        ex.then_inc(m_exp, 1)
                    elif st == 3:
                        act.wait_ge(m_pt, hn + 1)
                        act.activation(pt[j][:, :], B[:, 0:3 * P], ACT.Copy).then_inc(m_ptsb, 1)
                    elif st == 5:
                        act.wait_ge(head_free[j], i + 2)
                        act.activation(one(h_hi, hn), one(zo, hn), ACT.Copy).then_inc(m_hi, 1)
            for n in range(NBLOCKS["mla_out"]):
                output_block("mla_out", n // BODY, n % BODY, "post1", y1)
            root("post1")

        @block.vector
        def _(dve):
            chain = Chain(dve, dve_step)
            tt_ = dve.tensor_tensor
            ts_ = dve.tensor_scalar
            stt = dve.scalar_tensor_tensor

            def split(stage, i, b):
                for k in ahead(stage, i, b) if b is not None else range(AHEAD):
                    if k % 2 == 0:
                        dve.wait_ge(hi_ready, quarter(stage, i, k) + 1)
                        n = elems(stage, k)
                        tt_(w_lo[:, k % SLOTS, 0:n], raw_part(stage, k), whole(w_hi[:, k % SLOTS, 0:n]),
                            ALU.subtract).then_inc(lo_even, 1)

            def accumulate(u, k, cond, buf, full):
                dve.wait_ge(ada_full[full[0]], full[1])
                for r in range(2):
                    w, c = buf[:, r * UCOLS:(r + 1) * UCOLS], csil[:, cond, 2 * k + r:2 * k + r + 1]
                    if k + r == 0:
                        ins = ts_(acc[:, :], w, c, None, ALU.mult)
                    else:
                        ins = stt(acc[:, :], w, c, acc[:, :], ALU.mult, ALU.add)
                    if r == 0:
                        chain.link(ins)
                ins.then_inc(ada_used, 1)
                dve.wait_ge(ada_used, u * APIECES + (k + 1))

            def pieces(u, cond, ks):
                for k in ks:
                    accumulate(u, k, cond, ada[:, k % SLOTS, :], (k % SLOTS, u * 32 + (k // SLOTS + 1 - FIRST_UNITS) * 16))

            def take(u):
                dve.wait_ge(unit_summed, u + 1)
                cols = bass.ds(u * 4, 4) if not isinstance(u, int) else slice(4 * u, 4 * u + 4)
                bias = bass.ds(u * 4 + PCOL["bias"], 4) if not isinstance(u, int) else slice(PCOL["bias"] + 4 * u, PCOL["bias"] + 4 * u + 4)
                tt_(mods[:, cols], pv[:, 0:4], par[:, bias], ALU.add).then_inc(unit_taken, 1)
                dve.wait_ge(unit_taken, u + 1)

            def unit_at(u, cond, b):
                pieces(u, cond, body_pieces(b))
                if b == BODY - 1:
                    take(u)

            def clear_squares(*more):
                for buf in more:
                    dve.memset(flat(buf[:, :, :]), 0.0)
                chain.link(dve.memset(flat(ssq[:, :, :]), 0.0))

            def add_squares(name, i, b):
                dve.wait_ge(sq_ready, i * BODY + (b + 1 + ADDED[name] - PAIRS))
                tt_(ssq[:, :, :], ssq[:, :, :], sqt[:, :, :], ALU.add).then_inc(sq_added, 1)

            def rsqrt_mean(name, width, half=0, dst=rstd):
                dve.wait_ge(ss_ready, SUMS[{"final": "finalg", "kv": "q"}.get(name, name)])
                ts_(rstd[:, :], ps[:, half * T:(half + 1) * T], 1.0 / width, EPS, ALU.mult, ALU.add).then_inc(ms_ready, 1)
                dve.wait_ge(std_ready, SUMS[name])
                chain.link(dve.reciprocal(dst[:, :], rstd[:, :]))

            def modulation(norm, g, gc, scale):
                chain.link(stt(gain[:, H_NORMS.index(norm), :], mods[:, scale * KC:(scale + 1) * KC], 1.0, pcols(g, KC, gc),
                               ALU.add, ALU.mult))

            def normed(norm):
                def xn(kc):
                    tt_(nt[:, kc % 4, :], x[:, kc, :], rstd[:, :], ALU.mult).then_inc(xn_ready, 1)

                for kc in range(4):
                    xn(kc)
                for kc in range(KC):
                    dve.wait_ge(hh_ready, H_NORMS.index(norm) * KC + kc + 1)
                    tt_(h_lo[:, kc, :], sqt[:, kc % 2, :], whole(h_hi[:, kc, :]), ALU.subtract).then_inc(h_ready, 1)
                    if kc + 4 < KC:
                        xn(kc + 4)

            def residual(stage, i, b, gate):
                dve.wait_ge(quarter_done, done(stage, i, b))
                for j in range(2):
                    c = i * (2 * BODY) + (2 * b + j)
                    xc = one(x, c)
                    ins = stt(xc, pm[b % 2][:, j * T:(j + 1) * T], mod(gate, c), xc, ALU.mult, ALU.add)
                ins.then_inc(bank_free[b % 2], 1)

            dve.memset(ones[:, :], 1.0).then_inc(ones_set, 1)
            dve.memset(gates[0:GROW, :, :], 0.0)
            clear_squares()
            for p in range(PAIRS):
                add_squares("norm1", 0, p)
            dve.wait_ge(gw_hi_ready, 1)
            tt_(gw_lo[:, :, :], gw[:, :, :], whole(gw_hi[:, :, :]), ALU.subtract).then_inc(gw_lo_ready, 1)
            rsqrt_mean("norm1", D)
            dve.wait_ge(silu_c, 1)
            with dve.Fori(0, FIRST_UNITS) as u:
                chain.enter(u, APIECES)
                for k in range(APIECES):
                    accumulate(u, k, 0, ada[:, k, :] if k < SLOTS else e1[:, k - SLOTS, :], (k, u * 16 + 16))
                take(u)
                chain.leave(FIRST_UNITS)
            modulation("norm1", "g1", 0, SC1)
            normed("norm1")
            split("w_in", 0, None)

            G = slice(0, GROW)

            def gate_step(n):
                if n == 0:
                    dve.wait_ge(gate_ps, 1)
                    chain.link(ts_(gates[G, 0, :], px[0][G, 0:T], pcol("bi", 0, G), None, ALU.add))
                    chain.link(ts_(gates[G, 1, :], px[0][G, T:2 * T], pcol("bf", 0, G), None, ALU.add))
                    stt(gates[G, 2, :], gates[G, 1, :], -1.0, gates[G, 1, :], ALU.mult, ALU.min).then_inc(gate_rows, 1)
                elif n == 1:
                    dve.wait_ge(gate_exp, 1)
                    chain.link(stt(gates[G, 1, :], gates[G, 1, :], 0.0, gates[G, 3, :], ALU.min, ALU.subtract))
                    for rows, step in ((slice(0, NH_A), 1), (slice(32, GROW), -1)):
                        chain.link(dve.tensor_tensor_scan(gates[rows, 4, ::step], ones[rows, 0:1].to_broadcast([NH_A, T]),
                                                          gates[rows, 1, ::step], 0.0, ALU.mult, ALU.add))
                    chain.link(tt_(gates[G, 5, :], gates[G, 0, :], gates[G, 4, :], ALU.subtract))
                elif n == 2:
                    for rows, step in ((slice(0, NH_A), 1), (slice(32, GROW), -1)):
                        chain.link(dve.tensor_tensor_scan(gates[rows, 6, ::step], gates[rows, 5, ::step], gates[rows, 5, ::step],
                                                          -3.0e38, ALU.max, ALU.max))
                    chain.link(ts_(neg_rows[G, 0:T], gates[G, 6, :], -1.0, None, ALU.mult))
                    stt(neg_rows[G, T:2 * T], gates[G, 4, :], -1.0, gates[G, 6, :], ALU.mult, ALU.subtract).then_inc(rows_ready, 1)
                else:
                    dve.wait_ge(bcol_ps, 1)
                    dve.tensor_copy(flat(bcol[:, :, :]), px[1][:, 0:2 * GROW]).then_inc(bcol_ready, 1)

            def a_head_scores(hd_):
                dve.wait_ge(a_scores, hd_ + 1)
                if hd_:
                    dve.wait_ge(a_num, hd_)
                for d in range(2):
                    tt_(halves(decay[:, d, :]), over(px[1 + d][:, 0:T], 2), halves(mask_a[:, d, :]), ALU.add).then_inc(a_arg, 1)
                for d in range(2):
                    dve.wait_ge(a_exp, 2 * hd_ + d + 1)
                    stt(decay[:, d, :], px[0][:, :], SCALE_A, decay[:, d, :], ALU.mult, ALU.mult).then_inc(a_probs, 1)

            def a_head_mix(hd_):
                dve.wait_ge(a_num, hd_ + 1)
                em = flat(expm[:, :, :])
                chain.link(stt(em, px[3][:, :], -1.0, em, ALU.mult, ALU.max))
                chain.link(tt_(em, px[3][:, :], em, ALU.max))
                chain.link(dve.reciprocal(em, em))
                tt_(hf[:, :, :], halves(px[1][:, :]), over(expm[:, 0, :], 2), ALU.mult)
                chain.link(tt_(hb[:, :, :], halves(px[2][:, :]), over(expm[:, 1, :], 2), ALU.mult))
                tt_(hf[:, :, :], hf[:, :, :], hb[:, :, :], ALU.add).then_inc(a_h, 1)

            def a_head_norm(hd_):
                dve.wait_ge(a_ss, hd_ + 1)
                ts_(expm[:, 0, :], px[3][:, 0:T], 1.0 / DH_A, EPS, ALU.mult, ALU.add).then_inc(a_ms, 1)
                dve.wait_ge(a_std, hd_ + 1)
                chain.link(dve.reciprocal(expm[:, 0, :], expm[:, 0, :]))
                dve.wait_ge(bank_free[hd_ % 2], taken("w_in", 3, hd_))
                for ec in range(2):
                    ins = stt(hf[:, ec, :], hf[:, ec, :], pcol("ghead", 2 * hd_ + ec), expm[:, 0, :], ALU.mult, ALU.mult)
                chain.link(ins)
                oh = oa[:, 2 * hd_:2 * hd_ + 2, :]
                tt_(oh, oh, hf[:, :, :], ALU.mult).then_inc(a_out, 1)

            gate_step(0)
            for n in range(NBLOCKS["w_in"]):
                split("w_in", n // BODY, n % BODY)
                if n < 2:
                    gate_step(n + 1)
                if n == 4:
                    gate_step(3)
                if n % 2 == 0 and 0 < n <= 2 * W_IN_UNITS:
                    take(FIRST_UNITS + n // 2 - 1)
                for step, k in W_IN_STEPS.get(n, []):
                    {"scores": a_head_scores, "mix": a_head_mix, "norm": a_head_norm}[step](k)
                if n < 2 * W_IN_UNITS:
                    pieces(FIRST_UNITS + n // 2, 0, range(n % 2 * SLOTS, n % 2 * SLOTS + SLOTS))
                if n == 24:
                    dve.wait_ge(bias_in, 16)
                    dve.wait_ge(wmask_in, 16)
                    chain.link(tt_(bias_b[:, :, :], bias_b[:, :, :], over(wmask[:, :], NH_B * 6), ALU.add))

            bias_rows = flat(bias_b[:, :, :])
            for st, hd_ in waves(NH_B, 3):
                j = hd_ % 2
                if st == 0:
                    dve.wait_ge(b_scores, hd_ + 1)
                    if hd_ >= 2:
                        dve.wait_ge(b_pt, hd_ - 1)
                    for tt in range(TT):
                        lo = hd_ * 6 * GRID_W + (2 - 2 * tt) * GRID_W
                        ins = stt(s_b[j][:, tt, :], px[hd_ % 4][:, tt * T:(tt + 1) * T], SCALE_B, bias_rows[:, lo:lo + T],
                                  ALU.mult, ALU.add)
                    chain.link(ins)
                    chain.link(dve.tensor_reduce(small_b[:, j, 0, :], s_b[j], AX.X, ALU.max))
                    ts_(small_b[:, j, 1, :], small_b[:, j, 0, :], -1.0, None, ALU.mult).then_inc(b_negmax, 1)
                    if hd_ == 0:
                        for p in range(4):
                            dve.wait_ge(oa_hi, p + 1)
                            tt_(h_lo[:, 2 * p:2 * p + 2, :], oa[:, 2 * p:2 * p + 2, :], whole(h_hi[:, 2 * p:2 * p + 2, :]),
                                ALU.subtract).then_inc(mix_ready, 1)
                    dve.wait_ge(b_exp, hd_ + 1)
                    chain.link(dve.reciprocal(small_b[:, j, 3, :], small_b[:, j, 2, :]))
                    for tt in range(TT):
                        ins = ts_(s_b[j][:, tt, :], s_b[j][:, tt, :], small_b[:, j, 3, tt:tt + 1], None, ALU.mult)
                    ins.then_inc(b_probs, 1)
                elif st == 2:
                    dve.wait_ge(b_hi, hd_ + 1)
                    tt_(h_lo[:, 8 + hd_, :], px[hd_ % 4][:, 0:T], whole(h_hi[:, 8 + hd_, :]), ALU.subtract).then_inc(mix_ready, 1)

            clear_squares()
            with dve.Fori(0, NBLOCKS["w_out"] // BODY) as i:
                chain.enter(i, APIECES)
                for b in range(BODY):
                    split("w_out", i, b)
                    residual("w_out", i, b, GA1)
                    unit_at(i + 20, 0, b)
                    add_squares("norm2", i, b)
                chain.leave(NBLOCKS["w_out"] // BODY)
            rsqrt_mean("norm2", D)
            modulation("norm2", "g2", 0, SC2)
            normed("norm2")

            dve.memset(gpad[:, 0:1], 0.0)
            chain.link(dve.memset(gpad[:, T + 1:T + 2], 0.0))

            def up(half, i, b, unit, cond):
                stage, k = f"w_up{half}", i * BODY + (half * FH + b)
                due = list(body_pieces(b)) if unit is not None else []
                split(stage, i, b)
                if b:
                    dve.wait_ge(glu_lo_ready, k)
                dve.wait_ge(g_copied, k + 1)
                chain.link(ts_(conv[:, :], gpad[:, 0:T], pcol("conv", k * 4), pcol("conv", k * 4 + 3), ALU.mult, ALU.add))
                chain.link(stt(conv[:, :], gpad[:, 1:T + 1], pcol("conv", k * 4 + 1), conv[:, :], ALU.mult, ALU.add))
                stt(conv[:, :], gpad[:, 2:T + 2], pcol("conv", k * 4 + 2), conv[:, :], ALU.mult, ALU.add).then_inc(conv_ready, 1)
                pieces(unit, cond, due[:1])
                dve.wait_ge(gelu_ready, k + 1)
                tt_(conv[:, :], conv[:, :], pm[b % 2][:, T:2 * T], ALU.mult).then_inc(bank_free[b % 2], 1)
                pieces(unit, cond, due[1:2])
                dve.wait_ge(glu_hi_ready, k + 1)
                c = i * BODY + b
                tt_(one(glu_lo, c), conv[:, :], whole(one(glu_hi, c)), ALU.subtract).then_inc(glu_lo_ready, 1)
                pieces(unit, cond, due[2:])
                if unit is not None and b == BODY - 1:
                    take(unit)

            for half, runs in ((0, ((0, 2, 0), (2, 5, 1))), (1, ((0, 5, 1),))):
                for lo, hi, cond in runs:
                    with dve.Fori(lo, hi) as i:
                        chain.enter(i - lo, 2 * BODY + APIECES)
                        for b in range(BODY):
                            up(half, i, b, i + (27 if half else 22), cond)
                        chain.leave(hi - lo)
                for b in range(FH % BODY):
                    up(half, FH // BODY, b, None, 1)
                down = f"w_down{half}"
                if half == 1:
                    clear_squares(ssqg)
                with dve.Fori(0, NBLOCKS[down] // BODY) as i:
                    for b in range(BODY):
                        split(down, i, b)
                        residual(down, i, b, GA2)
                        if half == 1:
                            dve.wait_ge(sqg_ready, i * BODY + (b + 1))
                            tt_(ssqg[:, :, :], ssqg[:, :, :], sqtg[:, :, :], ALU.add).then_inc(sqg_added, 1)
                            add_squares("final", i, b)

            k = H_NORMS.index("pre0")
            modulation("pre0", "pre", 0, C0)
            chain.link(tt_(gain[:, k, :], gain[:, k, :], pcols("gfinal", KC), ALU.mult))
            rsqrt_mean("final", D, dst=rs1)
            chain.link(tt_(rstd[:, :], rs1[:, :], rs1[:, :], ALU.mult))
            chain.link(tt_(rstd[:, :], rstd[:, :], ps[:, T:2 * T], ALU.mult))
            ts_(rstd[:, :], rstd[:, :], 1.0 / D, EPS, ALU.mult, ALU.add).then_inc(ms_ready, 1)
            dve.wait_ge(std_ready, SUMS["finalg"])
            chain.link(dve.reciprocal(rstd[:, :], rstd[:, :]))
            chain.link(tt_(rstd[:, :], rstd[:, :], rs1[:, :], ALU.mult))
            normed("pre0")

            with dve.Fori(0, NBLOCKS["sgu_v"] // BODY) as i:
                chain.enter(i, APIECES + BODY)
                for b in range(BODY):
                    split("sgu_v", i, b)
                    c = i * BODY + b
                    chain.link(stt(one(x, c), one(x, c), pcol("gfinal", c), rs1[:, :], ALU.mult, ALU.mult))
                    unit_at(i + 32, 1, b)
                chain.leave(NBLOCKS["sgu_v"] // BODY)
            for b in range(2):
                dve.wait_ge(bank_free[b], BBASE["sgu_u"] // 2)
            for tt in range(TT):
                chain.link(dve.tensor_reduce(stat[:, tt, 24:25], stat[:, tt, 0:16], AX.X, ALU.add))
                chain.link(ts_(stat[:, tt, 25:26], stat[:, tt, 24:25], -1.0 / SGU_W, None, ALU.mult))
                ts_(v_sgu[:, tt, :], v_sgu[:, tt, :], stat[:, tt, 25:26], None, ALU.add).then_inc(v_mean, 1)

            def u_bodies(lo, hi):
                with dve.Fori(lo, hi) as i:
                    chain.enter(i - lo, APIECES)
                    for b in range(BODY):
                        split("sgu_u", i, b)
                        unit_at(i + 36, 1, b)
                    chain.leave(hi - lo)

            u_bodies(0, 2)
            dve.wait_ge(v_sq, 8)
            for tt in range(TT):
                chain.link(dve.tensor_reduce(stat[:, tt, 26:27], stat[:, tt, 16:24], AX.X, ALU.add))
                ts_(stat[:, tt, 27:28], stat[:, tt, 26:27], 1.0 / SGU_W, EPS, ALU.mult, ALU.add).then_inc(v_var, 1)
            for tt in range(TT):
                dve.wait_ge(v_std, tt + 1)
                chain.link(dve.reciprocal(stat[:, tt, 29:30], stat[:, tt, 28:29]))
                ts_(v_sgu[:, tt, :], v_sgu[:, tt, :], stat[:, tt, 29:30], None, ALU.mult).then_inc(v_normed, 1)
            u_bodies(2, 4)
            for b in range(2):
                dve.wait_ge(bank_free[b], BBASE["sgu_z"] // 2)
            for g in range(GROUPS):
                dve.wait_ge(vm_ready, g + 1)
                bs = mixw[:, g // 2 % 2, g % 2, 1, :]
                for c in range(2):
                    ins = stt(halves(stmp[:, g % 2, c * T:(c + 1) * T]), halves(px[g % 4][:, c * T:(c + 1) * T]),
                              pcol("gsgu", 2 * g + c), over(bs, 2), ALU.mult, ALU.add)
                chain.link(ins)
                gg = gu[:, 2 * g:2 * g + 2, :]
                tt_(gg, gg, halves(stmp[:, g % 2, :]), ALU.mult).then_inc(vm_taken, 1)
            with dve.Fori(0, NBLOCKS["sgu_z"] // BODY) as i:
                chain.enter(i, APIECES)
                for b in range(BODY):
                    split("sgu_z", i, b)
                    c = i * (2 * BODY) + 2 * b
                    due = list(body_pieces(b))
                    dve.wait_ge(bank_free[b % 2], taken("sgu_z", i, b))
                    tt_(at(gu, c, 2), at(gu, c, 2), halves(ztmp[:, b % 2, :]), ALU.mult).then_inc(y_ready, 1)
                    pieces(i + 40, 1, due[:1])
                    dve.wait_ge(y_hi_ready, i * BODY + (b + 1))
                    tt_(at(y_lo, c, 2), at(gu, c, 2), whole(at(y_hi, c, 2)), ALU.subtract).then_inc(y_lo_ready, 1)
                    pieces(i + 40, 1, due[1:])
                    if b == BODY - 1:
                        take(i + 40)
                chain.leave(NBLOCKS["sgu_z"] // BODY)
            clear_squares()
            with dve.Fori(0, NBLOCKS["sgu_out"] // BODY) as i:
                chain.enter(i, APIECES)
                for b in range(BODY):
                    split("sgu_out", i, b)
                    add_squares("post0", i, b)
                    unit_at(i + 44, 1, b)
                chain.leave(NBLOCKS["sgu_out"] // BODY)

            def post(name, layer, gate, y, taken_, then=None):
                chain.link(tt_(gain[:, 4, :], pcols("post", KC, layer * KC), mods[:, gate * KC:(gate + 1) * KC], ALU.mult))
                rsqrt_mean(name, D)
                for b in range(2):
                    dve.wait_ge(bank_free[b], taken_)
                for g in range(4):
                    for kc in range(4 * g, 4 * g + 4):
                        ins = stt(y[:, kc, :], y[:, kc, :], gain[:, 4, kc:kc + 1], rstd[:, :], ALU.mult, ALU.mult)
                    chain.link(ins)
                    xg = x[:, 4 * g:4 * g + 4, :]
                    tt_(xg, xg, y[:, 4 * g:4 * g + 4, :], ALU.add).then_inc(x_ready, 1)
                    if then is not None:
                        then(g)

            def pre1_squares(g):
                if g == 0:
                    clear_squares()
                else:
                    for p in (2 * g - 2, 2 * g - 1):
                        add_squares("pre1", 0, p)

            post("post0", 0, G0, y0, BBASE["lat"] // 2, pre1_squares)
            pre1_squares(4)
            modulation("pre1", "pre", KC, C1)
            rsqrt_mean("pre1", D)
            normed("pre1")

            for b in range(BODY):
                split("lat", 0, b)
                unit_at(46, 1, b)
            for n in range(NBLOCKS["mla_z"]):
                i, b = divmod(n, BODY)
                split("mla_z", i, b)
                if n == 1:
                    rsqrt_mean("kv", KVR)
                    for c in range(4):
                        ins = stt(lat[:, c, :], lat[:, c, :], pcol("gkv", c), rstd[:, :], ALU.mult, ALU.mult)
                    ins.then_inc(lat_normed, 1)
                    dve.wait_ge(lat_normed, 1)
                if n == 2:
                    rsqrt_mean("q", QR, 1)
                    for c in range(4):
                        rows = slice(0, P) if c < 3 else slice(64, P)
                        ins = stt(lat[rows, 4 + c, :], lat[rows, 4 + c, :], pcol("gq", c, rows), rstd[rows, :], ALU.mult, ALU.mult)
                    ins.then_inc(lat_normed, 1)
                    dve.wait_ge(lat_normed, 2)
                if n == 3:
                    for part in range(2):
                        dve.wait_ge(lat_hi_ready, part + 1)
                        tt_(lat_lo[:, 4 * part:4 * part + 4, :], lat[:, 4 * part:4 * part + 4, :],
                            whole(lat_hi[:, 4 * part:4 * part + 4, :]), ALU.subtract).then_inc(lat_lo_ready, 1)
                if i == 0:
                    unit_at(47, 1, b)
                if n == 5:
                    dve.wait_ge(kr_rot, 1)
                    tt_(rt[0], px[1][0:ROPE, 0:T], sin, ALU.mult)
                    chain.link(tt_(kro, lat[0:ROPE, 7, :], cos, ALU.mult))
                    tt_(kro, kro, rt[0], ALU.add).then_inc(kr_ready, 1)
            with dve.Fori(0, MH // BODY) as i:
                chain.enter(i, 4 * 4)
                for st, j in waves(BODY, 6):
                    hn = i * BODY + j
                    A, B = [pm[0], pm[1], ps, pv][j], px[j]
                    if st == 0:
                        split("heads", i, j)
                    elif st == 1:
                        dve.wait_ge(m_rot, hn + 1)
                        tt_(rt[j], B[0:ROPE, 0:T], sin, ALU.mult)
                        chain.link(tt_(qr[j], qr[j], cos, ALU.mult))
                        tt_(qr[j], qr[j], rt[j], ALU.add).then_inc(m_rope, 1)
                    elif st == 2:
                        dve.wait_ge(m_scores, hn + 1)
                        chain.link(stt(pr[j], A[:, 0:3 * P], SCALE_M, mask_m, ALU.mult, ALU.add))
                        dve.tensor_reduce(small_m[:, j, 0, 0:1], pr[j][:, 0:P], AX.X, ALU.max)
                        chain.link(dve.tensor_reduce(small_m[:, j, 0, 1:2], pr[j][:, P:3 * P], AX.X, ALU.max))
                        ts_(small_m[:, j, 1, :], small_m[:, j, 0, :], -1.0, None, ALU.mult).then_inc(m_negmax, 1)
                        dve.wait_ge(m_exp, hn + 1)
                        chain.link(dve.reciprocal(small_m[:, j, 3, :], small_m[:, j, 2, :]))
                        for lo, tt in ((0, 0), (P, 1)):
                            keys = P * (tt + 1)
                            ins = ts_(pr[j][:, lo:lo + keys], pr[j][:, lo:lo + keys], small_m[:, j, 3, tt:tt + 1], None, ALU.mult)
                        ins.then_inc(m_probs, 1)
                    elif st == 4:
                        dve.wait_ge(m_num, hn + 1)
                        zc = one(zo, hn)
                        tt_(zc, zc, A[:, 0:T], ALU.mult).then_inc(head_free[j], 1)
                    elif st == 5:
                        dve.wait_ge(m_hi, hn + 1)
                        tt_(one(h_lo, hn), one(zo, hn), whole(one(h_hi, hn)), ALU.subtract).then_inc(o_ready, 1)
                chain.leave(MH // BODY)
            clear_squares()
            for n in range(NBLOCKS["mla_out"]):
                split("mla_out", n // BODY, n % BODY)
                add_squares("post1", n // BODY, n % BODY)
            post("post1", 1, G1, y1, BBASE["mla_out"] // 2 + NBLOCKS["mla_out"] // 2)


def constants():
    f = np.float32
    t = np.arange(T)
    mask_a = np.zeros((P, 2, TT, T), f)
    for sc in range(TT):
        s = (np.arange(P) + sc * P)[:, None]
        mask_a[:, 0, sc] = np.where(t[None] >= s, 0.0, NEG)
        mask_a[:, 1, sc] = np.where(t[None] <= s, 0.0, NEG)
    c = np.arange(GRID_W)
    lo = np.clip(c - WIN_COLS // 2, 0, GRID_W - WIN_COLS)[:, None]
    win = np.where((c[None] >= lo) & (c[None] < lo + WIN_COLS), 0.0, NEG).astype(f)
    cst = np.zeros((P, 1024), f)
    inv = (f(10000.0) ** (-np.arange(0, ROPE, 2, dtype=f) / f(ROPE))).astype(f)
    ang = (t.astype(f)[:, None] * inv[None, :]).astype(f)
    cst[0:64, 0:256] = np.concatenate([np.cos(ang), np.cos(ang)], axis=1).T
    cst[0:64, 256:512] = np.concatenate([np.sin(ang), np.sin(ang)], axis=1).T
    q = np.arange(P)[:, None]
    cst[:, 512:640] = np.where(t[None, :P] // 64 <= q // 64, 0.0, NEG)
    cst[:, 640:896] = np.where(t[None] // 64 <= (q + P) // 64, 0.0, NEG)
    half = ROPE // 2
    for m in range(half):
        cst[m + half, 896 + m] = -1.0
        cst[m, 896 + m + half] = 1.0
    return {"ident": np.eye(P, dtype=f), "mask_a": mask_a.reshape(P, -1), "wmask": np.concatenate([win, win]), "mla_cst": cst}


def blocks(w, k=PKC):
    kk, n = w.shape
    w = w.reshape(kk // (P * k), k, P, n // COLS, COLS).transpose(3, 0, 2, 1, 4)
    return np.ascontiguousarray(w).reshape(-1, P, k * COLS)


def columns_of(v):
    return np.asarray(v).reshape(-1, P).T


def lay_out(i):
    i = {n: np.asarray(v) for n, v in i.items()}
    f = np.float32
    d = constants()
    d["x"] = np.ascontiguousarray(i["x"][0].T.reshape(KC, P, T).transpose(1, 0, 2)).reshape(P, -1)
    par = np.zeros((P, NPAR), f)

    def put(name, cols, c=0):
        par[:cols.shape[0], PCOL[name] + c:PCOL[name] + c + cols.shape[1]] = cols

    put("c", columns_of(i["c"][0]))
    put("c2", columns_of(i["c_2"][0]))
    put("bias", columns_of(i["b_ada"][0]))
    put("bias", columns_of(i["ada_b_2"].reshape(-1)), 6 * KC)
    put("g1", columns_of(i["g_norm1"][0]))
    put("ghead", columns_of(i["g_head_a"][0]))
    put("g2", columns_of(i["g_norm2"][0]))
    conv = np.concatenate([i["conv_w"][0], i["conv_b"]], axis=0).reshape(4, FC, P).transpose(2, 1, 0)
    put("conv", conv.reshape(P, -1))
    put("gfinal", columns_of(i["g_final"]))
    put("pre", columns_of(i["pre_g_2"].reshape(-1)))
    put("post", columns_of(i["post_g_2"].reshape(-1)))
    put("gsgu", columns_of(i["sgu_norm_g_2"][0]))
    gq = i["mla_q_norm_g_2"][0]
    put("gq", columns_of(np.concatenate([gq[:384], np.zeros(64, f), gq[384:]])))
    put("gkv", columns_of(i["mla_kv_norm_g_2"][0]))

    def gate_rows(v, first):
        out = np.zeros(v.shape[:-1] + (GROW,), f)
        out[..., 0:NH_A] = v[..., first * NH_A:(first + 1) * NH_A]
        out[..., 32:GROW] = v[..., (first + 2) * NH_A:(first + 3) * NH_A]
        return out

    put("bi", gate_rows(i["b_gates"][0], 0)[:, None])
    put("bf", gate_rows(i["b_gates"][0], 1)[:, None])
    d["par"] = par

    w = i["w_in"][0]
    q_a, k_a, v_a, o_a = (w[:, n * 1024:(n + 1) * 1024] for n in range(4))
    gw = w[:, 4096:4112]
    q_b, k_b, v_b = (w[:, 4112 + n * 1024:4112 + (n + 1) * 1024] for n in range(3))
    gate_w = np.zeros((P, 2, GPAD), f)
    for g in range(2):
        gate_w[:, g, :KC * GROW] = gate_rows(gw, g).reshape(KC, P, GROW).transpose(1, 0, 2).reshape(P, -1)
    d["gate_w"] = gate_w.reshape(P, -1)
    d["w_in"] = blocks(np.concatenate([k_a, q_a, v_a, o_a, q_b, k_b, v_b], axis=1))
    d["w_out"] = blocks(i["w_out"][0])
    up = i["w_up"][0]
    u, g = up[:, :D_FF].reshape(D, FC, 1, P), up[:, D_FF:].reshape(D, FC, 1, P)
    up = np.concatenate([g, u], axis=2)
    for half in range(2):
        d[f"w_up{half}"] = blocks(up[:, half * FH:(half + 1) * FH].reshape(D, -1))
        d[f"w_down{half}"] = blocks(i["w_down"][0][half * FH * P:(half + 1) * FH * P], FH)

    rpb = i["rpb"][0]
    c = np.arange(GRID_W)
    dc = np.clip(c[None] - c[:, None] + WIN_COLS - 1, 0, 2 * WIN_COLS - 2)
    rows = []
    for half in range(2):
        dr = np.arange(6) + 5 - half
        rows.append(rpb[:, dr][:, :, dc].transpose(2, 0, 1, 3).reshape(GRID_W, -1))
    d["bias_b"] = np.concatenate(rows)

    ada = np.concatenate([i["w_ada"][0], i["ada_w_2"][0], i["ada_w_2"][1]], axis=1)
    ada = ada.reshape(APIECES, KC // APIECES, P, 12 * UNITS, UCOLS).transpose(3, 0, 2, 1, 4)
    d["ada"] = np.ascontiguousarray(ada).reshape(-1, P, APIECE)

    w = i["sgu_w_in_2"][0]
    d["sgu_u"], d["sgu_v"], d["sgu_z"] = (blocks(w[:, n * SGU_W:(n + 1) * SGU_W]) for n in range(3))
    ws = i["sgu_w_s_2"][0].transpose(0, 2, 1)
    bs = np.broadcast_to(i["sgu_b_s_2"][0][:, None, :], (GROUPS, P, P))
    d["mix"] = np.ascontiguousarray(np.stack([ws, bs], axis=2).reshape(GROUPS // 2, 2, P, 2, P).transpose(0, 2, 1, 3, 4)).reshape(GROUPS // 2, P, -1)
    d["sgu_out"] = blocks(i["sgu_w_out_2"][0])

    w = i["mla_w_in_2"][0]
    cq, ckv, kr, z = w[:, :QR], w[:, QR:QR + KVR], w[:, QR + KVR:QR + KVR + ROPE], w[:, QR + KVR + ROPE:]
    d["lat"] = blocks(np.concatenate([ckv, cq[:, :384], kr, cq[:, 384:]], axis=1))
    d["mla_z"] = blocks(z)
    uq = i["mla_w_uq_2"][0]
    uq = np.concatenate([uq[:384], np.zeros((64, uq.shape[1]), f), uq[384:]])
    head = np.concatenate([uq.reshape(512, MH, 192), i["mla_w_ukv_2"][0].reshape(512, MH, 256)], axis=2)
    heads = np.zeros((MH, P, 2, QUARTER), f)
    heads[..., :2 * HEADW] = head.reshape(2, 2, P, MH, HEADW).transpose(3, 2, 0, 1, 4).reshape(MH, P, 2, -1)
    d["heads"] = heads.reshape(MH, P, -1)
    d["mla_out"] = blocks(i["mla_w_out_2"][0])
    return {n: np.ascontiguousarray(v, dtype=f) for n, v in d.items()}


def kernel(**inputs):
    import concourse.bacc as bacc
    from concourse.bass_utils import run_bass_kernel_spmd as run

    nc = bacc.Bacc("TRN2", target_bir_lowering=False, num_devices=1)
    arrays = {f"in_{n}": v for n, v in lay_out(inputs).items()}
    args = {n[3:]: nc.dram_tensor(n, v.shape, F32, kind="ExternalInput").ap() for n, v in arrays.items()}
    args["out"] = nc.dram_tensor("out_x", (P, KC * T), F32, kind="ExternalOutput").ap()
    build(nc, args)
    got = run(nc, [arrays], core_ids=[0]).results[0]["out_x"]
    return np.ascontiguousarray(got.reshape(P, KC, T).transpose(2, 1, 0)).reshape(1, T, D)
```

```python
from contextlib import ExitStack

import concourse.bass as bass
import numpy as np
from concourse import mybir

F32 = mybir.dt.float32
F32R = mybir.dt.float32r
ALU = mybir.AluOpType
ACT = mybir.ActivationFunctionType
AX = mybir.AxisListType

P = 128
D = 2048
KC = D // P
T = 256
TT = T // P
COLS = 256
PKC = 8
PIECE = PKC * COLS
QUARTER = PIECE // 2
SLOTS = 4
AHEAD = 3
BODY = 4
EPS = 1e-6
NEG = -1e30

NH_A, DH_A = 4, 256
NH_B, DH_B = 8, 128
GRID_W, WIN_COLS = 64, 16
D_FF = 5632
FC = D_FF // P
FH = FC // 2
SGU_W = 4096
SC = SGU_W // P
GROUPS = 16
MH, NOPE, ROPE, VD = 16, 128, 64, 128
QR, KVR = 448, 512
HEADW = NOPE + ROPE + NOPE + VD
SCALE_A = DH_A ** -0.5
SCALE_B = DH_B ** -0.5
SCALE_M = (NOPE + ROPE) ** -0.5
GROW = 36
GPAD = KC * GROW + P - GROW

STAGES = [("w_in", 28, [4] * 4), ("w_out", 8, [4] * 4), ("w_up0", FH, [4] * 4), ("w_down0", 8, [4] * 5 + [2]),
          ("w_up1", FH, [4] * 4), ("w_down1", 8, [4] * 5 + [2]), ("sgu_v", 16, [4] * 4), ("sgu_u", 16, [4] * 4),
          ("sgu_z", 16, [4] * 4), ("sgu_out", 8, [4] * 8), ("lat", 4, [4] * 4), ("mla_z", 8, [4] * 4),
          ("heads", MH, [2] * 2), ("mla_out", 8, [4] * 4)]
NBLOCKS = {n: b for n, b, _ in STAGES}
QUARTERS = {n: q for n, _, q in STAGES}
QBASE, BBASE, _q, _b = {}, {}, 0, 0
for _name, _blocks, _qs in STAGES:
    QBASE[_name], BBASE[_name] = _q, _b
    _q += _blocks * len(_qs)
    _b += _blocks if _name != "heads" else 0
    assert _q % (2 * SLOTS) == 0 and _b % 2 == 0
LAST = STAGES[-1][0]

SH1, SC1, GA1, SH2, SC2, GA2, S0, C0, G0, S1, C1, G1 = range(12)
UNITS = 4
UCOLS = D // UNITS
APIECES = 8
APIECE = D // P // APIECES * UCOLS
FIRST_UNITS = 2 * UNITS
BODY_PIECES = [3, 3, 2, 0]
W_IN_PIECES = [3, 3, 2] * 4 + [2] * 8 + [4] * 8
UNIT_OF = {"w_out": 18, "w_up0": 20, "w_down0": 25, "w_up1": 27, "sgu_v": 32, "sgu_u": 36, "sgu_z": 40, "sgu_out": 44,
           "lat": 46, "mla_z": 47}

PCOL, _n = {}, 0
for _name, _cols in [("c", KC), ("c2", KC), ("bias", 12 * KC), ("g1", KC), ("ghead", 8), ("g2", KC),
                     ("conv", FC * 4), ("gfinal", KC), ("pre", 2 * KC), ("post", 2 * KC), ("gsgu", SC),
                     ("gq", 4), ("gkv", 4), ("bi", 1), ("bf", 1)]:
    PCOL[_name] = _n
    _n += _cols
NPAR = _n

PAIRS = KC // 2
NORMS = ["norm1", "norm2", "final", "post0", "post1"]
ADDED = {n: PAIRS * (i + 1) for i, n in enumerate(NORMS)}
SUMS = {n: i + 1 for i, n in enumerate(["norm1", "norm2", "final", "finalg", "post0", "pre1", "kv", "q", "post1"])}
H_NORMS = ["norm1", "norm2", "pre0", "pre1"]

W_IN_STEPS = {11 + 3 * k + s: (step, k) for k in range(NH_A) for s, step in enumerate(("scores", "mix", "norm"))}


def waves(jobs, stages):
    return [(s, w - s) for w in range(jobs + stages - 1) for s in range(stages) if 0 <= w - s < jobs]


def head_stages(i, j):
    return [(s, i * BODY + (j - s), (j - s) % BODY) for s in (4, 3, 2, 1, 0)
            if not isinstance(i, int) or 0 <= i * BODY + j - s < MH]


class Chain:

    def __init__(self, eng, sem):
        self.eng, self.sem, self.count, self.i, self.per = eng, sem, 0, None, 0

    def link(self, ins):
        ins.then_inc(self.sem, 1)
        self.count += 1
        self.eng.wait_ge(self.sem, self.count if self.i is None else self.i * self.per + self.count)

    def enter(self, i, per):
        self.i, self.per, self.start = i, per, self.count

    def leave(self, trips):
        assert self.count - self.start == self.per, (self.count - self.start, self.per)
        self.count = self.start + trips * self.per
        self.i = None


def build(nc, a):
    with ExitStack() as ctx:
        base = (nc.sbuf_base + 63) // 64 * 64
        cursor = [0]

        def at_(name, shape, offset, dt=F32):
            assert base + 4 * (offset + int(np.prod(shape[1:]))) <= nc.sbuf_usable_end, name
            return nc.alloc_sbuf_tensor_at(name, shape, dt, offset=base + 4 * offset)

        def sb(name, shape, dt=F32):
            o = cursor[0]
            cursor[0] += (int(np.prod(shape[1:])) + 7) // 8 * 8
            return at_(name, shape, o, dt)

        def sem(name):
            return ctx.enter_context(nc.semaphore(name))

        x = sb("x", [P, KC, T])
        o_h = cursor[0]
        h_hi = sb("h_hi", [P, KC, T], F32R)
        h_lo = sb("h_lo", [P, KC, T], F32R)
        raw = sb("raw", [P, SLOTS, PIECE])
        w_hi = sb("w_hi", [P, SLOTS, QUARTER], F32R)
        w_lo = sb("w_lo", [P, SLOTS, QUARTER], F32R)
        ada = sb("ada", [P, SLOTS, APIECE])
        acc = sb("acc", [P, UCOLS])
        par = sb("par", [P, NPAR])
        mods = sb("mods", [P, 12 * KC])
        csil = sb("csil", [P, 2, KC])
        gain = sb("gain", [P, 5, KC])
        ident = sb("ident", [P, P])
        ones = sb("ones", [P, P])
        rstd = sb("rstd", [P, T])
        o_ssq = cursor[0]
        ssq = sb("ssq", [P, 2, T])
        sqt = sb("sqt", [P, 2, T])
        o_nt = cursor[0]
        nt = sb("nt", [P, 4, T])
        stat = sb("stat", [P, 2, 32])
        small_b = sb("small_b", [P, 2, 4, 2])
        small_m = sb("small_m", [P, 4, 4, 2])
        o_work = cursor[0]

        def work(name, shape, offset, dt=F32):
            return at_(name, shape, o_work + offset, dt)

        e1 = work("e1", [P, SLOTS, APIECE], 0)
        acc_first = work("acc_first", [P, 2, 2, UCOLS], 13968)
        ka = work("ka", [P, 8, T], 0)
        qa = work("qa", [P, 8, T], 2048)
        va = work("va", [P, TT, 1024], 4096)
        oa = work("oa", [P, 8, T], 6144)
        gw_lo = work("gw_lo", [P, 2, GPAD], 4096, F32R)
        gw_hi = work("gw_hi", [P, 2, GPAD], 6144, F32R)
        gates = work("gates", [P, 8, T], 8192)
        qb = work("qb", [P, 8, T], 8192)
        kb = work("kb", [P, 8, T], 0)
        vb = work("vb", [P, TT, 1024], 2048)
        mask_a = work("mask_a", [P, 2, 512], 10240)
        gw = work("gw", [P, 2, GPAD], 11264)
        bias_b = work("bias_b", [P, NH_B * 6, GRID_W], 10240)
        neg_rows = work("neg_rows", [P, 2 * T], 13312)
        bcol = work("bcol", [P, TT, GROW], 13824)
        wmask = work("wmask", [P, GRID_W], 13904)
        decay = work("decay", [P, 2, 2 * T], 13968)
        expm = work("expm", [P, 2, T], 14992)
        hf = work("hf", [P, 2, T], 15504)
        hb = sqt
        s_b = [decay[:, j, :].rearrange("p (a b) -> p a b", a=TT) for j in range(2)]
        pt_b = [expm, hf]
        glu_hi = work("glu_hi", [P, FH, T], 0, F32R)
        glu_lo = work("glu_lo", [P, FH, T], FH * T, F32R)
        gpad = work("gpad", [P, T + 2], 2 * FH * T)
        conv = work("conv", [P, T], 2 * FH * T + 264)
        ssqg = work("ssqg", [P, 2, T], 12288)
        sqtg = work("sqtg", [P, 2, T], 12800)
        v_sgu = work("v_sgu", [P, TT, SGU_W], 0)
        gu = work("gu", [P, SC, T], 2 * SGU_W)
        y_hi = work("y_hi", [P, SC, T], 0, F32R)
        y_lo = work("y_lo", [P, SC, T], 2 * SGU_W, F32R)
        stmp = at_("stmp", [P, 2, 2 * T], o_ssq)
        mixw = at_("mixw", [P, 2, 2, 2, P], o_nt)
        ztmp = at_("ztmp", [P, 2, 2 * T], o_nt)
        rs1 = at_("rs1", [P, T], o_ssq)
        pre_bufs = [nt[:, 0:2, :], nt[:, 2:4, :], ssq[:, :, :], sqt[:, :, :]]
        y0 = at_("y0", [P, KC, T], o_h)
        lat = work("lat", [P, 8, T], 0)
        lat_hi = work("lat_hi", [P, 8, T], 2048, F32R)
        lat_lo = work("lat_lo", [P, 8, T], 4096, F32R)
        lsq = work("lsq", [P, 8, T], 6144)
        zo = work("zo", [P, MH, T], 8192)
        y1 = work("y1", [P, KC, T], 8192)
        cst = work("cst", [P, 1024], 12288)
        cos, sin, mask_m, rot = cst[0:ROPE, 0:256], cst[0:ROPE, 256:512], cst[:, 512:896], cst[0:ROPE, 896:1024]
        kro = work("kro", [P, T], 13312)[0:ROPE, :]
        hd = [work(f"hd{j}", [P, 1408], o) for j, o in enumerate((0, 6144, 13568, 14976))]
        qn = [b[:, 0:256] for b in hd]
        qr = [b[0:ROPE, 256:512] for b in hd]
        kv = [b[:, 512:1024] for b in hd]
        pr = [b[:, 1024:1408] for b in hd]
        pt = [work(f"pt{j}", [P, 384], o) for j, o in enumerate((1408, 7552))] + \
             [at_(f"pt{j}", [P, 384], o_nt + 384 * (j - 2)) for j in (2, 3)]
        rt = [at_(f"rt{j}", [P, T], o_ssq + j * T)[0:ROPE, :] for j in range(4)]

        pm = [ctx.enter_context(nc.psum_tensor(f"pm{b}", [P, 512], F32)) for b in range(2)]
        px = [ctx.enter_context(nc.psum_tensor(f"px{b}", [P, 512], F32)) for b in range(4)]
        pv = ctx.enter_context(nc.psum_tensor("pv", [P, 512], F32))
        ps = ctx.enter_context(nc.psum_tensor("ps", [P, 512], F32))

        const_in = sem("const_in")
        x_in = sem("x_in")
        mix_const_in = sem("mix_const_in")
        wmask_in = sem("wmask_in")
        bias_in = sem("bias_in")
        mla_const_in = sem("mla_const_in")
        hi_ready = sem("hi_ready")
        lo_even = sem("lo_even")
        lo_odd = sem("lo_odd")
        quarter_done = sem("quarter_done")
        ada_used = sem("ada_used")
        first_even = sem("first_even")
        unit_summed = sem("unit_summed")
        unit_taken = sem("unit_taken")
        silu_c = sem("silu_c")
        ones_set = sem("ones_set")
        sq_ready = sem("sq_ready")
        sq_added = sem("sq_added")
        pre_sq = sem("pre_sq")
        pre_summed = sem("pre_summed")
        ss_ready = sem("ss_ready")
        ms_ready = sem("ms_ready")
        std_ready = sem("std_ready")
        rstd_ready = sem("rstd_ready")
        xn_ready = sem("xn_ready")
        hh_ready = sem("hh_ready")
        h_ready = sem("h_ready")
        y_scaled = sem("y_scaled")
        x_ready = sem("x_ready")
        x_pool = sem("x_pool")
        dve_step = sem("dve_step")
        act_step = sem("act_step")
        gw_hi_ready = sem("gw_hi_ready")
        gw_lo_ready = sem("gw_lo_ready")
        gate_ps = sem("gate_ps")
        gate_rows = sem("gate_rows")
        gate_exp = sem("gate_exp")
        rows_ready = sem("rows_ready")
        bcol_ps = sem("bcol_ps")
        bcol_ready = sem("bcol_ready")
        a_scores = sem("a_scores")
        a_arg = sem("a_arg")
        a_exp = sem("a_exp")
        a_probs = sem("a_probs")
        a_num = sem("a_num")
        a_sq = sem("a_sq")
        a_ss = sem("a_ss")
        a_ms = sem("a_ms")
        a_std = sem("a_std")
        a_out = sem("a_out")
        oa_hi = sem("oa_hi")
        mix_ready = sem("mix_ready")
        b_scores = sem("b_scores")
        b_negmax = sem("b_negmax")
        b_exp = sem("b_exp")
        b_probs = sem("b_probs")
        b_pt = sem("b_pt")
        b_ptsb = sem("b_ptsb")
        b_num = sem("b_num")
        b_hi = sem("b_hi")
        g_copied = sem("g_copied")
        conv_ready = sem("conv_ready")
        gelu_ready = sem("gelu_ready")
        glu_ready = sem("glu_ready")
        glu_hi_ready = sem("glu_hi_ready")
        glu_lo_ready = sem("glu_lo_ready")
        sqg_ready = sem("sqg_ready")
        sqg_added = sem("sqg_added")
        v_mean = sem("v_mean")
        v_sq = sem("v_sq")
        v_var = sem("v_var")
        v_std = sem("v_std")
        v_normed = sem("v_normed")
        vm_ready = sem("vm_ready")
        vm_taken = sem("vm_taken")
        z_silu = sem("z_silu")
        y_ready = sem("y_ready")
        y_hi_ready = sem("y_hi_ready")
        y_lo_ready = sem("y_lo_ready")
        lat_sq = sem("lat_sq")
        lat_normed = sem("lat_normed")
        lat_hi_ready = sem("lat_hi_ready")
        lat_lo_ready = sem("lat_lo_ready")
        kr_rot = sem("kr_rot")
        kr_ready = sem("kr_ready")
        m_proj = sem("m_proj")
        m_rot = sem("m_rot")
        m_rope = sem("m_rope")
        m_scores = sem("m_scores")
        m_negmax = sem("m_negmax")
        m_exp = sem("m_exp")
        m_probs = sem("m_probs")
        m_pt = sem("m_pt")
        m_ptsb = sem("m_ptsb")
        m_num = sem("m_num")
        m_gated = sem("m_gated")
        m_hi = sem("m_hi")
        o_ready = sem("o_ready")
        out_done = sem("out_done")
        slot_full = [sem(f"slot_full{s}") for s in range(SLOTS)]
        ada_full = [sem(f"ada_full{s}") for s in range(2 * SLOTS)]
        mixw_full = [sem(f"mixw_full{s}") for s in range(2)]
        bank_free = [sem(f"bank_free{b}") for b in range(2)]
        head_free = [sem(f"head_free{j}") for j in range(4)]

        def flat(ap):
            return ap.rearrange("p a b -> p (a b)")

        def pcol(name, c, rows=slice(0, P)):
            c = c + PCOL[name]
            return par[rows, c:c + 1] if isinstance(c, int) else par[rows, bass.ds(c, 1)]

        def pcols(name, n, c=0):
            return par[:, PCOL[name] + c:PCOL[name] + c + n]

        def mod(v, c):
            c = c + v * KC
            return mods[:, c:c + 1] if isinstance(c, int) else mods[:, bass.ds(c, 1)]

        def at(ap, i, n=1):
            return ap[:, i:i + n, :] if isinstance(i, int) else ap[:, bass.ds(i, n), :]

        def one(ap, i):
            return at(ap, i).rearrange("p a b -> p (a b)")

        def chunk(ap):
            return lambda c: ap[:, c, :]

        def over(ap, n):
            return ap.unsqueeze(1).to_broadcast([ap.shape[0], n, ap.shape[1]])

        def halves(ap, n=2):
            return ap.rearrange("p (a b) -> p a b", a=n)

        def whole(ap):
            return ap.bitcast(F32)

        def quarter(stage, i, k):
            return i * (BODY * len(QUARTERS[stage])) + (QBASE[stage] + k)

        def pairs(stage, i, k):
            return i * (BODY * len(QUARTERS[stage]) // 2) + ((QBASE[stage] + k) // 2 + 1)

        def done(stage, i, b):
            return quarter(stage, i, (b + 1) * len(QUARTERS[stage]))

        def taken(stage, i, b):
            return i * (BODY // 2) + ((BBASE[stage] + b) // 2 + 1)

        def ahead(stage, i, b):
            n = len(QUARTERS[stage])
            ks = range(b * n + AHEAD, (b + 1) * n + AHEAD)
            return [k for k in ks if stage != LAST or i * BODY * n + k < NBLOCKS[stage] * n]

        def elems(stage, k):
            return QUARTER if stage == "heads" else QUARTERS[stage][k % len(QUARTERS[stage])] * COLS

        def raw_part(stage, k):
            lo = k % 2 * QUARTER
            return raw[:, k // 2 % SLOTS, lo:lo + elems(stage, k)]

        def row(ap, n):
            return ap[n] if isinstance(n, int) else ap[bass.ds(n, 1)].rearrange("o p n -> (o p) n")

        def body_pieces(b):
            lo = sum(BODY_PIECES[:b])
            return range(lo, lo + BODY_PIECES[b])

        def w_in_pieces(n):
            lo = sum(W_IN_PIECES[:n])
            return FIRST_UNITS + lo // APIECES, range(lo % APIECES, lo % APIECES + W_IN_PIECES[n])

        def w_in_complete(n):
            hi = sum(W_IN_PIECES[:n + 1])
            return FIRST_UNITS + hi // APIECES - 1 if n >= 0 and hi % APIECES == 0 else None

        block = ctx.enter_context(nc.Block())

        @block.sync
        def _(sp):
            sp.dma_start(par[:, :], a["par"]).then_inc(const_in, 16)
            sp.dma_start(ident[:, :], a["ident"]).then_inc(const_in, 16)
            sp.dma_start(flat(x[:, :, :]), a["x"]).then_inc(x_in, 16)
            sp.dma_start(flat(gw[:, :, :]), a["gate_w"]).then_inc(mix_const_in, 16)
            sp.dma_start(flat(mask_a[:, :, :]), a["mask_a"]).then_inc(mix_const_in, 16)
            sp.dma_start(wmask[:, :], a["wmask"]).then_inc(wmask_in, 16)

            def first_unit_piece(u, k):
                buf = ada[:, k, :] if k < SLOTS else e1[:, k - SLOTS, :]
                sp.dma_start(buf, row(a["ada"], u * APIECES + k)).then_inc(ada_full[k], 16)

            for k in range(APIECES):
                first_unit_piece(0, k)
            with sp.Fori(1, FIRST_UNITS) as u:
                for k in range(APIECES):
                    sp.wait_ge(ada_used, u * APIECES + (k + 1 - APIECES))
                    first_unit_piece(u, k)

            def load(stage, i, j):
                if not (isinstance(i, int) and QBASE[stage] + i + j // SLOTS == 0):
                    sp.wait_ge(lo_even, pairs(stage, i, 2 * j) - SLOTS)
                    sp.wait_ge(lo_odd, pairs(stage, i, 2 * j) - SLOTS)
                n = len(QUARTERS[stage]) // 2
                if stage in ("w_down0", "w_down1"):
                    blk, part = i * BODY + j // n, j % n
                    size = elems(stage, 2 * part) + elems(stage, 2 * part + 1)
                    src = row(a[stage][:, :, part * PIECE:part * PIECE + size], blk)
                else:
                    size, src = PIECE, row(a[stage], i * (BODY * n) + j)
                sp.dma_start(raw[:, j % SLOTS, 0:size], src).then_inc(slot_full[j % SLOTS], 16)

            for stage, blocks_, qs in STAGES:
                per = BODY * len(qs) // 2
                first = 0
                if stage == "w_in":
                    for j in range(per):
                        load(stage, 0, j)
                    first = 1
                if blocks_ // BODY > first:
                    with sp.Fori(first, blocks_ // BODY) as i:
                        for j in range(per):
                            load(stage, i, j)
                for j in range(blocks_ % BODY * len(qs) // 2):
                    load(stage, blocks_ // BODY, j)
            for g in range(4):
                sp.wait_ge(x_ready, 4 + g + 1)
                sp.wait_ge(x_pool, 4 + g + 1)
                sp.dma_start(a["out"][:, 4 * g * T:4 * (g + 1) * T], flat(x[:, 4 * g:4 * g + 4, :])).then_inc(out_done, 16)
            sp.wait_ge(out_done, 4 * 16)

        @block.gpsimd
        def _(pool):
            def split(stage, i, k):
                if k % 2:
                    pool.wait_ge(hi_ready, quarter(stage, i, k) + 1)
                    n = elems(stage, k)
                    pool.tensor_tensor(w_lo[:, k % SLOTS, 0:n], raw_part(stage, k), whole(w_hi[:, k % SLOTS, 0:n]),
                                       ALU.subtract).then_inc(lo_odd, 1)

            for k in range(AHEAD):
                split("w_in", 0, k)
            for stage, blocks_, qs in STAGES:
                trips = blocks_ // BODY - (stage == LAST)
                with pool.Fori(0, trips) as i:
                    for b in range(BODY):
                        for k in ahead(stage, i if stage != LAST else 0, b):
                            split(stage, i, k)
                for b in range(blocks_ - trips * BODY):
                    for k in ahead(stage, trips, b):
                        split(stage, trips, k)
                if stage in ("sgu_out", LAST):
                    y, first = (y1, 4) if stage == LAST else (y0, 0)
                    for g in range(4):
                        pool.wait_ge(y_scaled, first + g + 1)
                        c = slice(4 * g + 2, 4 * g + 4)
                        pool.tensor_tensor(x[:, c, :], x[:, c, :], y[:, c, :], ALU.add).then_inc(x_pool, 1)

        @block.tensor
        def _(pe):
            def columns(stage, i, b, hi, lo, need=None, late=None):
                if not (isinstance(i, int) and taken(stage, i, b) == 1):
                    pe.wait_ge(bank_free[b % 2], taken(stage, i, b) - 1)
                qs, c = QUARTERS[stage], 0
                for q, n in enumerate(qs):
                    k = b * len(qs) + q
                    if need is not None:
                        need(q)
                    if late is not None and q == len(qs) // 2:
                        late()
                    pe.wait_ge(lo_odd if k % 2 else lo_even, pairs(stage, i, k))
                    wh = halves(w_hi[:, k % SLOTS, 0:n * COLS], n)
                    wl = halves(w_lo[:, k % SLOTS, 0:n * COLS], n)
                    for kc in range(n):
                        for j in range(2):
                            dst, cols = pm[b % 2][:, j * T:(j + 1) * T], slice(j * P, (j + 1) * P)
                            pe.matmul(dst, wh[:, kc, cols], hi(c + kc), start=(c + kc + j == 0), stop=False, skip_group_check=True)
                            pe.matmul(dst, wh[:, kc, cols], lo(c + kc), start=False, stop=False, skip_group_check=True)
                            mm = pe.matmul(dst, wl[:, kc, cols], hi(c + kc), start=False,
                                           stop=(q == len(qs) - 1 and kc == n - 1), skip_group_check=True)
                    mm.then_inc(quarter_done, 1)
                    c += n

            def tokens(stage, i, b, need=None, late=None):
                if not (isinstance(i, int) and taken(stage, i, b) == 1):
                    pe.wait_ge(bank_free[b % 2], taken(stage, i, b) - 1)
                for q in range(4):
                    k = b * 4 + q
                    if need is not None:
                        need(q)
                    if late is not None and q == 2:
                        late()
                    pe.wait_ge(lo_odd if k % 2 else lo_even, pairs(stage, i, k))
                    wh, wl = (halves(w[:, k % SLOTS, :], 4) for w in (w_hi, w_lo))
                    for kc in range(4):
                        for tt in range(TT):
                            dst, c, ts = pm[b % 2][:, tt * COLS:(tt + 1) * COLS], 4 * q + kc, slice(tt * P, (tt + 1) * P)
                            pe.matmul(dst, h_hi[:, c, ts], wh[:, kc, :], start=(c + tt == 0), stop=False, skip_group_check=True)
                            pe.matmul(dst, h_hi[:, c, ts], wl[:, kc, :], start=False, stop=False, skip_group_check=True)
                            mm = pe.matmul(dst, h_lo[:, c, ts], wh[:, kc, :], start=False, stop=(c == KC - 1), skip_group_check=True)
                    mm.then_inc(quarter_done, 1)

            def sum_unit(u):
                pe.wait_ge(ada_used, u * APIECES + APIECES)
                pe.wait_ge(unit_taken, u)
                for c in range(UCOLS // P):
                    mm = pe.matmul(pv[:, c:c + 1], acc[:, c * P:(c + 1) * P], ones[:, 0:1], start=True, stop=True)
                mm.then_inc(unit_summed, 1)

            def sum_first(u, first=False):
                n = u if first else u[0] * 2 + u[1]
                par_ = 0 if first else u[1]
                pe.wait_ge(ada_used, n * APIECES + APIECES)
                if not first:
                    pe.wait_ge(unit_taken, n)
                for c in range(UCOLS // P):
                    for r in range(2):
                        mm = pe.matmul(pv[:, c:c + 1], acc_first[:, par_, r, c * P:(c + 1) * P], ones[:, 0:1], start=(r == 0), stop=(r == 1))
                mm.then_inc(unit_summed, 1)

            def sum_squares(name, src=ssq, half=0):
                pe.wait_ge(sq_added if src is ssq else sqg_added, ADDED[name] if src is ssq else PAIRS)
                if SUMS[name] - half > 1:
                    pe.wait_ge(ms_ready, SUMS[name] - half - 1)
                for j in range(2):
                    mm = pe.matmul(ps[:, half * T:(half + 1) * T], ones[:, :], src[:, j, :], start=(j == 0), stop=(j == 1))
                mm.then_inc(ss_ready, 1)

            def h_needed(norm):
                return lambda q: pe.wait_ge(h_ready, H_NORMS.index(norm) * KC + 4 * (q + 1))

            def stage_columns(stage, need=None, hi=None):
                with pe.Fori(0, hi or NBLOCKS[stage] // BODY) as i:
                    for b in range(BODY):
                        late = (lambda: sum_unit(i + UNIT_OF[stage])) if b == BODY - 1 and stage in UNIT_OF else None
                        columns(stage, i, b, chunk(h_hi), chunk(h_lo), need if b == 0 else None, late)

            pe.wait_ge(const_in, 32)
            pe.wait_ge(ones_set, 1)
            sum_squares("norm1")
            sum_first(0, True)
            sum_first((0, 1))
            with pe.Fori(1, FIRST_UNITS // 2) as i:
                for parity in range(2):
                    sum_first((i, parity))

            pe.wait_ge(gw_lo_ready, 1)
            for kc in range(KC):
                pe.wait_ge(h_ready, kc + 1)
                for g in range(2):
                    dst, cols = px[0][:, g * T:(g + 1) * T], slice(kc * GROW, kc * GROW + P)
                    pe.matmul(dst, gw_hi[:, g, cols], h_hi[:, kc, :], start=(kc + g == 0), stop=False, skip_group_check=True)
                    pe.matmul(dst, gw_hi[:, g, cols], h_lo[:, kc, :], start=False, stop=False, skip_group_check=True)
                    mm = pe.matmul(dst, gw_lo[:, g, cols], h_hi[:, kc, :], start=False, stop=(kc == KC - 1), skip_group_check=True)
            mm.then_inc(gate_ps, 1)

            def a_head_scores(hd_):
                pe.wait_ge(rows_ready, 1)
                if hd_ == 0:
                    for b in range(2):
                        pe.wait_ge(bank_free[b], taken("w_in", 1, 2 + b))
                else:
                    pe.wait_ge(a_out, hd_)
                for sc in range(TT):
                    for dc in range(2):
                        pe.matmul(px[0][:, sc * T:(sc + 1) * T], ka[:, 2 * hd_ + dc, sc * P:(sc + 1) * P],
                                  qa[:, 2 * hd_ + dc, :], start=(dc == 0), stop=(dc == 1))
                for d in range(2):
                    r = hd_ + 32 * d
                    mm = pe.matmul(px[1 + d][:, :], ident[0:GROW, r:r + 1].to_broadcast([GROW, P]), neg_rows[0:GROW, :],
                                   start=True, stop=True)
                mm.then_inc(a_scores, 1)

            def a_head_mix(hd_):
                pe.wait_ge(a_probs, 2 * hd_ + 2)
                if hd_ == 0:
                    for b in range(2):
                        pe.wait_ge(bank_free[b], taken("w_in", 2, 2 + b))
                else:
                    pe.wait_ge(a_ms, hd_)
                for d in range(2):
                    for sc in range(TT):
                        pe.matmul(px[3][:, d * T:(d + 1) * T], ones[:, :], decay[:, d, sc * T:(sc + 1) * T],
                                  start=(sc == 0), stop=(sc == 1))
                    for ec in range(2):
                        for sc in range(TT):
                            mm = pe.matmul(px[1 + d][:, ec * T:(ec + 1) * T],
                                           va[:, sc, hd_ * DH_A + ec * P:hd_ * DH_A + (ec + 1) * P],
                                           decay[:, d, sc * T:(sc + 1) * T], start=(sc == 0), stop=(sc == 1))
                mm.then_inc(a_num, 1)

            def a_head_norm(hd_):
                pe.wait_ge(a_sq, hd_ + 1)
                for ec in range(2):
                    mm = pe.matmul(px[3][:, 0:T], ones[:, :], hb[:, ec, :], start=(ec == 0), stop=(ec == 1))
                mm.then_inc(a_ss, 1)

            for n in range(NBLOCKS["w_in"]):
                i, b = divmod(n, BODY)
                complete = w_in_complete(n - 1)
                late = (lambda: sum_unit(complete)) if complete is not None else None
                if n // 4 in (2, 6):
                    tokens("w_in", i, b, late=late)
                else:
                    columns("w_in", i, b, chunk(h_hi), chunk(h_lo), late=late)
                if n == 3:
                    pe.wait_ge(rows_ready, 1)
                    for sc in range(TT):
                        mm = pe.transpose(px[1][:, sc * GROW:(sc + 1) * GROW], gates[0:GROW, 5, sc * P:(sc + 1) * P],
                                          ident[0:GROW, 0:GROW])
                    mm.then_inc(bcol_ps, 1)
                if n in W_IN_STEPS:
                    step, k = W_IN_STEPS[n]
                    {"scores": a_head_scores, "mix": a_head_mix, "norm": a_head_norm}[step](k)

            for st, hd_ in waves(NH_B, 3):
                bank = px[hd_ % 4]
                if st == 0:
                    if hd_ == 0:
                        for b in range(2):
                            pe.wait_ge(bank_free[b], BBASE["w_out"] // 2)
                        pe.wait_ge(a_out, NH_A)
                    if hd_ >= 4:
                        pe.wait_ge(mix_ready, 4 + hd_ - 3)
                    for tt in range(TT):
                        mm = pe.matmul(bank[:, tt * T:(tt + 1) * T], qb[:, hd_, tt * P:(tt + 1) * P], kb[:, hd_, :],
                                       start=True, stop=True)
                    mm.then_inc(b_scores, 1)
                elif st == 1:
                    pe.wait_ge(b_probs, hd_ + 1)
                    for sc in range(TT):
                        for tt in range(TT):
                            mm = pe.transpose(bank[:, sc * T + tt * P:sc * T + (tt + 1) * P],
                                              s_b[hd_ % 2][:, tt, sc * P:(sc + 1) * P], ident[:, :])
                    mm.then_inc(b_pt, 1)
                else:
                    pe.wait_ge(b_ptsb, hd_ + 1)
                    for sc in range(TT):
                        mm = pe.matmul(bank[:, 0:T], vb[:, sc, hd_ * DH_B:(hd_ + 1) * DH_B], pt_b[hd_ % 2][:, sc, :],
                                       start=(sc == 0), stop=(sc == 1))
                    mm.then_inc(b_num, 1)

            sum_unit(w_in_complete(NBLOCKS["w_in"] - 1))
            pe.wait_ge(mix_ready, 4 + NH_B)
            stage_columns("w_out")
            sum_squares("norm2")

            for half in range(2):
                up, down = f"w_up{half}", f"w_down{half}"
                stage_columns(up, h_needed("norm2"))
                for b in range(FH % BODY):
                    columns(up, FH // BODY, b, chunk(h_hi), chunk(h_lo))
                with pe.Fori(0, NBLOCKS[down] // BODY) as i:
                    for b in range(BODY):
                        need = (lambda q: pe.wait_ge(glu_lo_ready, half * FH + min(4 * q + 4, FH))) if b == 0 else None
                        late = (lambda: sum_unit(i + UNIT_OF[down])) if b == BODY - 1 and down in UNIT_OF else None
                        columns(down, i, b, chunk(glu_hi), chunk(glu_lo), need, late)
            sum_squares("final")
            sum_squares("final" + "g", ssqg, 1)

            with pe.Fori(0, NBLOCKS["sgu_v"] // BODY) as i:
                for b in range(BODY):
                    tokens("sgu_v", i, b, h_needed("pre0") if b == 0 else None,
                           (lambda: sum_unit(i + UNIT_OF["sgu_v"])) if b == BODY - 1 else None)
            stage_columns("sgu_u", hi=2)

            def mix_group(g):
                s, r = g // 2 % 2, g % 2
                if g == 0:
                    pe.wait_ge(v_normed, 2)
                if r == 0:
                    pe.wait_ge(mixw_full[s], (g // 4 + 1) * 16)
                if g >= 4:
                    pe.wait_ge(vm_taken, g - 3)
                for c in range(2):
                    for n in range(TT):
                        for part in range(2):
                            seen = slice(0, 64 * (part + 1))
                            t0 = 64 * part
                            mm = pe.matmul(px[g % 4][:, c * T + n * P + t0:c * T + n * P + t0 + 64],
                                           v_sgu[seen, n, g * 2 * P + c * P:g * 2 * P + (c + 1) * P],
                                           mixw[seen, s, r, 0, t0:t0 + 64], start=True, stop=True)
                mm.then_inc(vm_ready, 1)

            for n in range(8, 16):
                i, b = divmod(n, BODY)
                columns("sgu_u", i, b, chunk(h_hi), chunk(h_lo),
                        late=(lambda: sum_unit(i + UNIT_OF["sgu_u"])) if b == BODY - 1 else None)
                for g in (2 * n - 16, 2 * n - 15):
                    mix_group(g)
            stage_columns("sgu_z")
            with pe.Fori(0, NBLOCKS["sgu_out"] // BODY) as i:
                for b in range(BODY):
                    columns("sgu_out", i, b, chunk(y_hi), chunk(y_lo),
                            (lambda q: pe.wait_ge(y_lo_ready, 2 * (q + 1))) if b == 0 else None,
                            (lambda: sum_unit(i + UNIT_OF["sgu_out"])) if b == BODY - 1 else None)
            sum_squares("post0")
            pe.wait_ge(ms_ready, SUMS["post0"])
            for c in range(KC):
                if c % 2 == 0:
                    pe.wait_ge(pre_sq, c // 2 + 1)
                mm = pe.matmul(ps[:, 0:T], ones[:, :], pre_bufs[c // 2 % 4][:, c % 2, :], start=(c == 0), stop=(c == KC - 1))
                if c % 2:
                    mm.then_inc(pre_summed if c < KC - 1 else ss_ready, 1)

            for b in range(BODY):
                columns("lat", 0, b, chunk(h_hi), chunk(h_lo), h_needed("pre1") if b == 0 else None,
                        (lambda: sum_unit(UNIT_OF["lat"])) if b == BODY - 1 else None)

            def latent_squares():
                pe.wait_ge(lat_sq, 2)
                pe.wait_ge(ms_ready, SUMS["pre1"])
                for c in range(4):
                    mm = pe.matmul(ps[:, 0:T], ones[:, :], lsq[:, c, :], start=(c == 0), stop=(c == 3))
                mm.then_inc(ss_ready, 1)
                for c in range(4, 8):
                    rows = slice(0, P) if c < 7 else slice(64, P)
                    mm = pe.matmul(ps[:, T:2 * T], ones[rows, :], lsq[rows, c, :], start=(c == 4), stop=(c == 7))
                mm.then_inc(ss_ready, 1)

            def rotated_key():
                pe.wait_ge(mla_const_in, 16)
                pe.wait_ge(vm_taken, GROUPS)
                pe.matmul(px[1][:, 0:T], rot, lat[0:ROPE, 7, :], start=True, stop=True).then_inc(kr_rot, 1)

            for n in range(NBLOCKS["mla_z"]):
                columns("mla_z", n // BODY, n % BODY, chunk(h_hi), chunk(h_lo),
                        late={0: latent_squares, 3: lambda: sum_unit(UNIT_OF["mla_z"]), 4: rotated_key}.get(n))
            for b in range(2):
                pe.wait_ge(bank_free[b], BBASE["heads"] // 2)
            pe.wait_ge(ms_ready, SUMS["q"])
            pe.wait_ge(unit_taken, 12 * UNITS)
            pe.wait_ge(lat_lo_ready, 2)
            pe.wait_ge(kr_ready, 1)
            for j in range(4):
                pe.sem_inc(head_free[j], 1)
            bank_a = [pm[0], pm[1], ps, pv]

            def head_step(i, step):
                for st, hn, j in head_stages(i, step):
                    A, B = bank_a[j], px[j]
                    if st == 0:
                        pe.wait_ge(head_free[j], i + 1)
                        for q in range(2):
                            k = 2 * j + q
                            pe.wait_ge(lo_odd if k % 2 else lo_even, pairs("heads", i, k))
                            wh, wl = (halves(w[:, k % SLOTS, 0:2 * HEADW]) for w in (w_hi, w_lo))
                            for kc in range(2 * q, 2 * q + 2):
                                first, last = kc == 0, kc == 3
                                rows = slice(0, P) if kc < 3 else slice(64, P)
                                for dst, lo, c, r in ((A[:, 0:T], 0, 4 + kc, rows), (A[:, T:2 * T], NOPE, 4 + kc, rows),
                                                      (B[:, 0:T], NOPE + ROPE, kc, slice(0, P))):
                                    cols = slice(lo, lo + P)
                                    pe.matmul(dst, wh[r, kc % 2, cols], lat_hi[r, c, :], start=(first and lo != NOPE), stop=False,
                                              skip_group_check=True)
                                    pe.matmul(dst, wh[r, kc % 2, cols], lat_lo[r, c, :], start=False, stop=False, skip_group_check=True)
                                    pe.matmul(dst, wl[r, kc % 2, cols], lat_hi[r, c, :], start=False, stop=last, skip_group_check=True)
                                for tt in range(TT):
                                    dst, ts = B[:, T + tt * P:T + (tt + 1) * P], slice(tt * P, (tt + 1) * P)
                                    vc = slice(HEADW - VD, HEADW)
                                    pe.matmul(dst, lat_hi[:, kc, ts], wh[:, kc % 2, vc], start=False, stop=False, skip_group_check=True)
                                    pe.matmul(dst, lat_hi[:, kc, ts], wl[:, kc % 2, vc], start=False, stop=False, skip_group_check=True)
                                    mm = pe.matmul(dst, lat_lo[:, kc, ts], wh[:, kc % 2, vc], start=False, stop=last, skip_group_check=True)
                            mm.then_inc(quarter_done, 1)
                    elif st == 1:
                        pe.wait_ge(m_proj, hn + 1)
                        pe.matmul(B[:, 0:T], rot, qr[j], start=True, stop=True).then_inc(m_rot, 1)
                    elif st == 2:
                        pe.wait_ge(m_rope, hn + 1)
                        for lo, tt in ((0, 0), (P, 1)):
                            keys = P * (tt + 1)
                            pe.matmul(A[:, lo:lo + keys], qn[j][:, tt * P:(tt + 1) * P], kv[j][:, 0:keys],
                                      start=True, stop=False)
                            mm = pe.matmul(A[:, lo:lo + keys], qr[j][:, tt * P:(tt + 1) * P], kro[:, 0:keys],
                                           start=False, stop=True)
                        mm.then_inc(m_scores, 1)
                    elif st == 3:
                        pe.wait_ge(m_probs, hn + 1)
                        for lo in (0, P, 2 * P):
                            mm = pe.transpose(B[:, lo:lo + P], pr[j][:, lo:lo + P], ident[:, :])
                        mm.then_inc(m_pt, 1)
                    else:
                        pe.wait_ge(m_ptsb, hn + 1)
                        pe.matmul(A[:, 0:T], kv[j][:, T:T + P], pt[j][:, 0:T], start=True, stop=False, skip_group_check=True)
                        pe.matmul(A[:, P:T], kv[j][:, T + P:2 * T], pt[j][:, T:T + P], start=False, stop=True,
                                  skip_group_check=True).then_inc(m_num, 1)

            for j in range(BODY):
                head_step(0, j)
            with pe.Fori(1, MH // BODY) as i:
                for j in range(BODY):
                    head_step(i, j)
            for j in range(BODY):
                head_step(MH // BODY, j)
            for j in range(4):
                pe.wait_ge(head_free[j], MH // BODY + 1)
            stage_columns("mla_out", lambda q: pe.wait_ge(o_ready, 4 * (q + 1)))
            sum_squares("post1")

        @block.scalar
        def _(act):
            chain = Chain(act, act_step)

            def split(stage, i, b, loads=()):
                ks = ahead(stage, i, b) if b is not None else range(AHEAD)
                for n, k in enumerate(ks):
                    if k % 2 == 0:
                        act.wait_ge(slot_full[k // 2 % SLOTS], (quarter(stage, i, 0) + k) * 2 + 16 - (QBASE[stage] + k) % 8 * 2)
                    if not (isinstance(i, int) and quarter(stage, i, k) < SLOTS):
                        act.wait_ge(quarter_done, quarter(stage, i, k) - (SLOTS - 1))
                    act.activation(w_hi[:, k % SLOTS, 0:elems(stage, k)], raw_part(stage, k), ACT.Copy).then_inc(hi_ready, 1)
                    share = -(-len(loads) // len(ks))
                    for u, piece in loads[n * share:(n + 1) * share]:
                        load_piece(u, piece)

            def load_piece(u, k):
                act.wait_ge(ada_used, u * APIECES + (k + 1 - SLOTS))
                act.dma_start(ada[:, k % SLOTS, :], row(a["ada"], u * APIECES + k)).then_inc(ada_full[k % SLOTS], 16)

            def freed(u, pieces):
                last = 12 * UNITS * APIECES
                return [(u, k + SLOTS) for k in pieces if not (isinstance(u, int) and u * APIECES + k + SLOTS >= last)]

            def freed_in_body(stage, i, b):
                return freed(i + UNIT_OF[stage], body_pieces(b - 1)) if b and stage in UNIT_OF else []

            def squares(name, i, b, src):
                c = i * BODY + (b + ADDED[name] - PAIRS)
                if not (isinstance(c, int) and c == 0):
                    act.wait_ge(sq_added, c)
                act.activation(flat(sqt[:, :, :]), src, ACT.Square).then_inc(sq_ready, 1)

            def root(name):
                act.wait_ge(ms_ready, SUMS[name])
                act.activation(rstd[:, :], rstd[:, :], ACT.Sqrt).then_inc(std_ready, 1)

            def modulate(norm, shift):
                k = H_NORMS.index(norm)
                for kc in range(KC):
                    act.wait_ge(xn_ready, k * KC + kc + 1)
                    act.activation(h_hi[:, kc, :], nt[:, kc % 4, :], ACT.Identity, bias=mod(shift, kc)).then_inc(hh_ready, 1)

            act.wait_ge(const_in, 32)
            act.activation(flat(csil[:, :, :]), pcols("c", 2 * KC), ACT.Silu).then_inc(silu_c, 1)
            act.wait_ge(x_in, 16)
            for p in range(PAIRS):
                squares("norm1", 0, p, flat(x[:, 2 * p:2 * p + 2, :]))
            act.wait_ge(mix_const_in, 32)
            act.activation(flat(gw_hi[:, :, :]), flat(gw[:, :, :]), ACT.Copy).then_inc(gw_hi_ready, 1)
            root("norm1")
            for k in range(SLOTS):
                load_piece(FIRST_UNITS, k)
            modulate("norm1", SH1)
            split("w_in", 0, None)

            act.wait_ge(gate_rows, 1)
            chain.link(act.activation(gates[0:GROW, 3, :], gates[0:GROW, 2, :], ACT.Exp))
            act.activation(gates[0:GROW, 3, :], gates[0:GROW, 3, :], ACT.Ln, bias=1.0).then_inc(gate_exp, 1)

            def a_head_scores(hd_):
                for d in range(2):
                    r = hd_ + 32 * d
                    act.wait_ge(a_arg, 2 * hd_ + d + 1)
                    for sc in range(TT):
                        act.activation(decay[:, d, sc * T:(sc + 1) * T], decay[:, d, sc * T:(sc + 1) * T], ACT.Exp,
                                       bias=bcol[:, sc, r:r + 1])
                    act.activation(expm[:, d, :], px[1 + d][:, T:2 * T], ACT.Exp).then_inc(a_exp, 1)
                if hd_ == NH_A - 1:
                    act.dma_start(flat(bias_b[:, :, :]), a["bias_b"]).then_inc(bias_in, 16)

            def a_head_norm(hd_):
                act.wait_ge(a_ms, hd_ + 1)
                act.activation(expm[:, 0, :], expm[:, 0, :], ACT.Sqrt).then_inc(a_std, 1)

            dsts = [ka, qa, va, oa, qb, kb, vb]
            for n in range(NBLOCKS["w_in"]):
                i, b = divmod(n, BODY)
                split("w_in", i, b, freed(*w_in_pieces(n - 1)) if n else [])
                act.wait_ge(quarter_done, done("w_in", i, b))
                dst = dsts[i][:, :, b * COLS:(b + 1) * COLS] if i in (2, 6) else dsts[i][:, 2 * b:2 * b + 2, :]
                if n == 16:
                    act.wait_ge(rows_ready, 1)
                    act.wait_ge(bcol_ready, 1)
                act.activation(dst, halves(pm[b % 2][:, :]), ACT.Sigmoid if i == 3 else ACT.Copy).then_inc(bank_free[b % 2], 1)
                if n in W_IN_STEPS and W_IN_STEPS[n][0] != "mix":
                    step, k = W_IN_STEPS[n]
                    {"scores": a_head_scores, "norm": a_head_norm}[step](k)

            act.wait_ge(a_out, NH_A)
            for p in range(4):
                act.activation(h_hi[:, 2 * p:2 * p + 2, :], oa[:, 2 * p:2 * p + 2, :], ACT.Copy).then_inc(oa_hi, 1)
            for u, k in freed(*w_in_pieces(NBLOCKS["w_in"] - 1)):
                load_piece(u, k)
            for st, hd_ in waves(NH_B, 3):
                j = hd_ % 2
                if st == 0:
                    act.wait_ge(b_negmax, hd_ + 1)
                    for tt in range(TT):
                        ex = act.activation(s_b[j][:, tt, :], s_b[j][:, tt, :], ACT.Exp, bias=small_b[:, j, 1, tt:tt + 1],
                                            accum_out=small_b[:, j, 2, tt:tt + 1])
                    ex.then_inc(b_exp, 1)
                elif st == 1:
                    act.wait_ge(b_pt, hd_ + 1)
                    if hd_ >= 2:
                        act.wait_ge(b_num, hd_ - 1)
                    act.activation(flat(pt_b[j][:, :, :]), px[hd_ % 4][:, :], ACT.Copy).then_inc(b_ptsb, 1)
                else:
                    act.wait_ge(b_num, hd_ + 1)
                    act.activation(h_hi[:, 8 + hd_, :], px[hd_ % 4][:, 0:T], ACT.Copy).then_inc(b_hi, 1)

            with act.Fori(0, NBLOCKS["w_out"] // BODY) as i:
                for b in range(BODY):
                    split("w_out", i, b, freed_in_body("w_out", i, b))
                    act.wait_ge(bank_free[b % 2], taken("w_out", i, b))
                    squares("norm2", i, b, at(x, i * (2 * BODY) + 2 * b, 2).rearrange("p a b -> p (a b)"))
            root("norm2")
            modulate("norm2", SH2)

            def up(half, i, b, loads=()):
                stage, k = f"w_up{half}", i * BODY + (half * FH + b)
                split(stage, i, b, loads)
                act.wait_ge(quarter_done, done(stage, i, b))
                act.activation(gpad[:, 1:1 + T], pm[b % 2][:, 0:T], ACT.Copy).then_inc(g_copied, 1)
                act.wait_ge(conv_ready, k + 1)
                act.activation(conv[:, :], conv[:, :], ACT.Gelu).then_inc(gelu_ready, 1)
                act.wait_ge(bank_free[b % 2], taken(stage, i, b))
                act.activation(one(glu_hi, i * BODY + b), conv[:, :], ACT.Copy).then_inc(glu_hi_ready, 1)

            for half in range(2):
                down = f"w_down{half}"
                with act.Fori(0, FH // BODY) as i:
                    for b in range(BODY):
                        up(half, i, b, freed_in_body(f"w_up{half}", i, b))
                for b in range(FH % BODY):
                    up(half, FH // BODY, b)
                with act.Fori(0, NBLOCKS[down] // BODY) as i:
                    for b in range(BODY):
                        split(down, i, b, freed_in_body(down, i, b))
                        if half == 1:
                            act.wait_ge(bank_free[b % 2], taken(down, i, b))
                            c = i * (2 * BODY) + 2 * b
                            squares("final", i, b, at(x, c, 2).rearrange("p a b -> p (a b)"))
                            for j in range(2):
                                sg = act.activation(sqtg[:, j, :], one(x, c + j), ACT.Square, scale=pcol("gfinal", c + j))
                            sg.then_inc(sqg_ready, 1)
            root("final")
            root("finalg")
            modulate("pre0", S0)

            with act.Fori(0, NBLOCKS["sgu_v"] // BODY) as i:
                for b in range(BODY):
                    split("sgu_v", i, b, freed_in_body("sgu_v", i, b))
                    act.wait_ge(quarter_done, done("sgu_v", i, b))
                    for tt in range(TT):
                        ge = act.activation(v_sgu[:, tt, bass.ds((i * BODY + b) * COLS, COLS)], pm[b % 2][:, tt * COLS:(tt + 1) * COLS],
                                            ACT.Gelu, accum_out=stat[:, tt, bass.ds(i * BODY + b, 1)])
                    ge.then_inc(bank_free[b % 2], 1)
            act.wait_ge(h_ready, 3 * KC)

            def load_mix(p):
                act.dma_start(mixw[:, p % 2, :, :, :].rearrange("p a b c -> p (a b c)"), a["mix"][p]).then_inc(mixw_full[p % 2], 16)

            for p in range(2):
                load_mix(p)

            def u_block(i, b):
                split("sgu_u", i, b, freed_in_body("sgu_u", i, b))
                act.wait_ge(quarter_done, done("sgu_u", i, b))
                act.activation(at(gu, i * (2 * BODY) + 2 * b, 2), halves(pm[b % 2][:, :]), ACT.Gelu).then_inc(bank_free[b % 2], 1)

            with act.Fori(0, 2) as i:
                for b in range(BODY):
                    u_block(i, b)
                    tt = b // 2
                    act.wait_ge(v_mean, tt + 1)
                    for r in range(2):
                        part = i * 4 + (b % 2 * 2 + r)
                        sq = act.activation(stmp[:, r, :], v_sgu[:, tt, bass.ds(part * 512, 512)], ACT.Square,
                                            accum_out=stat[:, tt, bass.ds(part + 16, 1)])
                    sq.then_inc(v_sq, 1)
                    act.wait_ge(v_sq, i * BODY + (b + 1))
            for tt in range(TT):
                act.wait_ge(v_var, tt + 1)
                act.activation(stat[:, tt, 28:29], stat[:, tt, 27:28], ACT.Sqrt).then_inc(v_std, 1)
            for n in range(8, 16):
                u_block(*divmod(n, BODY))
                p = n - 7
                if 2 <= p < GROUPS // 2:
                    act.wait_ge(vm_taken, 2 * p - 2)
                    load_mix(p)
            act.wait_ge(vm_taken, GROUPS)
            with act.Fori(0, NBLOCKS["sgu_z"] // BODY) as i:
                for b in range(BODY):
                    split("sgu_z", i, b, freed_in_body("sgu_z", i, b))
                    act.wait_ge(quarter_done, done("sgu_z", i, b))
                    act.activation(ztmp[:, b % 2, :], pm[b % 2][:, :], ACT.Silu).then_inc(bank_free[b % 2], 1)
                    act.wait_ge(y_ready, i * BODY + (b + 1))
                    act.activation(at(y_hi, i * (2 * BODY) + 2 * b, 2), at(gu, i * (2 * BODY) + 2 * b, 2), ACT.Copy).then_inc(y_hi_ready, 1)

            def output_block(stage, i, b, norm, dst):
                split(stage, i, b, freed_in_body(stage, i, b))
                act.wait_ge(quarter_done, done(stage, i, b))
                squares(norm, i, b, pm[b % 2][:, :])
                act.activation(at(dst, i * (2 * BODY) + 2 * b, 2), halves(pm[b % 2][:, :]), ACT.Copy).then_inc(bank_free[b % 2], 1)

            with act.Fori(0, NBLOCKS["sgu_out"] // BODY) as i:
                for b in range(BODY):
                    output_block("sgu_out", i, b, "post0", y0)
            root("post0")
            for p in range(PAIRS):
                act.wait_ge(x_pool if p % 2 else x_ready, p // 2 + 1)
                if p >= 4:
                    act.wait_ge(pre_summed, p - 3)
                act.activation(pre_bufs[p % 4], x[:, 2 * p:2 * p + 2, :], ACT.Square).then_inc(pre_sq, 1)
            root("pre1")
            modulate("pre1", S1)

            for b in range(BODY):
                split("lat", 0, b, freed_in_body("lat", 0, b))
                act.wait_ge(quarter_done, done("lat", 0, b))
                if b == 0:
                    act.dma_start(cst[:, :], a["mla_cst"]).then_inc(mla_const_in, 16)
                act.activation(lat[:, 2 * b:2 * b + 2, :], halves(pm[b % 2][:, :]), ACT.Copy).then_inc(bank_free[b % 2], 1)
            for b in range(2):
                act.wait_ge(bank_free[b], BBASE["mla_z"] // 2)
            for part in range(2):
                act.activation(lsq[:, 4 * part:4 * part + 4, :], lat[:, 4 * part:4 * part + 4, :], ACT.Square).then_inc(lat_sq, 1)
            for n in range(NBLOCKS["mla_z"]):
                i, b = divmod(n, BODY)
                split("mla_z", i, b, freed_in_body("mla_z", 0, b) if i == 0 else [])
                act.wait_ge(quarter_done, done("mla_z", i, b))
                act.activation(zo[:, 2 * n:2 * n + 2, :], halves(pm[b % 2][:, :]), ACT.Silu).then_inc(bank_free[b % 2], 1)
                if n in (1, 2):
                    root({1: "kv", 2: "q"}[n])
                if n == 3:
                    for part in range(2):
                        act.wait_ge(lat_normed, part + 1)
                        act.activation(lat_hi[:, 4 * part:4 * part + 4, :], lat[:, 4 * part:4 * part + 4, :], ACT.Copy).then_inc(lat_hi_ready, 1)

            def head_step(i, step):
                for st, hn, j in head_stages(i, step):
                    A, B = [pm[0], pm[1], ps, pv][j], px[j]
                    if st == 0:
                        split("heads", i, j)
                        act.wait_ge(quarter_done, done("heads", i, j))
                        act.activation(qn[j], A[:, 0:T], ACT.Copy)
                        act.activation(qr[j], A[0:ROPE, T:2 * T], ACT.Copy)
                        act.activation(kv[j], B[:, :], ACT.Copy).then_inc(m_proj, 1)
                    elif st == 2:
                        act.wait_ge(m_negmax, hn + 1)
                        for lo, tt in ((0, 0), (P, 1)):
                            keys = P * (tt + 1)
                            ex = act.activation(pr[j][:, lo:lo + keys], pr[j][:, lo:lo + keys], ACT.Exp,
                                                bias=small_m[:, j, 1, tt:tt + 1], accum_out=small_m[:, j, 2, tt:tt + 1])
                        ex.then_inc(m_exp, 1)
                    elif st == 3:
                        act.wait_ge(m_pt, hn + 1)
                        act.activation(pt[j][:, :], B[:, 0:3 * P], ACT.Copy).then_inc(m_ptsb, 1)
                for st, hn, j in head_stages(i, step):
                    if st == 4:
                        act.wait_ge(head_free[j], i + 1)
                        act.activation(one(h_hi, hn), one(zo, hn), ACT.Copy).then_inc(m_hi, 1)

            for j in range(BODY):
                head_step(0, j)
            with act.Fori(1, MH // BODY) as i:
                for j in range(BODY):
                    head_step(i, j)
            for j in range(BODY):
                head_step(MH // BODY, j)
            for n in range(NBLOCKS["mla_out"]):
                output_block("mla_out", n // BODY, n % BODY, "post1", y1)
            root("post1")

        @block.vector
        def _(dve):
            chain = Chain(dve, dve_step)
            tt_ = dve.tensor_tensor
            ts_ = dve.tensor_scalar
            stt = dve.scalar_tensor_tensor

            def split(stage, i, b, due=()):
                ks = [k for k in (ahead(stage, i, b) if b is not None else range(AHEAD)) if k % 2 == 0]
                for m, k in enumerate(ks):
                    dve.wait_ge(hi_ready, quarter(stage, i, k) + 1)
                    n = elems(stage, k)
                    tt_(w_lo[:, k % SLOTS, 0:n], raw_part(stage, k), whole(w_hi[:, k % SLOTS, 0:n]),
                        ALU.subtract).then_inc(lo_even, 1)
                    if due:
                        if m == 0 and due[3] is not None:
                            take(due[3])
                        share = -(-len(due[2]) // len(ks))
                        pieces(due[0], due[1], due[2][m * share:(m + 1) * share])

            def pieces(u, cond, ks):
                for k in ks:
                    dve.wait_ge(ada_full[k % SLOTS], u * 32 + (k // SLOTS + 1 - FIRST_UNITS) * 16)
                    for r in range(2):
                        w, c = ada[:, k % SLOTS, r * UCOLS:(r + 1) * UCOLS], csil[:, cond, 2 * k + r:2 * k + r + 1]
                        if k + r == 0:
                            ins = ts_(acc[:, :], w, c, None, ALU.mult)
                        else:
                            ins = stt(acc[:, :], w, c, acc[:, :], ALU.mult, ALU.add)
                        if r == 0:
                            chain.link(ins)
                    ins.then_inc(ada_used, 1)
                    dve.wait_ge(ada_used, u * APIECES + (k + 1))

            def first_piece(u, parity, k):
                dve.wait_ge(ada_full[k], u * 16 + 16)
                buf = ada[:, k, :] if k < SLOTS else e1[:, k - SLOTS, :]
                for r in range(2):
                    w, c = buf[:, r * UCOLS:(r + 1) * UCOLS], csil[:, 0, 2 * k + r:2 * k + r + 1]
                    dst = acc_first[:, parity, r, :]
                    if k == 0:
                        ins = ts_(dst, w, c, None, ALU.mult)
                    else:
                        dve.wait_ge(first_even if r == 0 else ada_used, u * APIECES + k)
                        ins = stt(dst, w, c, dst, ALU.mult, ALU.add)
                    ins.then_inc(first_even if r == 0 else ada_used, 1)

            def take(u):
                dve.wait_ge(unit_summed, u + 1)
                cols = bass.ds(u * 4, 4) if not isinstance(u, int) else slice(4 * u, 4 * u + 4)
                bias = bass.ds(u * 4 + PCOL["bias"], 4) if not isinstance(u, int) else slice(PCOL["bias"] + 4 * u, PCOL["bias"] + 4 * u + 4)
                tt_(mods[:, cols], pv[:, 0:4], par[:, bias], ALU.add).then_inc(unit_taken, 1)
                dve.wait_ge(unit_taken, u + 1)

            def due_in_body(stage, i, b, cond):
                return i + UNIT_OF[stage], cond, body_pieces(b), None

            def take_in_body(stage, i, b):
                if b == BODY - 1:
                    take(i + UNIT_OF[stage])

            def clear_squares(*more):
                for buf in more:
                    dve.memset(flat(buf[:, :, :]), 0.0)
                chain.link(dve.memset(flat(ssq[:, :, :]), 0.0))

            def add_squares(name, i, b):
                dve.wait_ge(sq_ready, i * BODY + (b + 1 + ADDED[name] - PAIRS))
                tt_(ssq[:, :, :], ssq[:, :, :], sqt[:, :, :], ALU.add).then_inc(sq_added, 1)

            def rsqrt_mean(name, width, half=0, dst=rstd):
                dve.wait_ge(ss_ready, SUMS[{"final": "finalg", "kv": "q"}.get(name, name)])
                ts_(rstd[:, :], ps[:, half * T:(half + 1) * T], 1.0 / width, EPS, ALU.mult, ALU.add).then_inc(ms_ready, 1)
                dve.wait_ge(std_ready, SUMS[name])
                chain.link(dve.reciprocal(dst[:, :], rstd[:, :]))

            def modulation(norm, g, gc, scale):
                chain.link(stt(gain[:, H_NORMS.index(norm), :], mods[:, scale * KC:(scale + 1) * KC], 1.0, pcols(g, KC, gc),
                               ALU.add, ALU.mult))

            def normed(norm, shift):
                k = H_NORMS.index(norm)

                def xn(kc):
                    stt(nt[:, kc % 4, :], x[:, kc, :], gain[:, k, kc:kc + 1], rstd[:, :], ALU.mult, ALU.mult).then_inc(xn_ready, 1)

                for kc in range(3):
                    xn(kc)
                for kc in range(KC):
                    dve.wait_ge(hh_ready, k * KC + kc + 1)
                    stt(h_lo[:, kc, :], nt[:, kc % 4, :], mod(shift, kc), whole(h_hi[:, kc, :]), ALU.add, ALU.subtract).then_inc(h_ready, 1)
                    if kc + 3 < KC:
                        if kc:
                            dve.wait_ge(h_ready, k * KC + kc)
                        xn(kc + 3)

            def residual(stage, i, b, gate):
                dve.wait_ge(quarter_done, done(stage, i, b))
                for j in range(2):
                    c = i * (2 * BODY) + (2 * b + j)
                    xc = one(x, c)
                    ins = stt(xc, pm[b % 2][:, j * T:(j + 1) * T], mod(gate, c), xc, ALU.mult, ALU.add)
                ins.then_inc(bank_free[b % 2], 1)

            dve.memset(ones[:, :], 1.0).then_inc(ones_set, 1)
            dve.memset(gates[0:GROW, :, :], 0.0)
            clear_squares()
            for p in range(PAIRS):
                add_squares("norm1", 0, p)
            dve.wait_ge(gw_hi_ready, 1)
            tt_(gw_lo[:, :, :], gw[:, :, :], whole(gw_hi[:, :, :]), ALU.subtract).then_inc(gw_lo_ready, 1)
            rsqrt_mean("norm1", D)
            dve.wait_ge(silu_c, 1)
            for k in range(APIECES):
                first_piece(0, 0, k)
            with dve.Fori(0, FIRST_UNITS // 2 - 1) as i:
                for parity in range(2):
                    u = i * 2 + parity
                    for k in range(APIECES):
                        first_piece(u + 1, 1 - parity, k)
                    take(u)
            for k in range(APIECES):
                first_piece(FIRST_UNITS - 1, 1, k)
            take(FIRST_UNITS - 2)
            take(FIRST_UNITS - 1)
            modulation("norm1", "g1", 0, SC1)
            normed("norm1", SH1)
            split("w_in", 0, None)

            G = slice(0, GROW)

            def gate_step(n):
                if n == 0:
                    dve.wait_ge(gate_ps, 1)
                    chain.link(ts_(gates[G, 0, :], px[0][G, 0:T], pcol("bi", 0, G), None, ALU.add))
                    chain.link(ts_(gates[G, 1, :], px[0][G, T:2 * T], pcol("bf", 0, G), None, ALU.add))
                    stt(gates[G, 2, :], gates[G, 1, :], -1.0, gates[G, 1, :], ALU.mult, ALU.min).then_inc(gate_rows, 1)
                elif n == 1:
                    dve.wait_ge(gate_exp, 1)
                    chain.link(stt(gates[G, 1, :], gates[G, 1, :], 0.0, gates[G, 3, :], ALU.min, ALU.subtract))
                    for rows, step in ((slice(0, NH_A), 1), (slice(32, GROW), -1)):
                        chain.link(dve.tensor_tensor_scan(gates[rows, 4, ::step], ones[rows, 0:1].to_broadcast([NH_A, T]),
                                                          gates[rows, 1, ::step], 0.0, ALU.mult, ALU.add))
                    chain.link(tt_(gates[G, 5, :], gates[G, 0, :], gates[G, 4, :], ALU.subtract))
                elif n == 2:
                    for rows, step in ((slice(0, NH_A), 1), (slice(32, GROW), -1)):
                        chain.link(dve.tensor_tensor_scan(gates[rows, 6, ::step], gates[rows, 5, ::step], gates[rows, 5, ::step],
                                                          -3.0e38, ALU.max, ALU.max))
                    chain.link(ts_(neg_rows[G, 0:T], gates[G, 6, :], -1.0, None, ALU.mult))
                    stt(neg_rows[G, T:2 * T], gates[G, 4, :], -1.0, gates[G, 6, :], ALU.mult, ALU.subtract).then_inc(rows_ready, 1)
                else:
                    dve.wait_ge(bcol_ps, 1)
                    dve.tensor_copy(flat(bcol[:, :, :]), px[1][:, 0:2 * GROW]).then_inc(bcol_ready, 1)

            def a_head_scores(hd_):
                dve.wait_ge(a_scores, hd_ + 1)
                if hd_:
                    dve.wait_ge(a_num, hd_)
                for d in range(2):
                    tt_(halves(decay[:, d, :]), over(px[1 + d][:, 0:T], 2), halves(mask_a[:, d, :]), ALU.add).then_inc(a_arg, 1)
                for d in range(2):
                    dve.wait_ge(a_exp, 2 * hd_ + d + 1)
                    stt(decay[:, d, :], px[0][:, :], SCALE_A, decay[:, d, :], ALU.mult, ALU.mult).then_inc(a_probs, 1)

            def a_head_mix(hd_):
                dve.wait_ge(a_num, hd_ + 1)
                em = flat(expm[:, :, :])
                chain.link(stt(em, px[3][:, :], -1.0, em, ALU.mult, ALU.max))
                chain.link(tt_(em, px[3][:, :], em, ALU.max))
                chain.link(dve.reciprocal(em, em))
                tt_(hf[:, :, :], halves(px[1][:, :]), over(expm[:, 0, :], 2), ALU.mult)
                chain.link(tt_(hb[:, :, :], halves(px[2][:, :]), over(expm[:, 1, :], 2), ALU.mult))
                chain.link(tt_(hf[:, :, :], hf[:, :, :], hb[:, :, :], ALU.add))
                tt_(hb[:, :, :], hf[:, :, :], hf[:, :, :], ALU.mult).then_inc(a_sq, 1)

            def a_head_norm(hd_):
                dve.wait_ge(a_ss, hd_ + 1)
                ts_(expm[:, 0, :], px[3][:, 0:T], 1.0 / DH_A, EPS, ALU.mult, ALU.add).then_inc(a_ms, 1)
                dve.wait_ge(a_std, hd_ + 1)
                chain.link(dve.reciprocal(expm[:, 0, :], expm[:, 0, :]))
                dve.wait_ge(bank_free[hd_ % 2], taken("w_in", 3, hd_))
                for ec in range(2):
                    ins = stt(hf[:, ec, :], hf[:, ec, :], pcol("ghead", 2 * hd_ + ec), expm[:, 0, :], ALU.mult, ALU.mult)
                chain.link(ins)
                oh = oa[:, 2 * hd_:2 * hd_ + 2, :]
                tt_(oh, oh, hf[:, :, :], ALU.mult).then_inc(a_out, 1)

            gate_step(0)
            for n in range(NBLOCKS["w_in"]):
                u, ks = w_in_pieces(n)
                split("w_in", n // BODY, n % BODY, (u, 0, ks, w_in_complete(n - 1)))
                if n < 2:
                    gate_step(n + 1)
                if n == 4:
                    gate_step(3)
                if n in W_IN_STEPS:
                    step, k = W_IN_STEPS[n]
                    {"scores": a_head_scores, "mix": a_head_mix, "norm": a_head_norm}[step](k)
                if n == 25:
                    dve.wait_ge(bias_in, 16)
                    dve.wait_ge(wmask_in, 16)
                    chain.link(tt_(bias_b[:, :, :], bias_b[:, :, :], over(wmask[:, :], NH_B * 6), ALU.add))

            bias_rows = flat(bias_b[:, :, :])
            for st, hd_ in waves(NH_B, 4):
                j = hd_ % 2
                if st == 0:
                    dve.wait_ge(b_scores, hd_ + 1)
                    if hd_ >= 2:
                        dve.wait_ge(b_pt, hd_ - 1)
                    for tt in range(TT):
                        lo = hd_ * 6 * GRID_W + (2 - 2 * tt) * GRID_W
                        ins = stt(s_b[j][:, tt, :], px[hd_ % 4][:, tt * T:(tt + 1) * T], SCALE_B, bias_rows[:, lo:lo + T],
                                  ALU.mult, ALU.add)
                    chain.link(ins)
                    chain.link(dve.tensor_reduce(small_b[:, j, 0, :], s_b[j], AX.X, ALU.max))
                    ts_(small_b[:, j, 1, :], small_b[:, j, 0, :], -1.0, None, ALU.mult).then_inc(b_negmax, 1)
                    if hd_ == 0:
                        for p in range(4):
                            dve.wait_ge(oa_hi, p + 1)
                            tt_(h_lo[:, 2 * p:2 * p + 2, :], oa[:, 2 * p:2 * p + 2, :], whole(h_hi[:, 2 * p:2 * p + 2, :]),
                                ALU.subtract).then_inc(mix_ready, 1)
                elif st == 1:
                    dve.wait_ge(b_exp, hd_ + 1)
                    chain.link(dve.reciprocal(small_b[:, j, 3, :], small_b[:, j, 2, :]))
                    for tt in range(TT):
                        ins = ts_(s_b[j][:, tt, :], s_b[j][:, tt, :], small_b[:, j, 3, tt:tt + 1], None, ALU.mult)
                    ins.then_inc(b_probs, 1)
                elif st == 3:
                    dve.wait_ge(b_hi, hd_ + 1)
                    tt_(h_lo[:, 8 + hd_, :], px[hd_ % 4][:, 0:T], whole(h_hi[:, 8 + hd_, :]), ALU.subtract).then_inc(mix_ready, 1)

            take(w_in_complete(NBLOCKS["w_in"] - 1))
            clear_squares()
            with dve.Fori(0, NBLOCKS["w_out"] // BODY) as i:
                chain.enter(i, APIECES)
                for b in range(BODY):
                    split("w_out", i, b, due_in_body("w_out", i, b, 0))
                    residual("w_out", i, b, GA1)
                    take_in_body("w_out", i, b)
                    add_squares("norm2", i, b)
                chain.leave(NBLOCKS["w_out"] // BODY)
            rsqrt_mean("norm2", D)
            modulation("norm2", "g2", 0, SC2)
            normed("norm2", SH2)

            dve.memset(gpad[:, 0:1], 0.0)
            chain.link(dve.memset(gpad[:, T + 1:T + 2], 0.0))

            def up(half, i, b, unit, cond):
                stage, k = f"w_up{half}", i * BODY + (half * FH + b)
                due = list(body_pieces(b)) if unit is not None else []
                split(stage, i, b)
                if b:
                    dve.wait_ge(glu_lo_ready, k)
                dve.wait_ge(g_copied, k + 1)
                chain.link(ts_(conv[:, :], gpad[:, 0:T], pcol("conv", k * 4), pcol("conv", k * 4 + 3), ALU.mult, ALU.add))
                chain.link(stt(conv[:, :], gpad[:, 1:T + 1], pcol("conv", k * 4 + 1), conv[:, :], ALU.mult, ALU.add))
                stt(conv[:, :], gpad[:, 2:T + 2], pcol("conv", k * 4 + 2), conv[:, :], ALU.mult, ALU.add).then_inc(conv_ready, 1)
                dve.wait_ge(gelu_ready, k + 1)
                tt_(conv[:, :], conv[:, :], pm[b % 2][:, T:2 * T], ALU.mult).then_inc(bank_free[b % 2], 1)
                pieces(unit, cond, due[:1])
                dve.wait_ge(glu_hi_ready, k + 1)
                c = i * BODY + b
                tt_(one(glu_lo, c), conv[:, :], whole(one(glu_hi, c)), ALU.subtract).then_inc(glu_lo_ready, 1)
                pieces(unit, cond, due[1:])
                if unit is not None and b == BODY - 1:
                    take(unit)

            for half, runs in ((0, ((0, 4, 0), (4, 5, 1))), (1, ((0, 5, 1),))):
                for lo, hi, cond in runs:
                    with dve.Fori(lo, hi) as i:
                        chain.enter(i - lo, 2 * BODY + APIECES)
                        for b in range(BODY):
                            up(half, i, b, i + UNIT_OF[f"w_up{half}"], cond)
                        chain.leave(hi - lo)
                for b in range(FH % BODY):
                    up(half, FH // BODY, b, None, 1)
                down = f"w_down{half}"
                if half == 1:
                    clear_squares(ssqg)
                with dve.Fori(0, NBLOCKS[down] // BODY) as i:
                    chain.enter(i, APIECES if down in UNIT_OF else 0)
                    for b in range(BODY):
                        split(down, i, b, due_in_body(down, i, b, 1) if down in UNIT_OF else ())
                        residual(down, i, b, GA2)
                        if down in UNIT_OF:
                            take_in_body(down, i, b)
                        if half == 1:
                            dve.wait_ge(sqg_ready, i * BODY + (b + 1))
                            tt_(ssqg[:, :, :], ssqg[:, :, :], sqtg[:, :, :], ALU.add).then_inc(sqg_added, 1)
                            add_squares("final", i, b)
                    chain.leave(NBLOCKS[down] // BODY)

            k = H_NORMS.index("pre0")
            modulation("pre0", "pre", 0, C0)
            chain.link(tt_(gain[:, k, :], gain[:, k, :], pcols("gfinal", KC), ALU.mult))
            rsqrt_mean("final", D, dst=rs1)
            chain.link(tt_(rstd[:, :], rs1[:, :], rs1[:, :], ALU.mult))
            chain.link(tt_(rstd[:, :], rstd[:, :], ps[:, T:2 * T], ALU.mult))
            ts_(rstd[:, :], rstd[:, :], 1.0 / D, EPS, ALU.mult, ALU.add).then_inc(ms_ready, 1)
            dve.wait_ge(std_ready, SUMS["finalg"])
            chain.link(dve.reciprocal(rstd[:, :], rstd[:, :]))
            chain.link(tt_(rstd[:, :], rstd[:, :], rs1[:, :], ALU.mult))
            normed("pre0", S0)

            with dve.Fori(0, NBLOCKS["sgu_v"] // BODY) as i:
                chain.enter(i, APIECES + BODY)
                for b in range(BODY):
                    split("sgu_v", i, b, due_in_body("sgu_v", i, b, 1))
                    c = i * BODY + b
                    chain.link(stt(one(x, c), one(x, c), pcol("gfinal", c), rs1[:, :], ALU.mult, ALU.mult))
                    take_in_body("sgu_v", i, b)
                chain.leave(NBLOCKS["sgu_v"] // BODY)
            for b in range(2):
                dve.wait_ge(bank_free[b], BBASE["sgu_u"] // 2)
            for tt in range(TT):
                chain.link(dve.tensor_reduce(stat[:, tt, 24:25], stat[:, tt, 0:16], AX.X, ALU.add))
                chain.link(ts_(stat[:, tt, 25:26], stat[:, tt, 24:25], -1.0 / SGU_W, None, ALU.mult))
                ts_(v_sgu[:, tt, :], v_sgu[:, tt, :], stat[:, tt, 25:26], None, ALU.add).then_inc(v_mean, 1)

            with dve.Fori(0, 2) as i:
                chain.enter(i, APIECES)
                for b in range(BODY):
                    split("sgu_u", i, b, due_in_body("sgu_u", i, b, 1))
                    take_in_body("sgu_u", i, b)
                chain.leave(2)
            dve.wait_ge(v_sq, 8)
            for tt in range(TT):
                chain.link(dve.tensor_reduce(stat[:, tt, 26:27], stat[:, tt, 16:24], AX.X, ALU.add))
                ts_(stat[:, tt, 27:28], stat[:, tt, 26:27], 1.0 / SGU_W, EPS, ALU.mult, ALU.add).then_inc(v_var, 1)
            for tt in range(TT):
                dve.wait_ge(v_std, tt + 1)
                chain.link(dve.reciprocal(stat[:, tt, 29:30], stat[:, tt, 28:29]))
                ts_(v_sgu[:, tt, :], v_sgu[:, tt, :], stat[:, tt, 29:30], None, ALU.mult).then_inc(v_normed, 1)

            def mixed_group(g):
                dve.wait_ge(vm_ready, g + 1)
                bs = mixw[:, g // 2 % 2, g % 2, 1, :]
                for c in range(2):
                    ins = stt(halves(stmp[:, g % 2, c * T:(c + 1) * T]), halves(px[g % 4][:, c * T:(c + 1) * T]),
                              pcol("gsgu", 2 * g + c), over(bs, 2), ALU.mult, ALU.add)
                chain.link(ins)
                gg = gu[:, 2 * g:2 * g + 2, :]
                dve.wait_ge(bank_free[g % 2], taken("sgu_u", *divmod(g, BODY)))
                tt_(gg, gg, halves(stmp[:, g % 2, :]), ALU.mult).then_inc(vm_taken, 1)

            for n in range(8, 16):
                i, b = divmod(n, BODY)
                split("sgu_u", i, b, due_in_body("sgu_u", i, b, 1))
                take_in_body("sgu_u", i, b)
                for g in (2 * n - 16, 2 * n - 15):
                    mixed_group(g)
            with dve.Fori(0, NBLOCKS["sgu_z"] // BODY) as i:
                chain.enter(i, APIECES)
                for b in range(BODY):
                    split("sgu_z", i, b)
                    c = i * (2 * BODY) + 2 * b
                    due = list(body_pieces(b))
                    dve.wait_ge(bank_free[b % 2], taken("sgu_z", i, b))
                    tt_(at(gu, c, 2), at(gu, c, 2), halves(ztmp[:, b % 2, :]), ALU.mult).then_inc(y_ready, 1)
                    pieces(i + UNIT_OF["sgu_z"], 1, due[:1])
                    dve.wait_ge(y_hi_ready, i * BODY + (b + 1))
                    tt_(at(y_lo, c, 2), at(gu, c, 2), whole(at(y_hi, c, 2)), ALU.subtract).then_inc(y_lo_ready, 1)
                    pieces(i + UNIT_OF["sgu_z"], 1, due[1:])
                    if b == BODY - 1:
                        take(i + UNIT_OF["sgu_z"])
                chain.leave(NBLOCKS["sgu_z"] // BODY)
            clear_squares()
            with dve.Fori(0, NBLOCKS["sgu_out"] // BODY) as i:
                chain.enter(i, APIECES)
                for b in range(BODY):
                    split("sgu_out", i, b, due_in_body("sgu_out", i, b, 1))
                    add_squares("post0", i, b)
                    take_in_body("sgu_out", i, b)
                chain.leave(NBLOCKS["sgu_out"] // BODY)

            def post(name, layer, gate, y, taken_):
                chain.link(tt_(gain[:, 4, :], pcols("post", KC, layer * KC), mods[:, gate * KC:(gate + 1) * KC], ALU.mult))
                rsqrt_mean(name, D)
                for b in range(2):
                    dve.wait_ge(bank_free[b], taken_)
                for p in range(PAIRS):
                    for kc in (2 * p, 2 * p + 1):
                        ins = stt(y[:, kc, :], y[:, kc, :], gain[:, 4, kc:kc + 1], rstd[:, :], ALU.mult, ALU.mult)
                    if p % 2:
                        ins.then_inc(y_scaled, 1)
                    else:
                        chain.link(ins)
                        xp = x[:, 2 * p:2 * p + 2, :]
                        tt_(xp, xp, y[:, 2 * p:2 * p + 2, :], ALU.add).then_inc(x_ready, 1)

            post("post0", 0, G0, y0, BBASE["lat"] // 2)
            modulation("pre1", "pre", KC, C1)
            rsqrt_mean("pre1", D)
            normed("pre1", S1)

            for b in range(BODY):
                split("lat", 0, b, due_in_body("lat", 0, b, 1))
                take_in_body("lat", 0, b)
            for n in range(NBLOCKS["mla_z"]):
                i, b = divmod(n, BODY)
                split("mla_z", i, b, due_in_body("mla_z", 0, b, 1) if i == 0 else ())
                if n == 1:
                    rsqrt_mean("kv", KVR)
                    for c in range(4):
                        ins = stt(lat[:, c, :], lat[:, c, :], pcol("gkv", c), rstd[:, :], ALU.mult, ALU.mult)
                    ins.then_inc(lat_normed, 1)
                    dve.wait_ge(lat_normed, 1)
                if n == 2:
                    rsqrt_mean("q", QR, 1)
                    for c in range(4):
                        rows = slice(0, P) if c < 3 else slice(64, P)
                        ins = stt(lat[rows, 4 + c, :], lat[rows, 4 + c, :], pcol("gq", c, rows), rstd[rows, :], ALU.mult, ALU.mult)
                    ins.then_inc(lat_normed, 1)
                    dve.wait_ge(lat_normed, 2)
                if n == 3:
                    for part in range(2):
                        dve.wait_ge(lat_hi_ready, part + 1)
                        tt_(lat_lo[:, 4 * part:4 * part + 4, :], lat[:, 4 * part:4 * part + 4, :],
                            whole(lat_hi[:, 4 * part:4 * part + 4, :]), ALU.subtract).then_inc(lat_lo_ready, 1)
                if i == 0:
                    take_in_body("mla_z", 0, b)
                if n == 5:
                    dve.wait_ge(kr_rot, 1)
                    tt_(rt[0], px[1][0:ROPE, 0:T], sin, ALU.mult)
                    chain.link(tt_(kro, lat[0:ROPE, 7, :], cos, ALU.mult))
                    tt_(kro, kro, rt[0], ALU.add).then_inc(kr_ready, 1)

            def head_step(i, step):
                for st, hn, j in head_stages(i, step):
                    A, B = [pm[0], pm[1], ps, pv][j], px[j]
                    if st == 0:
                        split("heads", i, j)
                    elif st == 1:
                        dve.wait_ge(m_rot, hn + 1)
                        tt_(rt[j], B[0:ROPE, 0:T], sin, ALU.mult)
                        chain.link(tt_(qr[j], qr[j], cos, ALU.mult))
                        tt_(qr[j], qr[j], rt[j], ALU.add).then_inc(m_rope, 1)
                    elif st == 2:
                        dve.wait_ge(m_scores, hn + 1)
                        chain.link(stt(pr[j], A[:, 0:3 * P], SCALE_M, mask_m, ALU.mult, ALU.add))
                        dve.tensor_reduce(small_m[:, j, 0, 0:1], pr[j][:, 0:P], AX.X, ALU.max)
                        chain.link(dve.tensor_reduce(small_m[:, j, 0, 1:2], pr[j][:, P:3 * P], AX.X, ALU.max))
                        ts_(small_m[:, j, 1, :], small_m[:, j, 0, :], -1.0, None, ALU.mult).then_inc(m_negmax, 1)
                        dve.wait_ge(m_exp, hn + 1)
                        chain.link(dve.reciprocal(small_m[:, j, 3, :], small_m[:, j, 2, :]))
                        for lo, tt in ((0, 0), (P, 1)):
                            keys = P * (tt + 1)
                            ins = ts_(pr[j][:, lo:lo + keys], pr[j][:, lo:lo + keys], small_m[:, j, 3, tt:tt + 1], None, ALU.mult)
                        ins.then_inc(m_probs, 1)
                    elif st == 4:
                        dve.wait_ge(m_num, hn + 1)
                        zc = one(zo, hn)
                        tt_(zc, zc, A[:, 0:T], ALU.mult).then_inc(head_free[j], 1)
                for st, hn, j in head_stages(i, step):
                    if st == 4:
                        dve.wait_ge(m_hi, hn + 1)
                        tt_(one(h_lo, hn), one(zo, hn), whole(one(h_hi, hn)), ALU.subtract).then_inc(o_ready, 1)

            for j in range(BODY):
                head_step(0, j)
            with dve.Fori(1, MH // BODY) as i:
                chain.enter(i - 1, 4 * BODY)
                for j in range(BODY):
                    head_step(i, j)
                chain.leave(MH // BODY - 1)
            for j in range(BODY):
                head_step(MH // BODY, j)
            clear_squares()
            for n in range(NBLOCKS["mla_out"]):
                split("mla_out", n // BODY, n % BODY)
                add_squares("post1", n // BODY, n % BODY)
            post("post1", 1, G1, y1, BBASE["mla_out"] // 2 + NBLOCKS["mla_out"] // 2)


def constants():
    f = np.float32
    t = np.arange(T)
    mask_a = np.zeros((P, 2, TT, T), f)
    for sc in range(TT):
        s = (np.arange(P) + sc * P)[:, None]
        mask_a[:, 0, sc] = np.where(t[None] >= s, 0.0, NEG)
        mask_a[:, 1, sc] = np.where(t[None] <= s, 0.0, NEG)
    c = np.arange(GRID_W)
    lo = np.clip(c - WIN_COLS // 2, 0, GRID_W - WIN_COLS)[:, None]
    win = np.where((c[None] >= lo) & (c[None] < lo + WIN_COLS), 0.0, NEG).astype(f)
    cst = np.zeros((P, 1024), f)
    inv = (f(10000.0) ** (-np.arange(0, ROPE, 2, dtype=f) / f(ROPE))).astype(f)
    ang = (t.astype(f)[:, None] * inv[None, :]).astype(f)
    cst[0:64, 0:256] = np.concatenate([np.cos(ang), np.cos(ang)], axis=1).T
    cst[0:64, 256:512] = np.concatenate([np.sin(ang), np.sin(ang)], axis=1).T
    q = np.arange(P)[:, None]
    cst[:, 512:640] = np.where(t[None, :P] // 64 <= q // 64, 0.0, NEG)
    cst[:, 640:896] = np.where(t[None] // 64 <= (q + P) // 64, 0.0, NEG)
    half = ROPE // 2
    for m in range(half):
        cst[m + half, 896 + m] = -1.0
        cst[m, 896 + m + half] = 1.0
    return {"ident": np.eye(P, dtype=f), "mask_a": mask_a.reshape(P, -1), "wmask": np.concatenate([win, win]), "mla_cst": cst}


def blocks(w, k=PKC):
    kk, n = w.shape
    w = w.reshape(kk // (P * k), k, P, n // COLS, COLS).transpose(3, 0, 2, 1, 4)
    return np.ascontiguousarray(w).reshape(-1, P, k * COLS)


def columns_of(v):
    return np.asarray(v).reshape(-1, P).T


def lay_out(i):
    i = {n: np.asarray(v) for n, v in i.items()}
    f = np.float32
    d = constants()
    d["x"] = np.ascontiguousarray(i["x"][0].T.reshape(KC, P, T).transpose(1, 0, 2)).reshape(P, -1)
    par = np.zeros((P, NPAR), f)

    def put(name, cols, c=0):
        par[:cols.shape[0], PCOL[name] + c:PCOL[name] + c + cols.shape[1]] = cols

    put("c", columns_of(i["c"][0]))
    put("c2", columns_of(i["c_2"][0]))
    put("bias", columns_of(i["b_ada"][0]))
    put("bias", columns_of(i["ada_b_2"].reshape(-1)), 6 * KC)
    put("g1", columns_of(i["g_norm1"][0]))
    put("ghead", columns_of(i["g_head_a"][0]))
    put("g2", columns_of(i["g_norm2"][0]))
    conv = np.concatenate([i["conv_w"][0], i["conv_b"]], axis=0).reshape(4, FC, P).transpose(2, 1, 0)
    put("conv", conv.reshape(P, -1))
    put("gfinal", columns_of(i["g_final"]))
    put("pre", columns_of(i["pre_g_2"].reshape(-1)))
    put("post", columns_of(i["post_g_2"].reshape(-1)))
    put("gsgu", columns_of(i["sgu_norm_g_2"][0]))
    gq = i["mla_q_norm_g_2"][0]
    put("gq", columns_of(np.concatenate([gq[:384], np.zeros(64, f), gq[384:]])))
    put("gkv", columns_of(i["mla_kv_norm_g_2"][0]))

    def gate_rows(v, first):
        out = np.zeros(v.shape[:-1] + (GROW,), f)
        out[..., 0:NH_A] = v[..., first * NH_A:(first + 1) * NH_A]
        out[..., 32:GROW] = v[..., (first + 2) * NH_A:(first + 3) * NH_A]
        return out

    put("bi", gate_rows(i["b_gates"][0], 0)[:, None])
    put("bf", gate_rows(i["b_gates"][0], 1)[:, None])
    d["par"] = par

    w = i["w_in"][0]
    q_a, k_a, v_a, o_a = (w[:, n * 1024:(n + 1) * 1024] for n in range(4))
    gw = w[:, 4096:4112]
    q_b, k_b, v_b = (w[:, 4112 + n * 1024:4112 + (n + 1) * 1024] for n in range(3))
    gate_w = np.zeros((P, 2, GPAD), f)
    for g in range(2):
        gate_w[:, g, :KC * GROW] = gate_rows(gw, g).reshape(KC, P, GROW).transpose(1, 0, 2).reshape(P, -1)
    d["gate_w"] = gate_w.reshape(P, -1)
    d["w_in"] = blocks(np.concatenate([k_a, q_a, v_a, o_a, q_b, k_b, v_b], axis=1))
    d["w_out"] = blocks(i["w_out"][0])
    up = i["w_up"][0]
    u, g = up[:, :D_FF].reshape(D, FC, 1, P), up[:, D_FF:].reshape(D, FC, 1, P)
    up = np.concatenate([g, u], axis=2)
    for half in range(2):
        d[f"w_up{half}"] = blocks(up[:, half * FH:(half + 1) * FH].reshape(D, -1))
        d[f"w_down{half}"] = blocks(i["w_down"][0][half * FH * P:(half + 1) * FH * P], FH)

    rpb = i["rpb"][0]
    c = np.arange(GRID_W)
    dc = np.clip(c[None] - c[:, None] + WIN_COLS - 1, 0, 2 * WIN_COLS - 2)
    rows = []
    for half in range(2):
        dr = np.arange(6) + 5 - half
        rows.append(rpb[:, dr][:, :, dc].transpose(2, 0, 1, 3).reshape(GRID_W, -1))
    d["bias_b"] = np.concatenate(rows)

    ada = np.concatenate([i["w_ada"][0], i["ada_w_2"][0], i["ada_w_2"][1]], axis=1)
    ada = ada.reshape(APIECES, KC // APIECES, P, 12 * UNITS, UCOLS).transpose(3, 0, 2, 1, 4)
    d["ada"] = np.ascontiguousarray(ada).reshape(-1, P, APIECE)

    w = i["sgu_w_in_2"][0]
    d["sgu_u"], d["sgu_v"], d["sgu_z"] = (blocks(w[:, n * SGU_W:(n + 1) * SGU_W]) for n in range(3))
    ws = i["sgu_w_s_2"][0].transpose(0, 2, 1)
    bs = np.broadcast_to(i["sgu_b_s_2"][0][:, None, :], (GROUPS, P, P))
    d["mix"] = np.ascontiguousarray(np.stack([ws, bs], axis=2).reshape(GROUPS // 2, 2, P, 2, P).transpose(0, 2, 1, 3, 4)).reshape(GROUPS // 2, P, -1)
    d["sgu_out"] = blocks(i["sgu_w_out_2"][0])

    w = i["mla_w_in_2"][0]
    cq, ckv, kr, z = w[:, :QR], w[:, QR:QR + KVR], w[:, QR + KVR:QR + KVR + ROPE], w[:, QR + KVR + ROPE:]
    d["lat"] = blocks(np.concatenate([ckv, cq[:, :384], kr, cq[:, 384:]], axis=1))
    d["mla_z"] = blocks(z)
    uq = i["mla_w_uq_2"][0]
    uq = np.concatenate([uq[:384], np.zeros((64, uq.shape[1]), f), uq[384:]])
    head = np.concatenate([uq.reshape(512, MH, 192), i["mla_w_ukv_2"][0].reshape(512, MH, 256)], axis=2)
    heads = np.zeros((MH, P, 2, QUARTER), f)
    heads[..., :2 * HEADW] = head.reshape(2, 2, P, MH, HEADW).transpose(3, 2, 0, 1, 4).reshape(MH, P, 2, -1)
    d["heads"] = heads.reshape(MH, P, -1)
    d["mla_out"] = blocks(i["mla_w_out_2"][0])
    return {n: np.ascontiguousarray(v, dtype=f) for n, v in d.items()}


def kernel(**inputs):
    import concourse.bacc as bacc
    from concourse.bass_utils import run_bass_kernel_spmd as run

    nc = bacc.Bacc("TRN2", target_bir_lowering=False, num_devices=1)
    arrays = {f"in_{n}": v for n, v in lay_out(inputs).items()}
    args = {n[3:]: nc.dram_tensor(n, v.shape, F32, kind="ExternalInput").ap() for n, v in arrays.items()}
    args["out"] = nc.dram_tensor("out_x", (P, KC * T), F32, kind="ExternalOutput").ap()
    build(nc, args)
    got = run(nc, [arrays], core_ids=[0]).results[0]["out_x"]
    return np.ascontiguousarray(got.reshape(P, KC, T).transpose(2, 1, 0)).reshape(1, T, D)
```
